# Optimizing a Trainium2 kernel written in Bass

```python
import jax, jax.numpy as jnp
from jax import lax
import numpy as np

D_MODEL = 1024
BATCH = 1
SEQ = 4096
DEPTH = 1

HEAD_DIM = 64
FOX_HEADS = 8
FOX_W = FOX_HEADS * HEAD_DIM
RWKV_HEADS = 4
RWKV_W = RWKV_HEADS * HEAD_DIM
POOL_GROUPS = 4
POOL_GROUP_DIM = 64
POOL_W = POOL_GROUPS * POOL_GROUP_DIM
POOL_WINDOWS = (2, 4, 8, 16)
D_MIX = FOX_W + RWKV_W + POOL_W
RWKV_DECAY_RANK = 64
RWKV_ICL_RANK = 64
RWKV_SHIFT_W = 3 * RWKV_W + RWKV_DECAY_RANK + RWKV_ICL_RANK
Q_BLOCK = 128
NORM_EPS = 1e-6
RWKV_GN_EPS = 64e-5
DECAY_SCALE = float(np.exp(-0.5))
IN_SPLITS = (FOX_W, FOX_W, FOX_W, FOX_HEADS, RWKV_SHIFT_W, POOL_W, D_MIX)
D_IN = int(sum(IN_SPLITS))
IN_IDX = [int(i) for i in np.cumsum(IN_SPLITS)[:-1]]
RWKV_IDX = [int(i) for i in np.cumsum((RWKV_W, RWKV_W, RWKV_W, RWKV_DECAY_RANK))]

kernel_name = "hymba_fox_rwkv7_pool_adaln"

def rms_norm(z, g):
    zf = z.astype(jnp.float32)
    y = zf * lax.rsqrt(jnp.mean(zf * zf, axis=-1, keepdims=True) + NORM_EPS)
    return (y * g.astype(jnp.float32)).astype(z.dtype)

def token_shift(z):
    return jnp.pad(z, ((0, 0), (1, 0), (0, 0)))[:, :-1]

def fox_attention(q, k, v, f_logit, q_gain, k_gain, f_bias):
    B, S, _ = q.shape

    def heads(z):
        return z.reshape(B, S, FOX_HEADS, HEAD_DIM).transpose(0, 2, 1, 3)

    qh = rms_norm(heads(q), q_gain).astype(jnp.float32) * (HEAD_DIM ** -0.5)
    kh = rms_norm(heads(k), k_gain).astype(jnp.float32)
    vh = heads(v).astype(jnp.float32)
    log_f = jax.nn.log_sigmoid((f_logit + f_bias).astype(jnp.float32))
    cum = jnp.cumsum(log_f, axis=1).transpose(0, 2, 1)
    outs = []
    for i in range(S // Q_BLOCK):
        q0 = i * Q_BLOCK
        L = q0 + Q_BLOCK
        s = jnp.einsum('bhqd,bhkd->bhqk', qh[:, :, q0:L], kh[:, :, :L])
        s = s + cum[:, :, q0:L, None] - cum[:, :, None, :L]
        causal = jnp.arange(L)[None, :] <= (q0 + jnp.arange(Q_BLOCK))[:, None]
        p = jax.nn.softmax(jnp.where(causal, s, -jnp.inf), axis=-1)
        outs.append(jnp.einsum('bhqk,bhkd->bhqd', p, vh[:, :, :L]))
    o = jnp.concatenate(outs, axis=2)
    return o.transpose(0, 2, 1, 3).reshape(B, S, FOX_W).astype(q.dtype)

def rwkv7_time_mix(z, mu, w0, w2, a0, a2, k_k, k_a, r_k, ln_g, ln_b):
    B, S, _ = z.shape
    zf = z.astype(jnp.float32)
    zf = zf + (token_shift(zf) - zf) * mu.astype(jnp.float32)
    r, k, v, wd, ad = jnp.split(zf, RWKV_IDX, axis=-1)
    log_w = -DECAY_SCALE * jax.nn.sigmoid(w0 + jnp.tanh(wd) @ w2)
    a = jax.nn.sigmoid(a0 + ad @ a2)
    kk = (k * k_k).reshape(B, S, RWKV_HEADS, HEAD_DIM)
    kk = kk / jnp.maximum(jnp.linalg.norm(kk, axis=-1, keepdims=True), 1e-12)
    k = k * (1.0 + (a - 1.0) * k_a)

    def hd(t):
        return t.reshape(B, S, RWKV_HEADS, HEAD_DIM)

    rh, kh, vh, ah = hd(r), hd(k), hd(v), hd(a)
    wh = jnp.exp(hd(log_w))
    xs = tuple(t.transpose(1, 0, 2, 3) for t in (rh, wh, kh, vh, kk, ah))

    def step(state, inp):
        r_t, w_t, k_t, v_t, kk_t, a_t = inp
        sa = jnp.einsum('bhij,bhj->bhi', state, -kk_t)
        state = (state * w_t[:, :, None, :]
                 + sa[..., :, None] * (kk_t * a_t)[:, :, None, :]
                 + v_t[..., :, None] * k_t[:, :, None, :])
        return state, jnp.einsum('bhij,bhj->bhi', state, r_t)

    state0 = jnp.zeros((B, RWKV_HEADS, HEAD_DIM, HEAD_DIM), jnp.float32)
    _, o = lax.scan(step, state0, xs)
    o = o.transpose(1, 0, 2, 3)
    mean = jnp.mean(o, axis=-1, keepdims=True)
    var = jnp.mean(jnp.square(o - mean), axis=-1, keepdims=True)
    o = ((o - mean) * lax.rsqrt(var + RWKV_GN_EPS)).reshape(B, S, RWKV_W) * ln_g + ln_b
    bonus = jnp.sum(rh * kh * r_k, axis=-1, keepdims=True) * vh
    return (o + bonus.reshape(B, S, RWKV_W)).astype(z.dtype)

def trailing_mean(z, w):
    S = z.shape[1]
    cs = jnp.pad(jnp.cumsum(z, axis=1), ((0, 0), (1, 0), (0, 0)))
    upper = cs[:, 1:]
    lower = jnp.pad(cs, ((0, 0), (w - 1, 0), (0, 0)))[:, :S]
    count = jnp.minimum(jnp.arange(S) + 1, w).astype(jnp.float32)
    return (upper - lower) / count[None, :, None]

def multiscale_pool(p, pool_w, pool_scale):
    B, S, _ = p.shape
    pf = p.astype(jnp.float32).reshape(B, S, POOL_GROUPS, POOL_GROUP_DIM)
    pooled = jnp.stack([trailing_mean(pf[:, :, g], w) - pf[:, :, g]
                        for g, w in enumerate(POOL_WINDOWS)], axis=2)
    y = jnp.einsum('bsgc,gcd->bsgd', pooled, pool_w.astype(jnp.float32))
    return (y.reshape(B, S, POOL_W) * pool_scale).astype(p.dtype)

def setup_inputs(seed: int = 0) -> dict:
    key = jax.random.key(seed)
    ks = jax.random.split(key, 24)
    nrm = lambda k, shape: jax.random.normal(k, shape, jnp.float32)
    L, D = DEPTH, D_MODEL
    return {
        "x": nrm(ks[0], (BATCH, SEQ, D)),
        "c": nrm(ks[1], (BATCH, D)),
        "ada_w": nrm(ks[2], (L, D, 3 * D)) * D ** -0.5,
        "ada_b": nrm(ks[3], (L, 3 * D)) * 0.02,
        "norm_pre": 1.0 + 0.05 * nrm(ks[4], (L, D)),
        "norm_post": 1.0 + 0.05 * nrm(ks[5], (L, D)),
        "w_in": nrm(ks[6], (L, D, D_IN)) * D ** -0.5,
        "fox_q_gain": 1.0 + 0.05 * nrm(ks[7], (L, HEAD_DIM)),
        "fox_k_gain": 1.0 + 0.05 * nrm(ks[8], (L, HEAD_DIM)),
        "fox_f_bias": 2.0 + 0.5 * nrm(ks[9], (L, FOX_HEADS)),
        "rwkv_mu": jax.random.uniform(ks[10], (L, RWKV_SHIFT_W), jnp.float32),
        "rwkv_w0": 0.5 * nrm(ks[11], (L, RWKV_W)),
        "rwkv_w2": nrm(ks[12], (L, RWKV_DECAY_RANK, RWKV_W)) * 0.1,
        "rwkv_a0": 0.1 * nrm(ks[13], (L, RWKV_W)),
        "rwkv_a2": nrm(ks[14], (L, RWKV_ICL_RANK, RWKV_W)) * 0.1,
        "rwkv_k_k": 0.85 + 0.05 * nrm(ks[15], (L, RWKV_W)),
        "rwkv_k_a": 1.0 + 0.05 * nrm(ks[16], (L, RWKV_W)),
        "rwkv_r_k": 0.1 * nrm(ks[17], (L, RWKV_HEADS, HEAD_DIM)),
        "rwkv_ln_g": 1.0 + 0.05 * nrm(ks[18], (L, RWKV_W)),
        "rwkv_ln_b": 0.02 * nrm(ks[19], (L, RWKV_W)),
        "pool_w": nrm(ks[20], (L, POOL_GROUPS, POOL_GROUP_DIM, POOL_GROUP_DIM)) * POOL_GROUP_DIM ** -0.5,
        "pool_scale": 1.0 + 0.1 * nrm(ks[21], (L, POOL_W)),
        "w_out": nrm(ks[22], (L, D_MIX, D)) * D_MIX ** -0.5,
    }

def reference(x, c, ada_w, ada_b, norm_pre, norm_post, w_in, fox_q_gain, fox_k_gain, fox_f_bias,
              rwkv_mu, rwkv_w0, rwkv_w2, rwkv_a0, rwkv_a2, rwkv_k_k, rwkv_k_a, rwkv_r_k,
              rwkv_ln_g, rwkv_ln_b, pool_w, pool_scale, w_out):
    for l in range(DEPTH):
        mod = jax.nn.silu(c) @ ada_w[l] + ada_b[l]
        shift, scale, gate = jnp.split(mod[:, None, :], 3, axis=-1)
        h = rms_norm(x, norm_pre[l]) * (1.0 + scale) + shift
        u = h @ w_in[l]
        q, k, v, f_logit, z_rwkv, p_pool, g = jnp.split(u, IN_IDX, axis=-1)
        y_fox = fox_attention(q, k, v, f_logit, fox_q_gain[l], fox_k_gain[l], fox_f_bias[l])
        y_rwkv = rwkv7_time_mix(z_rwkv, rwkv_mu[l], rwkv_w0[l], rwkv_w2[l], rwkv_a0[l], rwkv_a2[l],
                                rwkv_k_k[l], rwkv_k_a[l], rwkv_r_k[l], rwkv_ln_g[l], rwkv_ln_b[l])
        y_pool = multiscale_pool(p_pool, pool_w[l], pool_scale[l])
        y = jnp.concatenate([y_fox, y_rwkv, y_pool], axis=-1) * jax.nn.silu(g)
        x = x + gate * rms_norm(y @ w_out[l], norm_post[l])
    return x


_drawn_inputs = setup_inputs


def setup_inputs(seed=0):
    import zlib

    import numpy as np

    out = dict(_drawn_inputs(seed))
    spreads = {}
    factors = {'fox_q_gain': 8.0,
     'fox_k_gain': 8.0,
     'rwkv_a0': 3.559,
     'rwkv_k_k': 22.511,
     'rwkv_ln_g': 4.436,
     'rwkv_ln_b': 27.422,
     'pool_scale': 5.574}
    for name, (base, spread) in spreads.items():
        noise = np.random.default_rng([zlib.crc32(name.encode()), seed]).standard_normal(out[name].shape)
        drawn = base * np.exp(spread * noise) if base else spread * noise
        out[name] = __import__('jax').numpy.asarray(drawn.astype(out[name].dtype))
    for name, factor in factors.items():
        out[name] = (out[name] * factor).astype(out[name].dtype)
    return out
```

```python
from contextlib import ExitStack

import concourse.bass as bass
from concourse import mybir

F32 = mybir.dt.float32
F16 = mybir.dt.float16
BF16 = mybir.dt.bfloat16
I32 = mybir.dt.int32
ALU = mybir.AluOpType
ACT = mybir.ActivationFunctionType
AX = mybir.AxisListType
RMAX = bass.bass_isa.ReduceOp.max

P = 128
SEQ, DM = 4096, 1024
HD = 64
FOX_HEADS, RWKV_HEADS = 8, 4
FOX_W, RWKV_W, POOL_W = 512, 256, 256
WINDOWS = (2, 4, 8, 16)
RANK = 64
D_IN = 3720
V_COL, F_COL, Z_COL, G_COL = 1024, 1536, 1544, 2696
ZC = 1152
KT = DM // P
BT = 512
NB = SEQ // BT
NT = SEQ // P
EPS = 1e-6
GN_EPS = 64e-5
DECAY = 0.6065306597126334
TOP = 32768.0


class Count:

    def __init__(self, sem, per, credit=0):
        self.sem, self.per, self.credit = sem, per, credit

    def past(self, turn, k):
        return turn * self.per + (self.credit + k)


class Layer:
    pass


def scope(nc, ctx, stage):
    sems = []

    def clear():
        nc.clear_and_free_semaphores(sems)
        nc.all_engine_barrier()

    ctx.callback(clear)

    def sb(name, shape, dt=F32):
        return ctx.enter_context(nc.sbuf_tensor(name, shape, dt))

    def ps(name, shape=(P, 512), dt=F32):
        return ctx.enter_context(nc.psum_tensor(name, list(shape), dt))

    def sem(name):
        sems.append(nc.alloc_semaphore(name=f"{stage}_{name}"))
        return sems[-1]

    def count(name, per, credit=0):
        return Count(sem(name), per, credit)

    return sb, ps, sem, count


def column(v):
    return v.rearrange("(p o) -> p o", o=1)


def prepare(nc, a, m):
    with ExitStack() as ctx:
        sb, ps, sem, count = scope(nc, ctx, "prepare")
        adaw = sb("adaw", [P, 2, 3 * DM])
        wst = sb("wst", [P, 2, D_IN])
        ccol = sb("ccol", [P, KT])
        csig = sb("csig", [P, KT])
        cbc = sb("cbc", [P, KT, P])
        onesf = sb("onesf", [P, P])
        abcol = sb("abcol", [P, 2 * KT])
        npre = sb("npre", [P, KT])
        rowmax = sb("rowmax", [P, KT])
        rinv = sb("rinv", [P, KT])
        gcol = sb("gcol", [P, KT])
        scol = sb("scol", [P, KT])
        t8 = sb("t8", [P, KT])
        bnd = sb("bnd", [P, 4])
        gains = sb("gains", [P, 2, HD])
        gm = sb("gm", [P, 4])
        pcol = ps("pcol")
        pg = [ps(f"pg{j}") for j in range(2)]

        small, halo = m.small, m.halo
        ada_in = [sem(f"p_ada_in{j}") for j in range(2)]
        w_in = [sem(f"p_w_in{j}") for j in range(2)]
        silu = sem("p_silu")
        ada_mm = sem("p_ada_mm")
        w_max = sem("p_w_max")
        w_hi = sem("p_w_hi")
        w_lo = sem("p_w_lo")
        step = sem("p_step")
        allmax = sem("p_allmax")
        const0 = sem("p_const0")
        zero = sb("zero", [P, m.HALO])
        nsmall = 10

        with nc.Block() as block:
            @block.sync
            def _(sp):
                for k in range(KT):
                    if k >= 2:
                        sp.wait_ge(ada_mm, k - 1)
                    sp.dma_start(adaw[:, k % 2, :], a.ada_w[0, k * P:(k + 1) * P, :]).then_inc(ada_in[k % 2], 16)
                    if k >= 2:
                        sp.wait_ge(w_lo, k - 1)
                    sp.dma_start(wst[:, k % 2, :], a.w_in[0, k * P:(k + 1) * P, :]).then_inc(w_in[k % 2], 16)

            @block.gpsimd
            def _(pool):
                nc.gpsimd.memset(m.ident[:], 0.0).then_inc(const0, 1)
                nc.gpsimd.memset(zero[:], 0.0).then_inc(const0, 1)
                pool.wait_ge(const0, 2)
                nc.gpsimd.affine_select(out=m.ident[:], in_=m.ident[:], compare_op=ALU.not_equal, fill=1.0,
                                        base=0, pattern=[[-1, P]], channel_multiplier=1).then_inc(const0, 1)
                pool.dma_start(ccol[:], a.c.rearrange("o (k p) -> p (o k)", p=P), allow_slow_non_contiguous=True).then_inc(small, 16)
                pool.dma_start(abcol[:], a.ada_b[0, 0:2 * DM].rearrange("(k p) -> p k", p=P), allow_slow_non_contiguous=True).then_inc(small, 16)
                pool.dma_start(npre[:], a.norm_pre[0].rearrange("(k p) -> p k", p=P), allow_slow_non_contiguous=True).then_inc(small, 16)
                pool.dma_start(m.gate[:], a.ada_b[0:1, 2 * DM:3 * DM].partition_broadcast(P)).then_inc(small, 16)
                pool.dma_start(gains[:, 0, :], a.fox_q_gain[0:1, :].partition_broadcast(P)).then_inc(small, 16)
                pool.dma_start(gains[:, 1, :], a.fox_k_gain[0:1, :].partition_broadcast(P)).then_inc(small, 16)
                for j, g in enumerate((a.fox_q_gain, a.fox_k_gain)):
                    for half in range(2):
                        pool.dma_start(m.qkgain[half * HD:(half + 1) * HD, j:j + 1],
                                       column(g[0]), allow_slow_non_contiguous=True).then_inc(small, 16)
                for k in range(ZC // P):
                    pool.dma_start(m.Z[k * P:(k + 1) * P, 0:m.HALO], zero[:]).then_inc(halo, 16)
                pool.wait_ge(w_max, KT + 1)
                nc.gpsimd.partition_all_reduce(bnd[:, 1:2], bnd[:, 0:1], P, RMAX).then_inc(allmax, 1)
                pool.wait_ge(halo, 16 * (ZC // P))

            @block.scalar
            def _(act):
                act.wait_ge(small, 16 * nsmall)
                nc.scalar.activation(csig[:], ccol[:], ACT.Sigmoid).then_inc(silu, 1)
                for k in range(KT):
                    act.wait_ge(w_max, k + 1)
                    nc.scalar.activation(m.wh[:, k, :], wst[:, k % 2, :], ACT.Copy,
                                         scale=rinv[:, k:k + 1]).then_inc(w_hi, 1)

            @block.tensor
            def _(pe):
                pe.wait_ge(silu, 3)
                for k in range(KT):
                    pe.wait_ge(ada_in[k % 2], 16 * (k // 2 + 1))
                    for j in range(2 * KT):
                        nc.tensor.matmul(pcol[:, j:j + 1], adaw[:, k % 2, j * P:(j + 1) * P], ccol[:, k:k + 1],
                                         start=(k == 0 and j == 0), stop=(k == KT - 1), skip_group_check=True)
                    for j in range(2):
                        mm = nc.tensor.matmul(pg[j][:], cbc[:, k, :],
                                              adaw[:, k % 2, 2 * DM + j * 512:2 * DM + (j + 1) * 512],
                                              start=(k == 0), stop=(k == KT - 1))
                    mm.then_inc(ada_mm, 1)

            @block.vector
            def _(dve):
                n = [0]

                def chain(ins):
                    n[0] += 1
                    ins.then_inc(step, 1)
                    dve.wait_ge(step, n[0])

                chain(nc.vector.memset(onesf[:], 1.0))
                nc.vector.memset(m.eps[:, 0:1], EPS)
                nc.vector.memset(m.eps[:, 1:2], GN_EPS)
                nc.vector.memset(m.eps[:, 2:3], 1e-24)
                chain(nc.vector.memset(m.eps[:, 3:4], 1.0))
                chain(nc.vector.memset(m.headmean[:], 0.0))
                for half in range(2):
                    sl = slice(half * HD, (half + 1) * HD)
                    chain(nc.vector.memset(m.headmean[sl, sl], 1.0 / HD))
                dve.wait_ge(silu, 1)
                dve.wait_ge(small, 16 * nsmall)
                nc.vector.tensor_tensor(ccol[:], ccol[:], csig[:], ALU.mult).then_inc(silu, 1)
                dve.wait_ge(silu, 2)
                for k in range(KT):
                    last = nc.vector.tensor_scalar(cbc[:, k, :], onesf[:], ccol[:, k:k + 1], None, ALU.mult)
                last.then_inc(silu, 1)
                chain(nc.vector.tensor_reduce(gm[:, 0:2], gains[:], AX.X, ALU.max, apply_absolute_value=True))
                chain(nc.vector.tensor_scalar(gm[:, 0:2], gm[:, 0:2], 0.5, 1.0 / 32.0, ALU.max, ALU.mult))
                chain(nc.vector.reciprocal(gm[:, 2:4], gm[:, 0:2]))
                chain(nc.vector.tensor_tensor(m.qkgain[:], m.qkgain[:], gm[:, 2:4], ALU.mult))
                chain(nc.vector.scalar_tensor_tensor(m.sc[:, 0:1], gm[:, 0:1], HD ** -0.5, gm[:, 1:2],
                                                     ALU.mult, ALU.mult))
                chain(nc.vector.reciprocal(m.sc[:, 1:2], m.sc[:, 0:1]))
                for k in range(KT):
                    dve.wait_ge(w_in[k % 2], 16 * (k // 2 + 1))
                    chain(nc.vector.tensor_reduce(rowmax[:, k:k + 1], wst[:, k % 2, :], AX.X, ALU.max,
                                                  apply_absolute_value=True))
                    chain(nc.vector.tensor_scalar(rowmax[:, k:k + 1], rowmax[:, k:k + 1], 1e-20, 1.0 / TOP,
                                                  ALU.max, ALU.mult))
                    nc.vector.reciprocal(rinv[:, k:k + 1], rowmax[:, k:k + 1]).then_inc(w_max, 1)
                    dve.wait_ge(w_hi, k + 1)
                    nc.vector.scalar_tensor_tensor(m.wl[:, k, :], wst[:, k % 2, :], rinv[:, k:k + 1],
                                                   m.wh[:, k, :], ALU.mult, ALU.subtract).then_inc(w_lo, 1)
                dve.wait_ge(ada_mm, KT)
                dve.wait_ge(w_lo, KT)
                chain(nc.vector.tensor_tensor(abcol[:], pcol[:, 0:2 * KT], abcol[:], ALU.add))
                for j in range(2):
                    chain(nc.vector.tensor_tensor(m.gate[:, j * 512:(j + 1) * 512], pg[j][:],
                                                  m.gate[:, j * 512:(j + 1) * 512], ALU.add))
                chain(nc.vector.scalar_tensor_tensor(gcol[:], abcol[:, KT:2 * KT], 1.0, npre[:], ALU.add, ALU.mult))
                chain(nc.vector.tensor_tensor(gcol[:], gcol[:], rowmax[:], ALU.mult))
                chain(nc.vector.tensor_tensor(scol[:], abcol[:, 0:KT], rowmax[:], ALU.mult))
                chain(nc.vector.tensor_reduce(bnd[:, 2:3], gcol[:], AX.X, ALU.max, apply_absolute_value=True))
                chain(nc.vector.tensor_reduce(bnd[:, 3:4], scol[:], AX.X, ALU.max, apply_absolute_value=True))
                nc.vector.tensor_tensor(bnd[:, 0:1], bnd[:, 2:3], bnd[:, 3:4], ALU.add).then_inc(w_max, 1)
                dve.wait_ge(allmax, 1)
                chain(nc.vector.tensor_scalar(m.sc[:, 2:3], bnd[:, 1:2], 1e-30, 32.0 / TOP, ALU.max, ALU.mult))
                chain(nc.vector.reciprocal(m.sc[:, 3:4], m.sc[:, 2:3]))
                chain(nc.vector.tensor_scalar(m.sc[:, 4:5], m.sc[:, 2:3], 2.0 ** 20, None, ALU.mult))
                chain(nc.vector.tensor_scalar(m.gcol[:], gcol[:], m.sc[:, 3:4], None, ALU.mult))
                chain(nc.vector.tensor_scalar(m.scol[:], scol[:], m.sc[:, 3:4], None, ALU.mult))


def project(nc, a, m):
    with ExitStack() as ctx:
        sb, ps, sem, count = scope(nc, ctx, "project")
        jobs = [("qk", n) for n in range(8)] + [("z", n) for n in range(ZC // P)] + \
            [("v", t) for t in range(4)] + [("g", (t, j)) for t in range(4) for j in range(2)]
        NJ = len(jobs)
        assert NJ % 2 == 1
        T_JOB = 11
        TURNS = NB // 2
        NQK = 16

        xt = sb("xt", [P, 4, DM])
        sqx = sb("sqx", [P, DM])
        ssq = sb("ssq", [P, 4])
        rstd = sb("rstd", [P, 4])
        rstd2 = sb("rstd2", [P, 4])
        h32 = sb("h32", [P, 2, BT])
        hh = sb("hh", [P, 2, KT, BT], F16)
        hl = sb("hl", [P, 2, KT, BT], F16)
        uq = sb("uq", [P, 2, BT])
        sq = sb("sq", [P, 2, BT])
        stdb = sb("stdb", [P, BT])
        rec = sb("rec", [P, BT])
        qn = sb("qn", [P, BT])
        sig = sb("sig", [P, BT])
        stage = [sb(f"stage{j}", [P, BT]) for j in range(2)]
        stage16 = [s[:, :].bitcast(F16).rearrange("p (two t) -> p two t", two=2) for s in stage]
        fbc = sb("fbc", [P, 4, FOX_HEADS])
        ptr = [ps(f"ptr{j}") for j in range(2)]
        pmm = [ps(f"pmm{j}") for j in range(2)]
        pss = ps("pss")
        pf = ps("pf")

        x_in = [sem(f"x_in{j}") for j in range(4)]
        sq_done, std_done = count("sq_done", 4), count("std_done", 1)
        rstd_done, xn_done = count("rstd_done", 1), count("xn_done", 4, 4)
        tr_done = count("tr_done", KT, KT)
        h32_done, hi_done, lo_done = count("h32_done", KT, 1), count("hi_done", KT), count("lo_done", KT, 1)
        f_mm, f_out = count("f_mm", 1), count("f_out", 1, 1)
        mm_done = count("mm_done", 2 * NJ)
        qk_sq, qk_ss, qk_std = count("qk_sq", NQK), count("qk_ss", NQK, 1), count("qk_std", NQK)
        qk_rec, qk_n, qk_hi, qk_u = count("qk_rec", NQK), count("qk_n", NQK, 1), count("qk_hi", NQK), count("qk_u", NQK)
        v_hi, sig_done = count("v_hi", 8), count("sig_done", 16)
        ready = [count(f"stage_ready{j}", NJ) for j in range(2)]
        sent = [count(f"stage_sent{j}", 16 * NJ) for j in range(2)]
        fb_in = sem("fb_in")
        passed, pool_passed = sem("passed"), sem("pool_passed")

        def slot(u, n):
            return (u * NJ + n) % 2, (u * NJ + n) // 2

        def wait_filled(eng, i, u, n):
            s, used = slot(u, n)
            eng.wait_ge(ready[s].sem, ready[s].past(i, used + 1))

        with nc.Block() as block:
            @block.sync
            def _(sp):
                for t in range(4):
                    sp.dma_start(fbc[:, t, :], a.fox_f_bias[0:1, :].partition_broadcast(P)).then_inc(fb_in, 16)

                def load_x(seq, blk):
                    sp.wait_ge(tr_done.sem, tr_done.past(seq, 0))
                    sp.sem_inc(passed, 1)
                    for j in range(4):
                        sp.dma_start(xt[:, j, :], a.x[0, bass.ds(blk * BT + j * P, P), :]).then_inc(x_in[j], 16)

                def store(i, u, n):
                    kind, w = jobs[n]
                    s, used = slot(u, n)
                    t0 = (i * 2 + u) * BT
                    if kind == "qk":
                        c0 = (w % 4) * P
                        dst = m.QK[w // 4, :, c0:c0 + P, bass.ds(t0, BT)].rearrange("two c t -> c two t")
                        src = stage16[s]
                    elif kind == "z":
                        dst, src = m.Z[w * P:(w + 1) * P, bass.ds(t0 + m.HALO, BT)], stage[s][:]
                    elif kind == "v":
                        dst, src = m.V[bass.ds(t0 + w * P, P), :, :], stage16[s]
                    else:
                        dst, src = m.G[bass.ds(t0 + w[0] * P, P), w[1] * 512:(w[1] + 1) * 512], stage[s][:]
                    sp.wait_ge(ready[s].sem, ready[s].past(i, used + 1))
                    sp.sem_inc(passed, 1)
                    sp.dma_start(dst, src).then_inc(sent[s].sem, 16)

                load_x(0, 0)
                with sp.Fori(0, TURNS) as i:
                    for u in range(2):
                        load_x(i * 2 + (u + 1), (i * 2 + (u + 1)) % NB)
                        for n in range(NJ):
                            store(i, u, n)
                for s in range(2):
                    sp.wait_ge(sent[s].sem, 16 * TURNS * NJ)

            @block.tensor
            def _(pe):
                pe.sem_inc(tr_done.sem, tr_done.credit)
                pe.sem_inc(qk_ss.sem, qk_ss.credit)

                def turn_x(seq, k):
                    if k == 0:
                        pe.wait_ge(xn_done.sem, xn_done.past(seq, 4))
                    pe.wait_ge(h32_done.sem, h32_done.past(seq, k - 1))
                    for j in range(4):
                        t = nc.tensor.transpose(ptr[k % 2][:, j * P:(j + 1) * P], xt[:, j, k * P:(k + 1) * P], m.ident[:])
                    t.then_inc(tr_done.sem, 1)

                def products(out, lhs, rhs):
                    for k in range(KT):
                        for c, (l, r) in enumerate(((0, 0), (0, 1), (1, 0))):
                            mm = nc.tensor.matmul(out, lhs(l, k), rhs(r, k), start=(k == 0 and c == 0),
                                                  stop=(k == KT - 1 and c == 2))
                    return mm

                h, w = (hh, hl), (m.wh, m.wl)

                def job(i, u, n):
                    kind, x = jobs[n]
                    s, used = slot(u, n)
                    if 2 <= n < 10:
                        pe.wait_ge(qk_u.sem, qk_u.past(i, u * 8 + n - 1))
                    else:
                        wait_filled(pe, i, u, n - 2)
                    if kind in ("qk", "z"):
                        c0 = x * P if kind == "qk" else Z_COL + x * P
                        products(pmm[s][:], lambda l, k: w[l][:, k, c0:c0 + P],
                                 lambda r, k: h[r][:, u, k, :]).then_inc(mm_done.sem, 1)
                    else:
                        t, c0 = (x, V_COL) if kind == "v" else (x[0], G_COL + x[1] * 512)
                        products(pmm[s][:], lambda l, k: h[l][:, u, k, t * P:(t + 1) * P],
                                 lambda r, k: w[r][:, k, c0:c0 + 512]).then_inc(mm_done.sem, 1)

                def head_means(i, u, x):
                    pe.wait_ge(qk_sq.sem, qk_sq.past(i, u * 8 + x + 1))
                    pe.wait_ge(qk_std.sem, qk_std.past(i, u * 8 + x))
                    nc.tensor.matmul(pss[:], m.headmean[:], sq[:, x % 2, :], start=True, stop=True).then_inc(qk_ss.sem, 1)

                for k in range(KT):
                    turn_x(0, k)
                with pe.Fori(0, TURNS) as i:
                    for u in range(2):
                        blk = i * 2 + u
                        pe.wait_ge(hi_done.sem, hi_done.past(blk, KT))
                        pe.wait_ge(lo_done.sem, lo_done.past(blk, KT))
                        pe.wait_ge(f_out.sem, f_out.past(blk, 0))
                        for t in range(4):
                            mm = products(pf[:, t * 8:(t + 1) * 8], lambda l, k: h[l][:, u, k, t * P:(t + 1) * P],
                                          lambda r, k: w[r][:, k, F_COL:F_COL + FOX_HEADS])
                        mm.then_inc(f_mm.sem, 1)
                        for n in range(NJ):
                            job(i, u, n)
                            if 1 <= n <= 8:
                                head_means(i, u, n - 1)
                            if T_JOB <= n < T_JOB + KT:
                                turn_x(i * 2 + (u + 1), n - T_JOB)

            @block.scalar
            def _(act):
                act.sem_inc(h32_done.sem, h32_done.credit)

                def x_squares(seq, j):
                    act.wait_ge(x_in[j], (seq + 1) * 16)
                    nc.scalar.activation(sqx[:], xt[:, j, :], ACT.Square, accum_out=ssq[:, j:j + 1]).then_inc(sq_done.sem, 1)
                    act.wait_ge(sq_done.sem, sq_done.past(seq, j + 1))

                def x_std(seq):
                    act.wait_ge(xn_done.sem, xn_done.past(seq, 0))
                    nc.scalar.activation(rstd[:], ssq[:], ACT.Sqrt, bias=m.eps[:, 0:1], scale=1.0 / DM)\
                        .then_inc(std_done.sem, 1)
                    act.wait_ge(std_done.sem, std_done.past(seq, 1))

                def h_hi(seq, side, k):
                    act.wait_ge(tr_done.sem, tr_done.past(seq, k + 1))
                    act.wait_ge(lo_done.sem, lo_done.past(seq, k - 1))
                    nc.scalar.activation(h32[:, k % 2, :], ptr[k % 2][:], ACT.Identity, bias=m.scol[:, k:k + 1],
                                         scale=m.gcol[:, k:k + 1]).then_inc(h32_done.sem, 1)
                    act.wait_ge(h32_done.sem, h32_done.past(seq, k + 1))
                    nc.scalar.activation(hh[:, side, k, :], h32[:, k % 2, :], ACT.Copy).then_inc(hi_done.sem, 1)

                def evacuate(i, u, n):
                    kind, x = jobs[n]
                    s, used = slot(u, n)
                    act.wait_ge(mm_done.sem, mm_done.past(i, u * NJ + n + 1))
                    if kind == "qk":
                        act.wait_ge(qk_ss.sem, qk_ss.past(i, u * 8 + x - 1))
                        nc.scalar.activation(sq[:, x % 2, :], pmm[s][:], ACT.Square, scale=m.sc[:, 2:3])\
                            .then_inc(qk_sq.sem, 1)
                        act.wait_ge(qk_n.sem, qk_n.past(i, u * 8 + x - 1))
                        nc.scalar.activation(uq[:, x % 2, :], pmm[s][:], ACT.Copy, scale=m.sc[:, 2:3])\
                            .then_inc(qk_u.sem, 1)
                    elif kind == "z":
                        act.wait_ge(sent[s].sem, sent[s].past(i, 16 * used))
                        nc.scalar.activation(stage[s][:], pmm[s][:], ACT.Copy, scale=m.sc[:, 2:3])\
                            .then_inc(ready[s].sem, 1)
                    elif kind == "v":
                        act.wait_ge(sent[s].sem, sent[s].past(i, 16 * used))
                        nc.scalar.activation(stage16[s][:, 0, :], pmm[s][:], ACT.Copy, scale=2.0 ** -20)\
                            .then_inc(v_hi.sem, 1)
                    else:
                        wait_filled(act, i, u, n - 1 if n > NJ - 8 else -1)
                        nc.scalar.activation(sig[:], pmm[s][:], ACT.Sigmoid, scale=m.sc[:, 2:3])\
                            .then_inc(sig_done.sem, 1)

                def head_std(i, u, x):
                    act.wait_ge(qk_ss.sem, qk_ss.past(i, u * 8 + x + 1))
                    act.wait_ge(qk_rec.sem, qk_rec.past(i, u * 8 + x))
                    nc.scalar.activation(stdb[:], pss[:], ACT.Sqrt, bias=m.eps[:, 0:1]).then_inc(qk_std.sem, 1)

                for j in range(4):
                    x_squares(0, j)
                x_std(0)
                for k in range(KT):
                    h_hi(0, 0, k)
                with act.Fori(0, TURNS) as i:
                    for u in range(2):
                        seq = i * 2 + (u + 1)
                        for n in range(NJ):
                            evacuate(i, u, n)
                            if 1 <= n <= 8:
                                head_std(i, u, n - 1)
                            if 2 <= n <= 5:
                                x_squares(seq, n - 2)
                            if n == 6:
                                x_std(seq)
                            if T_JOB <= n < T_JOB + KT:
                                h_hi(seq, 1 - u, n - T_JOB)

            @block.vector
            def _(dve):
                dve.sem_inc(xn_done.sem, xn_done.credit)
                dve.sem_inc(lo_done.sem, lo_done.credit)
                dve.sem_inc(f_out.sem, f_out.credit)
                dve.sem_inc(qk_n.sem, qk_n.credit)

                def x_scaled(seq):
                    dve.wait_ge(std_done.sem, std_done.past(seq, 1))
                    nc.vector.reciprocal(rstd2[:], rstd[:]).then_inc(rstd_done.sem, 1)
                    dve.wait_ge(rstd_done.sem, rstd_done.past(seq, 1))
                    for j in range(4):
                        nc.vector.tensor_scalar(xt[:, j, :], xt[:, j, :], rstd2[:, j:j + 1], None, ALU.mult)\
                            .then_inc(xn_done.sem, 1)

                def h_lo(seq, side, k):
                    dve.wait_ge(hi_done.sem, hi_done.past(seq, k + 1))
                    nc.vector.tensor_tensor(hl[:, side, k, :], h32[:, k % 2, :], hh[:, side, k, :], ALU.subtract)\
                        .then_inc(lo_done.sem, 1)

                def normalise(i, u, x):
                    dve.wait_ge(qk_std.sem, qk_std.past(i, u * 8 + x + 1))
                    nc.vector.reciprocal(rec[:], stdb[:]).then_inc(qk_rec.sem, 1)
                    dve.wait_ge(qk_rec.sem, qk_rec.past(i, u * 8 + x + 1))
                    wait_filled(dve, i, u, x - 1 if x else -2)
                    nc.vector.scalar_tensor_tensor(qn[:], uq[:, x % 2, :], m.qkgain[:, x // 4:x // 4 + 1], rec[:],
                                                   ALU.mult, ALU.mult).then_inc(qk_n.sem, 1)

                def finish(i, u, n):
                    kind, x = jobs[n]
                    s, used = slot(u, n)
                    if kind == "v":
                        dve.wait_ge(v_hi.sem, v_hi.past(i, u * 4 + x + 1))
                        nc.vector.scalar_tensor_tensor(stage16[s][:, 1, :], pmm[s][:], 2.0 ** -20, stage16[s][:, 0, :],
                                                       ALU.mult, ALU.subtract)\
                            .then_inc(ready[s].sem, 1)
                    elif kind == "g":
                        dve.wait_ge(sig_done.sem, sig_done.past(i, u * 8 + n - (NJ - 8) + 1))
                        dve.wait_ge(sent[s].sem, sent[s].past(i, 16 * used))
                        nc.vector.scalar_tensor_tensor(stage[s][:], pmm[s][:], m.sc[:, 2:3], sig[:], ALU.mult, ALU.mult)\
                            .then_inc(ready[s].sem, 1)

                x_scaled(0)
                for k in range(KT):
                    h_lo(0, 0, k)
                dve.wait_ge(fb_in, 64)
                with dve.Fori(0, TURNS) as i:
                    for u in range(2):
                        seq = i * 2 + (u + 1)
                        blk = i * 2 + u
                        dve.wait_ge(f_mm.sem, f_mm.past(blk, 1))
                        nc.vector.scalar_tensor_tensor(
                            m.fl[:, bass.ds(blk * (4 * FOX_HEADS), 4 * FOX_HEADS)], pf[:, 0:32],
                            m.sc[:, 2:3], fbc[:].rearrange("p t h -> p (t h)"), ALU.mult, ALU.add).then_inc(f_out.sem, 1)
                        for n in range(NJ):
                            finish(i, u, n)
                            if 1 <= n <= 8:
                                normalise(i, u, n - 1)
                            if n == 9:
                                x_scaled(seq)
                            if T_JOB <= n < T_JOB + KT:
                                h_lo(seq, 1 - u, n - T_JOB)

            @block.gpsimd
            def _(pool):
                with pool.Fori(0, TURNS) as i:
                    for u in range(2):
                        for x in range(8):
                            s, used = slot(u, x)
                            pool.wait_ge(qk_n.sem, qk_n.past(i, u * 8 + x + 1))
                            pool.wait_ge(sent[s].sem, sent[s].past(i, 16 * used))
                            pool.sem_inc(pool_passed, 1)
                            nc.gpsimd.tensor_copy(stage16[s][:, 0, :], qn[:]).then_inc(qk_hi.sem, 1)
                            pool.wait_ge(qk_hi.sem, qk_hi.past(i, u * 8 + x + 1))
                            nc.gpsimd.tensor_tensor(stage16[s][:, 1, :], qn[:], stage16[s][:, 0, :], ALU.subtract)\
                                .then_inc(ready[s].sem, 1)


def decay(nc, a, m):
    with ExitStack() as ctx:
        sb, ps, sem, count = scope(nc, ctx, "decay")
        NF = NT * FOX_HEADS
        tri = sb("tri", [P, P])
        ones = sb("ones", [P, P])
        ab, ex, ln = sb("ab", [P, NF]), sb("ex", [P, NF]), sb("ln", [P, NF])
        tot = sb("tot", [P, FOX_HEADS, NT])
        crow = sb("crow", [P, 2, P])
        clamp = sb("clamp", [P, 1])
        pw, pt, pc = ps("pw"), ps("pt"), ps("pc")
        made, ones_made = sem("d_made"), sem("d_ones")
        abs_done, exp_done, ln_done, log_done = (sem("d_" + n) for n in ("abs", "exp", "ln", "log"))
        sums, cum_done, turned, rows, stored, step = (sem("d_" + n) for n in ("sums", "cum", "turned", "rows", "stored", "step"))
        with nc.Block() as block:
            @block.gpsimd
            def _(pool):
                nc.gpsimd.memset(tri[:], 1.0).then_inc(made, 1)
                pool.wait_ge(made, 1)
                nc.gpsimd.affine_select(out=tri[:], in_=tri[:], compare_op=ALU.is_ge, fill=0.0, base=0,
                                        pattern=[[1, P]], channel_multiplier=-1).then_inc(made, 1)

            @block.scalar
            def _(act):
                act.wait_ge(abs_done, 1)
                nc.scalar.activation(ex[:], ab[:], ACT.Exp, scale=-1.0).then_inc(exp_done, 1)
                act.wait_ge(exp_done, 1)
                nc.scalar.activation(ln[:], ex[:], ACT.Ln, bias=m.eps[:, 3:4]).then_inc(ln_done, 1)

            @block.tensor
            def _(pe):
                pe.wait_ge(made, 2)
                pe.wait_ge(ones_made, 1)
                pe.wait_ge(log_done, 1)
                nc.tensor.matmul(pw[:, 0:NF], tri[:], m.fl[:], start=True, stop=True)
                nc.tensor.matmul(pt[:, 0:NF], ones[:], m.fl[:], start=True, stop=True).then_inc(sums, 1)
                pe.wait_ge(cum_done, 1)
                cums = m.cum[:].rearrange("p h t -> p (h t)")
                for j in range(2):
                    t = nc.tensor.transpose(pc[:, j * P:(j + 1) * P], cums[:, j * P:(j + 1) * P], m.ident[:])
                t.then_inc(turned, 1)

            @block.vector
            def _(dve):
                n = [0]

                def chain(ins):
                    n[0] += 1
                    ins.then_inc(step, 1)
                    dve.wait_ge(step, n[0])

                nc.vector.memset(ones[:], 1.0).then_inc(ones_made, 1)
                nc.vector.scalar_tensor_tensor(ab[:], m.fl[:], -1.0, m.fl[:], ALU.mult, ALU.max).then_inc(abs_done, 1)
                chain(nc.vector.tensor_scalar(clamp[:], m.sc[:, 0:1], -500.0 * 1024.0 * HD ** 0.5, None, ALU.mult))
                dve.wait_ge(ln_done, 1)
                chain(nc.vector.scalar_tensor_tensor(ab[:], m.fl[:], 0.0, ln[:], ALU.min, ALU.subtract))
                nc.vector.tensor_scalar(m.fl[:], ab[:], clamp[:, 0:1], None, ALU.max).then_inc(log_done, 1)
                dve.wait_ge(sums, 1)
                chain(nc.vector.tensor_copy(tot[:], pt[:, 0:NF].rearrange("p (t h) -> p h t", h=FOX_HEADS)))
                chain(nc.vector.memset(m.off[:], 0.0))
                for h in range(FOX_HEADS):
                    chain(nc.vector.tensor_tensor_scan(m.off[:, h, 1:NT], ones[:, 0:NT - 1], tot[:, h, 0:NT - 1], 0.0,
                                                       ALU.mult, ALU.add))
                nc.vector.tensor_tensor(m.cum[:], pw[:, 0:NF].rearrange("p (t h) -> p h t", h=FOX_HEADS), m.off[:],
                                        ALU.add).then_inc(cum_done, 1)
                dve.wait_ge(turned, 1)
                nc.vector.tensor_scalar(crow[:].rearrange("p j t -> p (j t)"), pc[:, 0:2 * P], m.sc[:, 1:2], -1.0,
                                        ALU.mult, ALU.mult).then_inc(rows, 1)

            @block.sync
            def _(sp):
                sp.wait_ge(rows, 1)
                sp.dma_start(m.NC.rearrange("h (t p) -> (h t) p", p=P).rearrange("(j q) p -> q j p", j=2), crow[:])\
                    .then_inc(stored, 16)
                sp.wait_ge(stored, 16)


def persistent(nc, ctx):
    sb, ps, sem, count = scope(nc, ctx, "layer")
    m = Layer()
    m.HALO = 16
    m.first = sem("attend_first")
    m.small, m.halo = sem("small_in"), sem("halo_out")
    m.passed = sem("passed_on")
    m.ident = sb("ident", [P, P])
    m.headmean = sb("headmean", [P, P])
    m.eps = sb("eps", [P, 4])
    m.sc = sb("sc", [P, 8])
    m.gcol = sb("gcol_s", [P, KT])
    m.scol = sb("scol_s", [P, KT])
    m.gate = sb("gate", [P, DM])
    m.qkgain = sb("qkgain", [P, 2])
    m.fl = sb("fl", [P, NT * FOX_HEADS])
    m.cum = sb("cum", [P, FOX_HEADS, NT])
    m.off = sb("off", [P, FOX_HEADS, NT])
    return m


def recur(nc, a, m):
    with ExitStack() as ctx:
        sb, ps, sem, count = scope(nc, ctx, "recur")
        C, CB = P, BT // P
        NR = 7
        H = RWKV_HEADS

        zin = sb("zin", [P, NR, BT + 1])
        pin = sb("pin", [P, 2, BT + 16])
        zf = sb("zf", [P, NR, BT])
        mu = sb("mu", [P, NR])
        vec = sb("vec", [P, 8, 2])
        wa = sb("wa", [P, 2, 2, P])
        rkc = sb("rkc", [P, 2, H])
        sw = sb("sw", [P, 2, BT])
        av = sb("av", [P, 2, BT])
        ls = sb("ls", [P, 2 * CB, C + 1])
        lc = sb("lc", [P, 2 * CB, C + 1])
        ec = sb("ec", [P, 2 * CB, C + 1])
        ei = sb("ei", [P, 2 * CB, C + 1])
        kk = sb("kk", [P, 2, BT])
        ksq = sb("ksq", [P, 2, BT])
        at, bt, kt, rt = (sb(n, [P, 2, BT]) for n in ("at", "bt", "kt", "rt"))
        rk = sb("rk", [P, 2, BT])
        ar = sb("ar", [P, 2, CB, 2, 2, C])
        onesf = sb("onesr", [P, C])
        mA = sb("mA", [P, 2, 2, C], I32)
        mX1 = sb("mX1", [P, 2, C], I32)
        mN = sb("mN", [P, 5, C], I32)
        mT = sb("mT", [P, 2, C], I32)
        mf = sb("mf", [P, C])
        abr = sb("abr", [P, 2, H, 2, C])
        akr = sb("akr", [P, 2, H, 2, C])
        X = sb("X", [P, 2, H, C])
        XT = sb("XT", [P, 2, H, C])
        T = sb("T", [P, 2, H, C])
        bkt = sb("bkt", [P, 2, 4, P])
        vt = sb("vt", [P, 2, 2, P])
        r1 = sb("r1", [P, 2 * P])
        U = sb("U", [P, 2 * P])
        S = sb("S", [P, 2, P])
        Zc = sb("Zc", [P, 2, P])
        Zs = sb("Zs", [P, 2, P])
        ost = sb("ost", [P, CB, 2 * P])
        bon = sb("bon", [P, CB, H])
        vall = sb("vall", [P, CB, 2 * P])
        st = sb("st", [P, 4, CB * H])
        osq = sb("osq", [P, CB, 2 * P])
        lng = sb("lng", [P, 2 * P])
        lnb = sb("lnb", [P, 2 * P])
        psc = sb("psc", [P, 2 * P])
        pwb = sb("pwb", [P, 2, P])
        s2, s4 = (sb(n, [P, 2, BT + 16]) for n in ("s2", "s4"))
        rc = sb("rc", [P, 2, BT])
        it16 = sb("it16", [P, 16])
        pooled = sb("pooled", [P, 2, BT])
        yp = sb("yp", [P, CB, 2 * P])
        bank = [ps(f"bank{j}") for j in range(8)]

        cst, par, cstep, dset, rc_set = sem("r_cst"), sem("r_par"), sem("r_cstep"), sem("r_dset"), sem("rc_set")
        z_in, p_in, y_out, yp_out = sem("z_in"), sem("p_in"), sem("y_out"), sem("yp_out")
        shifted, tanh_d, wa_mm, gates_d, lc_d, exp_d, ksq_d, kk_mm, kstd_d, ops_d, bd_d, gn_var, gn_std, gn_rec, y_d, \
            pin_read, pool_d, pp_mm, pp_d = (count(n, 1) for n in (
                "shifted", "tanh_d", "wa_mm", "gates_d", "lc_d", "exp_d", "ksq_d", "kk_mm", "kstd_d", "ops_d", "bd_d",
                "gn_var", "gn_std", "gn_rec", "y_d", "pin_read", "pool_d", "pp_mm", "pp_d"))
        tr_mm, tok_d, a_mm, a_d, r_mm, r_d, u_mm, u_d, s_mm, s_d, z_d, o_mm, o_d, v_d = (count("c_" + n, CB) for n in (
            "tr_mm", "tok_d", "a_mm", "a_d", "r_mm", "r_d", "u_mm", "u_d", "s_mm", "s_d", "z_d", "o_mm", "o_d", "v_d"))
        NL = 6
        t_mm, t_d, d_mm, x_d = count("t_mm", NL * CB), count("t_d", NL * CB), count("d_mm", NL * CB), count("x_d", (NL + 1) * CB)
        NDV, NPO = 41, 17
        dstep, pstep = count("dstep", NDV), count("pstep", NPO)
        npar = 14 + 5

        def level(c, l):
            return (c // 2) * 2 * NL + l * 2 + c % 2 + 1

        def inverse(c, l):
            return (c // 2) * 2 * (NL + 1) + (l + 1) * 2 + c % 2 + 1

        def chunked(t):
            return t[:].rearrange("p k (c t) -> p (k c) t", t=C)

        def heads4(mask):
            return mask.unsqueeze(1).to_broadcast([P, H, C])

        with nc.Block() as block:
            @block.sync
            def _(sp):
                n = [0]

                def load(dst, src):
                    n[0] += 1
                    sp.dma_start(dst, src, allow_slow_non_contiguous=True).then_inc(par, 16)

                load(mu[:], a.rwkv_mu[0].rearrange("(k p) -> p k", p=P))
                for j, v in enumerate((a.rwkv_w0, a.rwkv_a0, a.rwkv_k_k, a.rwkv_k_a)):
                    load(vec[:, j, :], v[0].rearrange("(k p) -> p k", p=P))
                sp.wait_ge(cst, 1)
                load(wa[0:RANK, 0, :, :], a.rwkv_w2[0].rearrange("r (k c) -> r k c", c=P))
                load(wa[RANK:P, 1, :, :], a.rwkv_a2[0].rearrange("r (k c) -> r k c", c=P))
                for g in range(4):
                    hs = slice((g % 2) * 64, (g % 2) * 64 + 64)
                    load(pwb[hs, g // 2, hs], a.pool_w[0, g])
                    load(rkc[hs, g // 2, g:g + 1], column(a.rwkv_r_k[0, g]))
                load(lng[:], a.rwkv_ln_g[0:1, :].partition_broadcast(P))
                load(lnb[:], a.rwkv_ln_b[0:1, :].partition_broadcast(P))
                load(psc[:], a.pool_scale[0:1, :].partition_broadcast(P))
                assert n[0] == npar - 1, n
                with sp.Fori(0, NB) as i:
                    sp.wait_ge(shifted.sem, shifted.past(i, 0))
                    sp.sem_inc(m.passed, 1)
                    sp.dma_start(zin[:], m.Z[0:NR * P, bass.ds(i * BT + (m.HALO - 1), BT + 1)]
                                 .rearrange("(k p) t -> p k t", p=P)).then_inc(z_in, 16)
                    sp.wait_ge(pool_d.sem, pool_d.past(i, 0))
                    sp.sem_inc(m.passed, 1)
                    sp.dma_start(pin[:], m.Z[NR * P:ZC, bass.ds(i * BT, BT + 16)]
                                 .rearrange("(k p) t -> p k t", p=P)).then_inc(p_in, 16)
                    sp.wait_ge(pp_d.sem, pp_d.past(i, 1))
                    sp.sem_inc(m.passed, 1)
                    sp.dma_start(m.Y[bass.ds(i * BT, BT), FOX_W + RWKV_W:DM].rearrange("(c p) f -> p c f", p=P), yp[:])\
                        .then_inc(yp_out, 16)
                    sp.wait_ge(y_d.sem, y_d.past(i, 1))
                    sp.sem_inc(m.passed, 1)
                    sp.dma_start(m.Y[bass.ds(i * BT, BT), FOX_W:FOX_W + RWKV_W].rearrange("(c p) f -> p c f", p=P), ost[:])\
                        .then_inc(y_out, 16)
                sp.wait_ge(y_out, 16 * NB)
                sp.wait_ge(yp_out, 16 * NB)

            @block.gpsimd
            def _(pool):
                n = [0]

                def chain(ins):
                    n[0] += 1
                    ins.then_inc(cstep, 1)
                    pool.wait_ge(cstep, n[0])

                for t in (wa, pwb, rkc):
                    chain(nc.gpsimd.memset(t[:], 0.0))
                pool.sem_inc(cst, 1)
                for t in (ar, abr, akr, S):
                    chain(nc.gpsimd.memset(t[:], 0.0))

                def keep(f, base, pattern, mult):
                    chain(nc.gpsimd.affine_select(out=f, in_=f, compare_op=ALU.is_ge, fill=0.0, base=base,
                                                  pattern=pattern, channel_multiplier=mult))

                for s, base in ((0, -1), (1, 0)):
                    chain(nc.gpsimd.memset(mf[:], 1.0))
                    keep(mf[:], base, [[1, C]], -1)
                    for j in range(2):
                        chain(nc.gpsimd.tensor_copy(mA[:, j, s, :], mf[:]))
                for n0, dst in [(2 << l, mN[:, l, :]) for l in range(5)] + [(-1, mX1[:, 0, :]), (-1, mX1[:, 1, :])] + \
                        [(-32, mT[:, 0, :]), (-64, mT[:, 1, :])]:
                    nn = abs(n0)
                    nb = C // (2 * nn)
                    f = mf[:].rearrange("p (b x) -> p b x", x=2 * nn)
                    chain(nc.gpsimd.memset(mf[:], 0.0))
                    chain(nc.gpsimd.memset(f[:, :, 0:nn] if n0 > 0 else f[:, :, nn:2 * nn], 1.0))
                    lo = nn if n0 > 0 else 0
                    keep(f, -lo, [[-2 * nn, nb], [0, 2 * nn]], 1)
                    keep(f, lo + nn - 1, [[2 * nn, nb], [0, 2 * nn]], -1)
                    chain(nc.gpsimd.tensor_copy(dst, mf[:]))
                chain(nc.gpsimd.iota(it16[:], pattern=[[1, 16]], base=1, channel_multiplier=0,
                                     allow_small_or_imprecise_dtypes=True))
                pool.sem_inc(cst, 1)
                pool.wait_ge(rc_set, 1)
                pool.wait_ge(par, 16 * (npar - 1))
                with pool.Fori(0, NB) as i:
                    k = [0]

                    def go(ins):
                        k[0] += 1
                        ins.then_inc(pstep.sem, 1)
                        pool.wait_ge(pstep.sem, pstep.past(i, k[0]))

                    pool.wait_ge(p_in, (i + 1) * 16)
                    E = BT + 16
                    tt = nc.gpsimd.tensor_tensor
                    go(tt(s2[:, :, 1:E], pin[:, :, 1:E], pin[:, :, 0:E - 1], ALU.add))
                    go(tt(s4[64:P, 0, 3:E], s2[64:P, 0, 3:E], s2[64:P, 0, 1:E - 2], ALU.add))
                    go(tt(s4[:, 1, 3:E], s2[:, 1, 3:E], s2[:, 1, 1:E - 2], ALU.add))
                    go(tt(s2[:, 1, 7:E], s4[:, 1, 7:E], s4[:, 1, 3:E - 4], ALU.add))
                    go(tt(s4[64:P, 1, 15:E], s2[64:P, 1, 15:E], s2[64:P, 1, 7:E - 8], ALU.add))
                    pool.wait_ge(pp_mm.sem, pp_mm.past(i, 0))
                    for g, sN in enumerate((s2, s4, s2, s4)):
                        hs = slice((g % 2) * 64, (g % 2) * 64 + 64)
                        go(tt(pooled[hs, g // 2, :], sN[hs, g // 2, 16:E], rc[hs, g // 2, :], ALU.mult))
                    tt(pooled[:], pooled[:], pin[:, :, 16:E], ALU.subtract).then_inc(pool_d.sem, 1)
                    for g, wn in enumerate(WINDOWS):
                        hs = slice((g % 2) * 64, (g % 2) * 64 + 64)
                        pool.sem_inc(m.passed, 1)
                        go(nc.gpsimd.memset(rc[hs, g // 2, 0:16], 1.0 / wn))
                    pool.wait_ge(gn_rec.sem, gn_rec.past(i, 1))
                    pool.wait_ge(v_d.sem, v_d.past(i, CB))
                    o3 = ost[:].rearrange("p c (h v) -> p (c h) v", v=HD)
                    v3 = vall[:].rearrange("p c (h v) -> p (c h) v", v=HD)
                    go(tt(o3, o3, st[:, 3, :].unsqueeze(2).to_broadcast([P, CB * H, HD]), ALU.mult))
                    go(tt(v3, v3, bon[:].rearrange("p c h -> p (c h)").unsqueeze(2).to_broadcast([P, CB * H, HD]), ALU.mult))
                    go(tt(ost[:], ost[:], lng[:].unsqueeze(1).to_broadcast([P, CB, 2 * P]), ALU.mult))
                    go(tt(ost[:], ost[:], lnb[:].unsqueeze(1).to_broadcast([P, CB, 2 * P]), ALU.add))
                    tt(ost[:], ost[:], vall[:], ALU.add).then_inc(y_d.sem, 1)
                    assert k[0] == NPO, k[0]

            @block.scalar
            def _(act):
                activate = nc.scalar.activation
                act.wait_ge(par, 16 * (npar - 1))
                with act.Fori(0, NB) as i:
                    act.wait_ge(shifted.sem, shifted.past(i, 1))
                    activate(zf[0:RANK, 6, :], zf[0:RANK, 6, :], ACT.Tanh).then_inc(tanh_d.sem, 1)
                    act.wait_ge(wa_mm.sem, wa_mm.past(i, 1))
                    for j in range(2):
                        activate(sw[:, j, :], bank[j][:], ACT.Sigmoid, bias=vec[:, 0, j:j + 1])
                    for j in range(2):
                        g = activate(av[:, j, :], bank[2 + j][:], ACT.Sigmoid, bias=vec[:, 1, j:j + 1])
                    g.then_inc(gates_d.sem, 1)
                    act.wait_ge(kk_mm.sem, kk_mm.past(i, 1))
                    for j in range(2):
                        g = activate(ksq[:, j, :], bank[6 + j][:], ACT.Sqrt, scale=float(HD))
                    g.then_inc(kstd_d.sem, 1)
                    act.wait_ge(lc_d.sem, lc_d.past(i, 1))
                    activate(ec[:], lc[:], ACT.Exp, scale=-DECAY)
                    activate(ei[:], lc[:], ACT.Exp, scale=DECAY).then_inc(exp_d.sem, 1)
                    act.wait_ge(ops_d.sem, ops_d.past(i, 1))
                    for j, src in enumerate((at, rt)):
                        for h in range(2):
                            hs = slice(h * 64, h * 64 + 64)
                            for k in range(2):
                                g = activate(ar[hs, k, :, h, j, :], src[hs, k, :].rearrange("p (c t) -> p c t", t=C), ACT.Copy)
                    g.then_inc(bd_d.sem, 1)
                    act.wait_ge(y_d.sem, y_d.past(i, 0))
                    act.wait_ge(y_out, i * 16)
                    for c0 in range(0, CB, 2):
                        for c in (c0, c0 + 1):
                            p = c % 2
                            act.wait_ge(tr_mm.sem, tr_mm.past(i, c + 1))
                            activate(bkt[:, p, :, :].rearrange("p k t -> p (k t)"), bank[4 + 2 * p][:], ACT.Copy)
                            activate(vt[:, p, :, :].rearrange("p k t -> p (k t)"), bank[5 + 2 * p][:, 0:2 * P], ACT.Copy)\
                                .then_inc(tok_d.sem, 1)
                            act.wait_ge(tok_d.sem, tok_d.past(i, c + 1))
                            activate(vall[:, c, :], vt[:, p, :, :].rearrange("p k t -> p (k t)"), ACT.Copy).then_inc(v_d.sem, 1)
                        for l in range(NL):
                            for c in (c0, c0 + 1):
                                p = c % 2
                                act.wait_ge(t_mm.sem, t_mm.past(i, level(c, l)))
                                activate(T[:, p, :, :].rearrange("p h t -> p (h t)"), bank[4 + 2 * p][:], ACT.Copy)\
                                    .then_inc(t_d.sem, 1)
                        for c in (c0, c0 + 1):
                            act.wait_ge(r_mm.sem, r_mm.past(i, c + 1))
                            activate(r1[:], bank[0][:, 0:2 * P], ACT.Copy).then_inc(r_d.sem, 1)
                            act.wait_ge(o_mm.sem, o_mm.past(i, c + 1))
                            activate(ost[:, c, :], bank[3][:, 0:2 * P], ACT.Copy)
                            activate(bon[:, c, :], bank[3][:, 2 * P:2 * P + H], ACT.Copy).then_inc(o_d.sem, 1)
                    act.wait_ge(gn_var.sem, gn_var.past(i, 1))
                    activate(st[:, 2, :], st[:, 1, :], ACT.Sqrt, bias=m.eps[:, 1:2], scale=1.0 / HD).then_inc(gn_std.sem, 1)

            @block.tensor
            def _(pe):
                mm = nc.tensor.matmul
                pe.wait_ge(cst, 2)
                pe.wait_ge(par, 16 * (npar - 1))
                with pe.Fori(0, NB) as i:
                    pe.wait_ge(tanh_d.sem, tanh_d.past(i, 1))
                    pe.wait_ge(o_d.sem, o_d.past(i, 0))
                    pe.wait_ge(s_d.sem, s_d.past(i, 0))
                    for j in range(2):
                        for k in range(2):
                            g = mm(bank[2 * j + k][:], wa[:, j, k, :], zf[:, 6, :], start=True, stop=True)
                    g.then_inc(wa_mm.sem, 1)
                    pe.wait_ge(ksq_d.sem, ksq_d.past(i, 1))
                    pe.wait_ge(pp_d.sem, pp_d.past(i, 0))
                    for k in range(2):
                        g = mm(bank[6 + k][:], m.headmean[:], ksq[:, k, :], start=True, stop=True)
                    g.then_inc(kk_mm.sem, 1)
                    pe.wait_ge(ops_d.sem, ops_d.past(i, 1))
                    pe.wait_ge(bd_d.sem, bd_d.past(i, 1))
                    for c0 in range(0, CB, 2):
                        for c in (c0, c0 + 1):
                            p, t0 = c % 2, c * C
                            if c0:
                                pe.wait_ge(x_d.sem, x_d.past(i, inverse(c - 2, NL - 1)))
                            for j, src in enumerate((bt, kt)):
                                for k in range(2):
                                    nc.tensor.transpose(bank[4 + 2 * p][:, (2 * j + k) * P:(2 * j + k + 1) * P],
                                                        src[:, k, t0:t0 + C], m.ident[:])
                            for k in range(2):
                                g = nc.tensor.transpose(bank[5 + 2 * p][:, k * P:(k + 1) * P], zf[:, 4 + k, t0:t0 + C], m.ident[:])
                            g.then_inc(tr_mm.sem, 1)
                        for c in (c0, c0 + 1):
                            t0 = c * C
                            if c == c0:
                                pe.wait_ge(gates_d.sem, gates_d.past(i, 1))
                                pe.wait_ge(o_d.sem, o_d.past(i, c))
                                pe.wait_ge(s_d.sem, s_d.past(i, c))
                            else:
                                pe.wait_ge(a_d.sem, a_d.past(i, c))
                            for j, src in enumerate((bt, kt)):
                                for k in range(2):
                                    g = mm(bank[2 * j + k][:], src[:, k, t0:t0 + C],
                                           ar[:, k, c, :, :, :].rearrange("p h j t -> p (h j t)"), start=True, stop=True)
                            g.then_inc(a_mm.sem, 1)
                        for l in range(NL):
                            for c in (c0, c0 + 1):
                                p = c % 2
                                pe.wait_ge(x_d.sem, x_d.past(i, inverse(c, l - 1)))
                                if l == 0:
                                    pe.wait_ge(tok_d.sem, tok_d.past(i, c + 1))
                                for h in range(H):
                                    g = mm(bank[4 + 2 * p][:, h * C:(h + 1) * C], abr[:, p, h, 0, :], X[:, p, h, :],
                                           start=True, stop=True)
                                g.then_inc(t_mm.sem, 1)
                            for c in (c0, c0 + 1):
                                p = c % 2
                                pe.wait_ge(t_d.sem, t_d.past(i, level(c, l)))
                                for h in range(H):
                                    if l < NL - 1:
                                        g = mm(bank[5 + 2 * p][:, h * C:(h + 1) * C], XT[:, p, h, :], T[:, p, h, :],
                                               start=True, stop=True)
                                    if l >= NL - 2:
                                        tb = bank[4 + 2 * p] if l == NL - 2 else bank[5 + 2 * p]
                                        g = mm(tb[:, h * C:(h + 1) * C], T[:, p, h, :], XT[:, p, h, :], start=True, stop=True)
                                g.then_inc(d_mm.sem, 1)
                        for c in (c0, c0 + 1):
                            p, t0 = c % 2, c * C
                            pe.wait_ge(z_d.sem, z_d.past(i, c + 1))
                            pe.wait_ge(a_d.sem, a_d.past(i, c0 + 2))
                            for k in range(2):
                                mm(bank[0][:, k * P:(k + 1) * P], at[:, k, t0:t0 + C], Zc[:, k, :], start=(k == 0), stop=False,
                                   skip_group_check=True)
                                for h in (2 * k, 2 * k + 1):
                                    g = mm(bank[0][:, h * HD:(h + 1) * HD], akr[:, p, h, 0, :],
                                           vt[:, p, k, (h % 2) * HD:(h % 2 + 1) * HD], start=False, stop=(h == H - 1),
                                           skip_group_check=True)
                            g.then_inc(r_mm.sem, 1)
                            pe.wait_ge(r_d.sem, r_d.past(i, c + 1))
                            pe.wait_ge(x_d.sem, x_d.past(i, inverse(c, NL - 1)))
                            for h in range(H):
                                g = mm(bank[1][:, h * HD:(h + 1) * HD], XT[:, p, h, :], r1[:, h * HD:(h + 1) * HD],
                                       start=True, stop=True)
                            g.then_inc(u_mm.sem, 1)
                            pe.wait_ge(u_d.sem, u_d.past(i, c + 1))
                            for k in range(2):
                                mm(bank[2][:, k * P:(k + 1) * P], bkt[:, p, k, :], U[:, k * P:(k + 1) * P], start=True, stop=False)
                                g = mm(bank[2][:, k * P:(k + 1) * P], bkt[:, p, 2 + k, :], vt[:, p, k, :], start=False, stop=True)
                            g.then_inc(s_mm.sem, 1)
                            pe.wait_ge(o_d.sem, o_d.past(i, c))
                            for k in range(2):
                                mm(bank[3][:, 2 * P:2 * P + H], rk[:, k, t0:t0 + C], rkc[:, k, :], start=(k == 0), stop=False,
                                   skip_group_check=True)
                            for k in range(2):
                                mm(bank[3][:, k * P:(k + 1) * P], rt[:, k, t0:t0 + C], Zc[:, k, :], start=False, stop=False,
                                   skip_group_check=True)
                                for h in (2 * k, 2 * k + 1):
                                    o = bank[3][:, h * HD:(h + 1) * HD]
                                    mm(o, abr[:, p, h, 1, :], U[:, h * HD:(h + 1) * HD], start=False, stop=False, skip_group_check=True)
                                    g = mm(o, akr[:, p, h, 1, :], vt[:, p, k, (h % 2) * HD:(h % 2 + 1) * HD], start=False,
                                           stop=(h == H - 1), skip_group_check=True)
                            g.then_inc(o_mm.sem, 1)
                    pe.wait_ge(pool_d.sem, pool_d.past(i, 1))
                    for c in range(CB):
                        for k in range(2):
                            g = mm(bank[6 + c // 2][:, (c % 2) * 2 * P + k * P:(c % 2) * 2 * P + (k + 1) * P],
                                   pooled[:, k, c * C:(c + 1) * C], pwb[:, k, :], start=True, stop=True)
                    g.then_inc(pp_mm.sem, 1)

            @block.vector
            def _(dve):
                tt, stt, ts = nc.vector.tensor_tensor, nc.vector.scalar_tensor_tensor, nc.vector.tensor_scalar
                n = [0]

                def chain(ins):
                    n[0] += 1
                    ins.then_inc(dset, 1)
                    dve.wait_ge(dset, n[0])

                chain(nc.vector.memset(onesf[:], 1.0))
                chain(nc.vector.memset(ls[:], 0.0))
                dve.wait_ge(par, 16 * (npar - 1))
                dve.wait_ge(cst, 2)
                chain(ts(vec[:, 4, :], vec[:, 3, :], -1.0, 1.0, ALU.mult, ALU.add))
                for g, wn in enumerate(WINDOWS):
                    hs = slice((g % 2) * 64, (g % 2) * 64 + 64)
                    chain(nc.vector.memset(rc[hs, g // 2, :], 1.0 / wn))
                    chain(ts(rc[hs, g // 2, 0:16], it16[hs, :], float(wn), None, ALU.min))
                    chain(nc.vector.reciprocal(rc[hs, g // 2, 0:16], rc[hs, g // 2, 0:16]))
                dve.sem_inc(rc_set, 1)
                with dve.Fori(0, NB) as i:
                    k = [0]

                    def go(ins):
                        k[0] += 1
                        ins.then_inc(dstep.sem, 1)
                        dve.wait_ge(dstep.sem, dstep.past(i, k[0]))

                    dve.wait_ge(z_in, (i + 1) * 16)
                    go(tt(zf[:], zin[:, :, 0:BT], zin[:, :, 1:BT + 1], ALU.subtract))
                    for j in range(NR):
                        g = stt(zf[:, j, :], zf[:, j, :], mu[:, j:j + 1], zin[:, j, 1:BT + 1], ALU.mult, ALU.add)
                    g.then_inc(shifted.sem, 1)
                    dve.wait_ge(shifted.sem, shifted.past(i, 1))
                    for j in range(2):
                        g = ts(kk[:, j, :], zf[:, 2 + j, :], vec[:, 2, j:j + 1], None, ALU.mult)
                    go(g)
                    tt(ksq[:], kk[:], kk[:], ALU.mult).then_inc(ksq_d.sem, 1)
                    dve.wait_ge(gates_d.sem, gates_d.past(i, 1))
                    for x in range(2 * CB):
                        g = nc.vector.tensor_tensor_scan(ls[:, x, 1:C + 1], onesf[:], chunked(sw)[:, x, :], 0.0, ALU.mult, ALU.add)
                    go(g)
                    tt(lc[:], ls[:], ls[:, :, C // 2:C // 2 + 1].to_broadcast([P, 2 * CB, C + 1]), ALU.subtract).then_inc(lc_d.sem, 1)
                    dve.wait_ge(kstd_d.sem, kstd_d.past(i, 1))
                    go(ts(ksq[:], ksq[:], 1e-12, None, ALU.max))
                    go(nc.vector.reciprocal(ksq[:], ksq[:]))
                    go(tt(kk[:], kk[:], ksq[:], ALU.mult))
                    for j in range(2):
                        g = ts(ksq[:, j, :], av[:, j, :], vec[:, 3, j:j + 1], vec[:, 4, j:j + 1], ALU.mult, ALU.add)
                    go(g)
                    go(tt(zf[:, 2:4, :], zf[:, 2:4, :], ksq[:], ALU.mult))
                    tt(rk[:], zf[:, 0:2, :], zf[:, 2:4, :], ALU.mult)
                    go(tt(av[:], kk[:], av[:], ALU.mult))
                    dve.wait_ge(exp_d.sem, exp_d.past(i, 1))
                    stt(chunked(at), chunked(kk), -1.0, ec[:, :, 0:C], ALU.mult, ALU.mult)
                    tt(chunked(bt), chunked(av), ei[:, :, 1:C + 1], ALU.mult)
                    tt(chunked(kt), zf[:, 2:4, :].rearrange("p k (c t) -> p (k c) t", t=C), ei[:, :, 1:C + 1], ALU.mult)
                    tt(chunked(rt), zf[:, 0:2, :].rearrange("p k (c t) -> p (k c) t", t=C), ec[:, :, 1:C + 1], ALU.mult)\
                        .then_inc(ops_d.sem, 1)

                    def enter(c):
                        for k2 in range(2):
                            x = k2 * CB + c
                            g = ts(Zc[:, k2, :], S[:, k2, :], ei[:, x, 0:1], None, ALU.mult)
                        go(g)
                        for k2 in range(2):
                            x = k2 * CB + c
                            g = ts(Zs[:, k2, :], Zc[:, k2, :], ec[:, x, C:C + 1], None, ALU.mult)
                        g.then_inc(z_d.sem, 1)

                    dve.wait_ge(s_d.sem, s_d.past(i, 0))
                    enter(0)
                    for c0 in range(0, CB, 2):
                        for c in (c0, c0 + 1):
                            p = c % 2
                            dve.wait_ge(a_mm.sem, a_mm.past(i, c + 1))
                            dve.sem_inc(m.passed, 1)
                            for j, dst in enumerate((abr, akr)):
                                for k2 in range(2):
                                    g = nc.vector.copy_predicated(
                                        dst[:, p, 2 * k2:2 * k2 + 2, :, :].rearrange("p h j t -> p (h j t)"),
                                        mA[:].rearrange("p h j t -> p (h j t)"), bank[2 * j + k2][:])
                            g.then_inc(a_d.sem, 1)
                            dve.wait_ge(a_d.sem, a_d.past(i, c + 1))
                            go(nc.vector.tensor_copy(XT[:, p, :, :], m.ident[:].unsqueeze(1).to_broadcast([P, H, C])))
                            dve.sem_inc(m.passed, 1)
                            go(nc.vector.copy_predicated(XT[:, p, :, :], heads4(mX1[:, 0, :]), abr[:, p, :, 0, :]))
                            nc.vector.transpose(X[:, p, :, :], XT[:, p, :, :]).then_inc(x_d.sem, 1)
                        for l in range(NL):
                            for c in (c0, c0 + 1):
                                p = c % 2
                                dve.wait_ge(d_mm.sem, d_mm.past(i, level(c, l)))
                                dve.sem_inc(m.passed, 1)
                                D = bank[5 + 2 * p][:].rearrange("p (h t) -> p h t", t=C)
                                if l < NL - 2:
                                    go(nc.vector.copy_predicated(X[:, p, :, :], heads4(mN[:, l, :]), D))
                                    nc.vector.transpose(XT[:, p, :, :], X[:, p, :, :]).then_inc(x_d.sem, 1)
                                elif l == NL - 2:
                                    nc.vector.copy_predicated(X[:, p, :, :], heads4(mN[:, l, :]), D)
                                    DT = bank[4 + 2 * p][:].rearrange("p (h t) -> p h t", t=C)
                                    nc.vector.copy_predicated(XT[:, p, :, :], heads4(mT[:, 0, :]), DT).then_inc(x_d.sem, 1)
                                else:
                                    nc.vector.copy_predicated(XT[:, p, :, :], heads4(mT[:, 1, :]), D).then_inc(x_d.sem, 1)
                        for c in (c0, c0 + 1):
                            dve.wait_ge(u_mm.sem, u_mm.past(i, c + 1))
                            nc.vector.tensor_copy(U[:], bank[1][:, 0:2 * P]).then_inc(u_d.sem, 1)
                            dve.wait_ge(s_mm.sem, s_mm.past(i, c + 1))
                            dve.wait_ge(z_d.sem, z_d.past(i, c + 1))
                            for k2 in range(2):
                                for h in range(2):
                                    hs = slice(h * 64, h * 64 + 64)
                                    x = k2 * CB + c
                                    g = stt(S[hs, k2, hs], bank[2][hs, k2 * P + h * 64:k2 * P + h * 64 + 64],
                                            ec[hs, x, C:C + 1], Zs[hs, k2, hs], ALU.mult, ALU.add)
                            g.then_inc(s_d.sem, 1)
                            if c < CB - 1:
                                dve.wait_ge(s_d.sem, s_d.past(i, c + 1))
                                dve.wait_ge(o_mm.sem, o_mm.past(i, c + 1))
                                enter(c + 1)
                    dve.wait_ge(o_d.sem, o_d.past(i, CB))
                    o3 = ost[:].rearrange("p c (h v) -> p (c h) v", v=HD)
                    q3 = osq[:].rearrange("p c (h v) -> p (c h) v", v=HD)
                    go(nc.vector.tensor_reduce(st[:, 0, :], o3, AX.X, ALU.add))
                    go(ts(st[:, 0, :], st[:, 0, :], 1.0 / HD, None, ALU.mult))
                    go(tt(o3, o3, st[:, 0, :].unsqueeze(2).to_broadcast([P, CB * H, HD]), ALU.subtract))
                    go(tt(osq[:], ost[:], ost[:], ALU.mult))
                    nc.vector.tensor_reduce(st[:, 1, :], q3, AX.X, ALU.add).then_inc(gn_var.sem, 1)
                    dve.wait_ge(pp_mm.sem, pp_mm.past(i, 1))
                    dve.wait_ge(yp_out, i * 16)
                    for j in range(2):
                        g = tt(yp[:, 2 * j:2 * j + 2, :], bank[6 + j][:].rearrange("p (c f) -> p c f", c=2),
                               psc[:].unsqueeze(1).to_broadcast([P, 2, 2 * P]), ALU.mult)
                    g.then_inc(pp_d.sem, 1)
                    dve.wait_ge(gn_std.sem, gn_std.past(i, 1))
                    nc.vector.reciprocal(st[:, 3, :], st[:, 2, :]).then_inc(gn_rec.sem, 1)
                    assert k[0] == NDV, k[0]


def attend(nc, a, m):
    with ExitStack() as ctx:
        sb, ps, sem, count = scope(nc, ctx, "attend")
        H, CB = FOX_HEADS, BT // P
        VW = 1 + 2 * HD
        MROW = HD
        NEG = -1e30

        qa = sb("qa", [P, 2, SEQ], F16)
        ka = sb("ka", [P, 2, SEQ], F16)
        qb = sb("qb", [P, 2, SEQ], F16)
        kb = sb("kb", [P, 2, SEQ], F16)
        v = sb("v", [P, 2, NT, VW + 1], F16)
        ncum = sb("ncum", [P, 2, SEQ])
        cumh = sb("cumh", [P, 2, NT])
        offh = sb("offh", [P, 2, NT])
        nb = sb("nb", [P, 2, NB, NT])
        p32 = sb("p32", [P, 4, BT])
        plo = sb("plo", [P, 4, BT], F16)
        junk = sb("junk", [P, 3, BT])
        mx = sb("mx", [P, 2, CB, NB])
        mm_ = sb("mm_", [P, 4, CB])
        mw = sb("mw", [P, CB, P], F16)
        id16 = sb("id16", [P, P], F16)
        idb = sb("idb", [P, P], BF16)
        mq = sb("mq", [P, P], BF16)
        mk = sb("mk", [P, P], BF16)
        oev = sb("oev", [P, 2, 2, VW])
        rl = sb("rl", [P, CB])
        osb = sb("osb", [P, 2, CB, HD])
        pm = [ps(f"pm{j}") for j in range(3)]
        pw = ps("pmw", (P, 4 * P), F16)
        psc = [ps(f"psc{j}") for j in range(2)]
        po = [ps(f"po{j}") for j in range(2)]

        def schedule(b):
            nq, nm = 4 * (b + 1), 4 * ((b + 1) % NB + 1)
            lag = 3
            lead = max(1, nq - 5)
            done = 0
            for x in range(nq + lag):
                if x < nq:
                    yield "qk", x
                want = nm if x >= lead - 1 else (x + 1) * nm // lead
                while done < want:
                    yield "mx", done
                    done += 1
                if x == min(lead, nq - 1):
                    yield "row", 0
                if x >= lag:
                    yield "pv", x - lag

        STEPS = [(u, b) for u in range(2) for b in range(NB)]
        NQK = 2 * sum(4 * (b + 1) for b in range(NB))
        FIRST = 4
        assert NQK % 12 == 0
        TURNS = H // 2

        width = [BT - max(0, j - 4 * b) * P for u, b in STEPS for j in range(4 * (b + 1))]
        start = {}
        for s, (u, b) in enumerate(STEPS):
            start[s] = sum(4 * (bb + 1) for uu, bb in STEPS[:s])

        def by_pool(n):
            return n % 4 == 3

        k_in = [sem(f"k_in{j}") for j in range(2)]
        q_in = [sem(f"q_in{j}") for j in range(2)]
        v_in = [sem(f"v_in{j}") for j in range(2)]
        c_in = [sem(f"c_in{j}") for j in range(2)]
        mx_mm, mx_d = count("mx_mm", NQK), count("mx_d", NQK, 3)
        row_mm, row_d, rows_w = count("row_mm", 16), count("row_d", 16), count("rows_w", 16)
        qk_mm, exp_d = count("qk_mm", NQK), count("exp_d", NQK, 2)
        lo_v, lo_p = count("lo_v", NQK * 3 // 4), count("lo_p", NQK // 4)
        pv_mm = count("pv_mm", NQK, 4)
        o_ev, o_ready = count("o_ev", 16, 1), count("o_ready", 16)
        out_d = [sem(f"fox_out{j}") for j in range(2)]
        made, cstep = sem("a_made"), sem("a_cstep")
        NDV = 16 * 9 + 2 * 2
        dstep = count("a_dstep", NDV)

        with nc.Block() as block:
            @block.sync
            def _(sp):
                def load_k(slot, head):
                    r = bass.ds(head * HD, HD)
                    for half in range(2):
                        sp.dma_start(qa[half * HD:(half + 1) * HD, slot, :], m.QK[0, half, r, :]).then_inc(q_in[slot], 16)
                        sp.dma_start(ka[half * HD:(half + 1) * HD, slot, :], m.QK[1, 0, r, :]).then_inc(k_in[slot], 16)
                    sp.dma_start(ncum[:, slot, :], m.NC[bass.ds(head, 1), :].partition_broadcast(P)).then_inc(c_in[slot], 16)
                    sp.dma_start(qb[0:HD, slot, :], m.QK[0, 0, r, :]).then_inc(q_in[slot], 16)
                    sp.dma_start(kb[0:HD, slot, :], m.QK[1, 1, r, :]).then_inc(k_in[slot], 16)
                    for half in range(2):
                        sp.dma_start(v[:, slot, :, 1 + half * HD:1 + (half + 1) * HD],
                                     m.V[:, half, r].rearrange("(t p) d -> p t d", p=P)).then_inc(v_in[slot], 16)

                sp.wait_ge(made, 1)
                load_k(0, 0)
                with sp.Fori(0, TURNS) as i:
                    for u in range(2):
                        sp.wait_ge(pv_mm.sem, pv_mm.past(i, u * (NQK // 2)))
                        sp.sem_inc(m.passed, 1)
                        sp.wait_ge(qk_mm.sem, qk_mm.past(i, u * (NQK // 2)))
                        sp.sem_inc(m.passed, 1)
                        load_k(1 - u, (i * 2 + (u + 1)) % H)
                        for b in range(NB):
                            s = u * NB + b
                            sp.wait_ge(o_ready.sem, o_ready.past(i, s + 1))
                            sp.sem_inc(m.passed, 1)
                            sp.dma_start(m.Y[b * BT:(b + 1) * BT, bass.ds((i * 2 + u) * HD, HD)]
                                         .rearrange("(c p) d -> p c d", p=P), osb[:, s % 2, :, :]).then_inc(out_d[s % 2], 16)
                for j in range(2):
                    sp.wait_ge(out_d[j], 16 * 8 * TURNS)
                sp.wait_ge(v_in[0], 32 * (TURNS + 1))
                sp.wait_ge(q_in[0], 48 * (TURNS + 1))
                sp.wait_ge(k_in[0], 48 * (TURNS + 1))
                sp.wait_ge(c_in[0], 16 * (TURNS + 1))

            @block.gpsimd
            def _(pool):
                n = [0]

                def chain(ins):
                    n[0] += 1
                    ins.then_inc(cstep, 1)
                    pool.wait_ge(cstep, n[0])

                chain(nc.gpsimd.memset(v[:, :, :, 0:1], 1.0))
                chain(nc.gpsimd.memset(kb[HD:P, :, :], 0.0))
                chain(nc.gpsimd.memset(qb[HD:P, :, :], 0.0))
                pool.sem_inc(made, 1)
                chain(nc.gpsimd.memset(mw[:], 0.0))
                for t in (id16, idb):
                    chain(nc.gpsimd.memset(t[:], 0.0))
                    chain(nc.gpsimd.affine_select(out=t[:], in_=t[:], compare_op=ALU.not_equal, fill=1.0,
                                                  base=0, pattern=[[-1, P]], channel_multiplier=1))
                for t, sign in ((mq, 1), (mk, -1)):
                    chain(nc.gpsimd.memset(t[:], 0.0))
                    chain(nc.gpsimd.affine_select(out=t[:], in_=t[:], compare_op=ALU.is_ge, fill=NEG,
                                                  base=0, pattern=[[-sign, P]], channel_multiplier=sign))
                for row, f in ((0, TOP), (1, 32.0), (2, 1.0 / 32)):
                    for s in range(2):
                        chain(nc.gpsimd.affine_select(out=kb[HD:P, s, :], in_=kb[HD:P, s, :], compare_op=ALU.not_equal, fill=f,
                                                      base=-row, pattern=[[0, SEQ]], channel_multiplier=1))
                pool.sem_inc(made, 1)
                with pool.Fori(0, TURNS) as i:
                    for x in range(NQK // 4):
                        k = 4 * x + 3
                        pool.wait_ge(exp_d.sem, exp_d.past(i, k + 1))
                        pool.wait_ge(pv_mm.sem, pv_mm.past(i, k + 1 - 4))
                        hi = p32[:, 3, :].bitcast(BF16).rearrange("p (t two) -> p t two", two=2)[:, :, 1]
                        w = width[k]
                        nc.gpsimd.tensor_tensor(plo[:, 3, 0:w], p32[:, 3, 0:w], hi[:, 0:w], ALU.subtract)\
                            .then_inc(lo_p.sem, 1)

            @block.scalar
            def _(act):
                act.sem_inc(exp_d.sem, exp_d.credit)
                act.sem_inc(o_ev.sem, o_ev.credit)
                with act.Fori(0, TURNS) as i:
                    for s, (u, b) in enumerate(STEPS):
                        for kind, x in schedule(b):
                            k = start[s] + x
                            if kind == "qk":
                                act.wait_ge(qk_mm.sem, qk_mm.past(i, k + 1))
                                act.wait_ge(pv_mm.sem, pv_mm.past(i, k + 1 - 4))
                                w = width[k]
                                nc.scalar.activation(p32[:, k % 4, 0:w], psc[k % 2][:, 0:w], ACT.Exp,
                                                     bias=nb[:, u, b, x:x + 1], scale=m.sc[:, 0:1]).then_inc(exp_d.sem, 1)
                        act.wait_ge(pv_mm.sem, pv_mm.past(i, start[s] + 4 * (b + 1)))
                        act.wait_ge(o_ready.sem, o_ready.past(i, s))
                        for j in range(2):
                            g = nc.scalar.activation(oev[:, j, :, :].rearrange("p c d -> p (c d)"), po[j][:, 0:2 * VW], ACT.Copy)
                        g.then_inc(o_ev.sem, 1)

            @block.tensor
            def _(pe):
                pe.sem_inc(pv_mm.sem, pv_mm.credit)
                pe.wait_ge(made, 2)

                def by_query(i, n, u, b, x, g):
                    t, q = x // (b + 1), x % (b + 1)
                    j = 4 * b + t
                    w = min(BT, (j + 1) * P - q * BT)
                    pe.wait_ge(mx_d.sem, n(mx_d, x + 1 - 3))
                    last = q == b
                    if last:
                        nc.tensor.matmul(pm[g][:, w - P:w], idb[:], mq[:], start=True, stop=False, skip_group_check=True)
                    nc.tensor.matmul(pm[g][:, 0:w], qa[:, u, j * P:(j + 1) * P], ka[:, u, q * BT:q * BT + w],
                                     start=not last, stop=True, skip_group_check=last).then_inc(mx_mm.sem, 1)

                def turn_row(i, val):
                    pe.wait_ge(row_d.sem, val(row_d, 1))
                    for t in range(CB):
                        g = nc.tensor.transpose(pw[:, t * P:(t + 1) * P], mw[:, t, :], id16[:])
                    g.then_inc(row_mm.sem, 1)

                pe.wait_ge(q_in[0], 48)
                pe.wait_ge(k_in[0], 48)
                for x in range(FIRST):
                    by_query(0, lambda c, k: c.credit + k, 0, 0, x, x % 3)
                turn_row(0, lambda c, k: c.credit + k)
                with pe.Fori(0, TURNS) as i:
                    done = 0
                    for s, (u, b) in enumerate(STEPS):
                        un, bn = STEPS[(s + 1) % 16]
                        if b == 0:
                            pe.wait_ge(v_in[u], (i + 1) * 32)
                        if b == NB - 1:
                            nth = i + 1 if u == 0 else i + 2
                            pe.wait_ge(q_in[1 - u], nth * 48)
                            pe.wait_ge(k_in[1 - u], nth * 48)
                        for kind, x in schedule(b):
                            k = start[s] + x
                            if kind == "qk":
                                if x == 0:
                                    pe.wait_ge(rows_w.sem, i * 16 + (s + 1))
                                d = max(0, x - 4 * b)
                                w = width[k]
                                t0 = b * BT + d * P
                                pe.wait_ge(exp_d.sem, exp_d.past(i, k + 1 - 2))
                                ks = slice(x * P, (x + 1) * P)
                                diag = x >= 4 * b
                                if diag:
                                    nc.tensor.matmul(psc[k % 2][:, 0:P], idb[:], mk[:], start=True, stop=False,
                                                     skip_group_check=True)
                                nc.tensor.matmul(psc[k % 2][:, 0:w], ka[:, u, ks], qa[:, u, t0:t0 + w], start=not diag,
                                                 stop=False, skip_group_check=diag)
                                nc.tensor.matmul(psc[k % 2][:, 0:w], kb[:, u, ks], qb[:, u, t0:t0 + w], start=False,
                                                 stop=True, skip_group_check=diag).then_inc(qk_mm.sem, 1)
                            elif kind == "mx":
                                by_query(i, lambda c, r, base=done: c.past(i, 0) + (base + FIRST + r), un, bn, x, (done + FIRST + x) % 3)
                            elif kind == "row":
                                turn_row(i, lambda c, r: c.past(i, 0) + (s + 1 + r))
                            else:
                                if x == 0:
                                    pe.wait_ge(o_ev.sem, o_ev.past(i, s))
                                if by_pool(k):
                                    pe.wait_ge(lo_p.sem, lo_p.past(i, k // 4 + 1))
                                else:
                                    pe.wait_ge(lo_v.sem, lo_v.past(i, k - k // 4 + 1))
                                d = max(0, x - 4 * b)
                                hi = p32[:, k % 4, :].bitcast(BF16).rearrange("p (t two) -> p t two", two=2)[:, :, 1]
                                for t in range(d, CB):
                                    c0 = (t - d) * P
                                    o = po[t // 2]
                                    oc = (t % 2) * VW
                                    nc.tensor.matmul(o[:, oc:oc + VW], hi[:, c0:c0 + P], v[:, u, x, 0:VW],
                                                     start=(x == 0 and t % 2 == 0), stop=False, skip_group_check=True)
                                    g = nc.tensor.matmul(o[:, oc:oc + 1 + HD], plo[:, k % 4, c0:c0 + P], v[:, u, x, 0:1 + HD],
                                                         start=False, stop=(x == 4 * b + t), skip_group_check=True)
                                g.then_inc(pv_mm.sem, 1)
                        done += 4 * (bn + 1)

            @block.vector
            def _(dve):
                tt, stt, ts = nc.vector.tensor_tensor, nc.vector.scalar_tensor_tensor, nc.vector.tensor_scalar
                dve.sem_inc(mx_d.sem, mx_d.credit)
                c1 = [0]

                def chain(ins):
                    c1[0] += 1
                    ins.then_inc(first, 1)
                    dve.wait_ge(first, c1[0])

                first = m.first

                def head_vectors(go, slot, head, sig):
                    c, o = m.cum[:].rearrange("p h t -> p (h t)"), m.off[:].rearrange("p h t -> p (h t)")
                    nc.vector.tensor_copy(cumh[:, slot, :], c[:, bass.ds(head * NT, NT)])
                    go(nc.vector.tensor_copy(offh[:, slot, :], o[:, bass.ds(head * NT, NT)]))
                    for b in range(NB):
                        g = ts(nb[:, slot, b, :], cumh[:, slot, :], -1.0, offh[:, slot, 4 * b:4 * b + 1], ALU.mult, ALU.add)
                    sig(g)

                def maximum(val, u, b, x, g, side):
                    t, q = x // (b + 1), x % (b + 1)
                    w = min(BT, (4 * b + t + 1) * P - q * BT)
                    dve.wait_ge(mx_mm.sem, val)
                    dve.sem_inc(m.passed, 1)
                    nc.vector.tensor_tensor_reduce(out=junk[:, g, 0:w], in0=pm[g][:, 0:w], in1=ncum[:, u, q * BT:q * BT + w],
                                                   scale=1.0, scalar=-3e38, op0=ALU.add, op1=ALU.max,
                                                   accum_out=mx[:, side, t, q:q + 1]).then_inc(mx_d.sem, 1)

                def parts(go, u, b, side, mxval, rowval, qval):
                    dve.wait_ge(mx_d.sem, mxval)
                    go(nc.vector.tensor_reduce(mm_[:, 0, :], mx[:, side, :, 0:b + 1], AX.X, ALU.max))
                    go(stt(mm_[:, 1, :], offh[:, u, 4 * b:4 * b + 1].to_broadcast([P, CB]), m.sc[:, 1:2], mm_[:, 0, :],
                           ALU.mult, ALU.add))
                    go(ts(mm_[:, 1, :], mm_[:, 1, :], -1.0, None, ALU.mult))
                    go(ts(mw[:, :, MROW], mm_[:, 1, :], 1.0 / TOP, None, ALU.mult))
                    go(stt(mm_[:, 2, :], mw[:, :, MROW], -TOP, mm_[:, 1, :], ALU.mult, ALU.add))
                    go(ts(mw[:, :, MROW + 1], mm_[:, 2, :], 1.0 / 32, None, ALU.mult))
                    go(stt(mm_[:, 3, :], mw[:, :, MROW + 1], -32.0, mm_[:, 2, :], ALU.mult, ALU.add))
                    ts(mw[:, :, MROW + 2], mm_[:, 3, :], 32.0, None, ALU.mult).then_inc(row_d.sem, 1)
                    dve.wait_ge(row_mm.sem, rowval)
                    nc.vector.tensor_copy(qb[MROW:P, u, b * BT:(b + 1) * BT], pw[MROW:P, :]).then_inc(rows_w.sem, 1)

                dve.wait_ge(made, 2)
                dve.wait_ge(c_in[0], 16)
                head_vectors(chain, 0, 0, chain)
                for x in range(FIRST):
                    maximum(x + 1, 0, 0, x, x % 3, 0)
                parts(chain, 0, 0, 0, mx_d.credit + FIRST, 1, None)
                with dve.Fori(0, TURNS) as i:
                    n = [0]

                    def go(ins):
                        n[0] += 1
                        ins.then_inc(dstep.sem, 1)
                        dve.wait_ge(dstep.sem, dstep.past(i, n[0]))

                    done = 0
                    for s, (u, b) in enumerate(STEPS):
                        un, bn = STEPS[(s + 1) % 16]
                        if b == NB - 1:
                            nth = i + 1 if u == 0 else i + 2
                            dve.wait_ge(c_in[1 - u], nth * 16)
                            head_vectors(go, 1 - u, (i * 2 + (u + 1)) % H, go)
                        for kind, x in schedule(b):
                            k = start[s] + x
                            if kind == "qk":
                                if not by_pool(k):
                                    w = width[k]
                                    dve.wait_ge(exp_d.sem, exp_d.past(i, k + 1))
                                    dve.wait_ge(pv_mm.sem, pv_mm.past(i, k + 1 - 4))
                                    hi = p32[:, k % 4, :].bitcast(BF16).rearrange("p (t two) -> p t two", two=2)[:, :, 1]
                                    tt(plo[:, k % 4, 0:w], p32[:, k % 4, 0:w], hi[:, 0:w], ALU.subtract).then_inc(lo_v.sem, 1)
                            elif kind == "mx":
                                maximum(i * NQK + (FIRST + done + x + 1), un, bn, x, (done + FIRST + x) % 3, (s + 1) % 2)
                            elif kind == "row":
                                parts(go, un, bn, (s + 1) % 2, mx_d.past(i, FIRST + done + 4 * (bn + 1)),
                                      i * 16 + (s + 2), None)
                        done += 4 * (bn + 1)
                        dve.wait_ge(o_ev.sem, o_ev.past(i, s + 1))
                        o4 = oev[:].rearrange("p a c d -> p (a c) d")
                        go(nc.vector.reciprocal(rl[:], o4[:, :, 0]))
                        if s >= 2:
                            dve.wait_ge(out_d[s % 2], i * 128 + 16 * (s // 2))
                        else:
                            dve.wait_ge(out_d[s % 2], i * 128)
                        go(tt(osb[:, s % 2, :, :], o4[:, :, 1:1 + HD], o4[:, :, 1 + HD:VW], ALU.add))
                        stt(osb[:, s % 2, :, :], osb[:, s % 2, :, :], m.sc[:, 4:5], rl[:].unsqueeze(2).to_broadcast([P, CB, HD]),
                            ALU.mult, ALU.mult).then_inc(o_ready.sem, 1)
                    assert n[0] == NDV, n[0]


def output(nc, a, m):
    with ExitStack() as ctx:
        sb, ps, sem, count = scope(nc, ctx, "output")
        HALF = 512
        wo32 = sb("wo32", [P, KT, DM])
        woh, wol = sb("woh", [P, KT, DM], F16), sb("wol", [P, KT, DM], F16)
        wmax = sb("wmax", [P, 4])
        gp = sb("gp", [P, DM])
        UN = 4
        y, g, x = (sb(n, [P, UN, DM]) for n in ("y", "g", "xr"))
        sqy, sqz = sb("sqy", [P, DM]), sb("sqz", [P, HALF])
        yst = sb("yst", [P, UN, 4])
        zst = sb("zst", [P, 2, 6])
        yh, yl = sb("yh", [P, 2, 2, HALF], F16), sb("yl", [P, 2, 2, HALF], F16)
        o = sb("o", [P, 2, DM])
        ptr = [ps(f"optr{j}") for j in range(2)]
        pz = [[ps(f"pz{s}{j}") for j in range(2)] for s in range(2)]

        w_in, gp_in, w_max, w_all, w_hi, w_lo, ostep = (sem("o_" + n) for n in (
            "w_in", "gp_in", "w_max", "w_all", "w_hi", "w_lo", "step"))
        yg_in = [sem(f"yg_in{s}") for s in range(UN)]
        xr_in = [sem(f"xr_in{s}") for s in range(UN)]
        gated, sq_d, norm_d, inv_d, scaled = (count("o_" + n, 1) for n in ("gated", "sq_d", "norm_d", "inv_d", "scaled"))
        tr_mm, hi_d, lo_d = count("o_tr_mm", 2, 2), count("o_hi_d", 2), count("o_lo_d", 2)
        z_mm = count("z_mm", 2 * UN)
        zs_d, z_sq, z_sum, z_std, z_fac = (count(n, UN) for n in ("zs_d", "z_sq", "z_sum", "z_std", "z_fac"))
        o_d, sum_d = count("o_o_d", UN, 2), count("sum_d", UN)
        z_fst, zf_d, rn_d = count("z_first", UN), count("zf_d", UN), count("rn_d", 1)
        sent = [sem(f"out_sent{s}") for s in range(2)]
        TURNS = NT // UN

        with nc.Block() as block:
            @block.sync
            def _(sp):
                sp.dma_start(wo32[:], a.w_out[0].rearrange("(k p) n -> p k n", p=P)).then_inc(w_in, 16)
                sp.dma_start(gp[:], a.norm_post[0:1, :].partition_broadcast(P)).then_inc(gp_in, 16)

                def load(seq, tile, s):
                    sp.wait_ge(tr_mm.sem, tr_mm.past(seq, 2 - 2 * UN))
                    sp.sem_inc(m.passed, 1)
                    r = bass.ds(tile * P, P)
                    sp.dma_start(y[:, s, :], m.Y[r, :]).then_inc(yg_in[s], 16)
                    sp.dma_start(g[:, s, :], m.G[r, :]).then_inc(yg_in[s], 16)

                def load_x(tile, s):
                    sp.dma_start(x[:, s, :], a.x[0, bass.ds(tile * P, P), :]).then_inc(xr_in[s], 16)

                for t in range(UN - 1):
                    r = slice(t * P, (t + 1) * P)
                    sp.dma_start(y[:, t, :], m.Y[r, :]).then_inc(yg_in[t], 16)
                    sp.dma_start(g[:, t, :], m.G[r, :]).then_inc(yg_in[t], 16)
                    if t < 2:
                        load_x(t, t)
                with sp.Fori(0, TURNS) as i:
                    for u in range(UN):
                        load(i * UN + (u + 3), (i * UN + (u + 3)) % NT, (u + 3) % UN)
                        load_x((i * UN + (u + 2)) % NT, (u + 2) % UN)
                        sp.wait_ge(sum_d.sem, sum_d.past(i, u + 1))
                        sp.sem_inc(m.passed, 1)
                        sp.dma_start(m.out[0, bass.ds((i * UN + u) * P, P), :], o[:, u % 2, :]).then_inc(sent[u % 2], 16)
                for s in range(2):
                    sp.wait_ge(sent[s], 16 * (NT // 2))
                for s in range(UN - 1):
                    sp.wait_ge(yg_in[s], 32 * (TURNS + 1))
                for s in range(2):
                    sp.wait_ge(xr_in[s], 16 * (TURNS + 1))

            @block.gpsimd
            def _(pool):
                pool.wait_ge(w_max, 1)
                nc.gpsimd.partition_all_reduce(wmax[:, 1:2], wmax[:, 0:1], P, RMAX).then_inc(w_all, 1)
                with pool.Fori(0, TURNS) as i:
                    for u in range(UN):
                        pool.wait_ge(o_d.sem, o_d.past(i, u + 1))
                        pool.wait_ge(xr_in[u], (i + 1) * 16)
                        nc.gpsimd.tensor_tensor(o[:, u % 2, :], o[:, u % 2, :], x[:, u, :], ALU.add).then_inc(sum_d.sem, 1)

            @block.scalar
            def _(act):
                act.wait_ge(w_max, 2)
                for k in range(KT):
                    ins = nc.scalar.activation(woh[:, k, :], wo32[:, k, :], ACT.Copy, scale=wmax[:, 3:4])
                    ins.then_inc(w_hi, 1)

                def norm(seq, s):
                    act.wait_ge(gated.sem, gated.past(seq, 1))
                    nc.scalar.activation(sqy[:], y[:, s, :], ACT.Square, accum_out=yst[:, s, 0:1]).then_inc(sq_d.sem, 1)
                    act.wait_ge(sq_d.sem, sq_d.past(seq, 1))
                    nc.scalar.activation(yst[:, s, 1:2], yst[:, s, 0:1], ACT.Sqrt, bias=m.eps[:, 2:3]).then_inc(norm_d.sem, 1)

                def hi(seq, s):
                    for j in range(2):
                        act.wait_ge(tr_mm.sem, tr_mm.past(seq, j + 1))
                        nc.scalar.activation(yh[:, s % 2, j, :], ptr[j][:], ACT.Copy).then_inc(hi_d.sem, 1)

                def square_z(i, u):
                    for j in range(2):
                        act.wait_ge(z_mm.sem, z_mm.past(i, 2 * u + j + 1))
                        if j == 0:
                            act.wait_ge(zs_d.sem, zs_d.past(i, u + 1))
                        ins = nc.scalar.activation(sqz[:], pz[u % 2][j][:], ACT.Square, scale=zst[:, u % 2, 0:1],
                                                   accum_out=zst[:, u % 2, 1 + j:2 + j])
                        if j == 0:
                            ins.then_inc(z_fst.sem, 1)
                            act.wait_ge(z_fst.sem, z_fst.past(i, u + 1))
                    ins.then_inc(z_sq.sem, 1)
                    act.wait_ge(z_sum.sem, z_sum.past(i, u + 1))
                    nc.scalar.activation(zst[:, u % 2, 4:5], zst[:, u % 2, 3:4], ACT.Sqrt, bias=m.eps[:, 0:1], scale=1.0 / DM)\
                        .then_inc(z_std.sem, 1)

                norm(0, 0)
                norm(1, 1)
                hi(0, 0)
                with act.Fori(0, TURNS) as i:
                    for u in range(UN):
                        hi(i * UN + (u + 1), (u + 1) % UN)
                        norm(i * UN + (u + 2), (u + 2) % UN)
                        square_z(i, u)

            @block.tensor
            def _(pe):
                pe.sem_inc(tr_mm.sem, tr_mm.credit)

                def turn_y(seq, s):
                    pe.wait_ge(scaled.sem, scaled.past(seq, 1))
                    for j in range(2):
                        for k in range(4):
                            c = (4 * j + k) * P
                            t = nc.tensor.transpose(ptr[j][:, k * P:(k + 1) * P], y[:, s, c:c + P], m.ident[:])
                        t.then_inc(tr_mm.sem, 1)

                def product(i, u, j):
                    for k in range(KT):
                        ks = slice((k % 4) * P, (k % 4 + 1) * P)
                        for c, (l, r) in enumerate(((yh, woh), (yh, wol), (yl, woh))):
                            mm = nc.tensor.matmul(pz[u % 2][j][:], l[:, u % 2, k // 4, ks], r[:, k, j * HALF:(j + 1) * HALF],
                                                  start=(k == 0 and c == 0), stop=(k == KT - 1 and c == 2))
                    mm.then_inc(z_mm.sem, 1)

                turn_y(0, 0)
                pe.wait_ge(w_lo, KT)
                with pe.Fori(0, TURNS) as i:
                    for u in range(UN):
                        seq = i * UN + u
                        pe.wait_ge(lo_d.sem, lo_d.past(seq, 2))
                        pe.wait_ge(o_d.sem, o_d.past(i, u - 1))
                        product(i, u, 0)
                        turn_y(i * UN + (u + 1), (u + 1) % UN)
                        product(i, u, 1)

            @block.vector
            def _(dve):
                tt, stt, ts = nc.vector.tensor_tensor, nc.vector.scalar_tensor_tensor, nc.vector.tensor_scalar
                n = [0]

                def chain(ins):
                    n[0] += 1
                    ins.then_inc(ostep, 1)
                    dve.wait_ge(ostep, n[0])

                dve.sem_inc(o_d.sem, o_d.credit)
                dve.wait_ge(gp_in, 16)
                chain(tt(gp[:], gp[:], m.gate[:], ALU.mult))
                dve.wait_ge(w_in, 16)
                nc.vector.tensor_reduce(wmax[:, 0:1], wo32[:].rearrange("p k n -> p (k n)"), AX.X, ALU.max,
                                        apply_absolute_value=True).then_inc(w_max, 1)
                dve.wait_ge(w_all, 1)
                chain(ts(wmax[:, 2:3], wmax[:, 1:2], 1e-30, 1.0 / TOP, ALU.max, ALU.mult))
                nc.vector.reciprocal(wmax[:, 3:4], wmax[:, 2:3]).then_inc(w_max, 1)
                for k in range(KT):
                    dve.wait_ge(w_hi, k + 1)
                    stt(wol[:, k, :], wo32[:, k, :], wmax[:, 3:4], woh[:, k, :], ALU.mult, ALU.subtract).then_inc(w_lo, 1)

                def prepare_y(seq, s, loads):
                    dve.wait_ge(yg_in[s], loads * 32)
                    tt(y[:, s, :], y[:, s, :], g[:, s, :], ALU.mult).then_inc(gated.sem, 1)
                    dve.wait_ge(norm_d.sem, norm_d.past(seq, 1))
                    ts(yst[:, s, 3:4], yst[:, s, 1:2], 1.0 / TOP, None, ALU.mult).then_inc(inv_d.sem, 1)
                    dve.wait_ge(inv_d.sem, inv_d.past(seq, 1))
                    nc.vector.reciprocal(yst[:, s, 2:3], yst[:, s, 3:4]).then_inc(rn_d.sem, 1)
                    dve.wait_ge(rn_d.sem, rn_d.past(seq, 1))
                    ts(y[:, s, :], y[:, s, :], yst[:, s, 2:3], None, ALU.mult).then_inc(scaled.sem, 1)

                def lo(seq, s):
                    for j in range(2):
                        dve.wait_ge(hi_d.sem, hi_d.past(seq, j + 1))
                        tt(yl[:, s % 2, j, :], ptr[j][:], yh[:, s % 2, j, :], ALU.subtract).then_inc(lo_d.sem, 1)

                prepare_y(0, 0, 1)
                prepare_y(1, 1, 1)
                lo(0, 0)
                with dve.Fori(0, TURNS) as i:
                    for u in range(UN):
                        s = u % 2
                        dve.wait_ge(o_d.sem, o_d.past(i, u))
                        ts(zst[:, s, 0:1], yst[:, u, 3:4], wmax[:, 2:3], None, ALU.mult).then_inc(zs_d.sem, 1)
                        dve.wait_ge(zs_d.sem, zs_d.past(i, u + 1))
                        lo(i * UN + (u + 1), (u + 1) % UN)
                        prepare_y(i * UN + (u + 2), (u + 2) % UN, i + (u + 2) // UN + 1)
                        dve.wait_ge(z_sq.sem, z_sq.past(i, u + 1))
                        tt(zst[:, s, 3:4], zst[:, s, 1:2], zst[:, s, 2:3], ALU.add).then_inc(z_sum.sem, 1)
                        dve.wait_ge(z_std.sem, z_std.past(i, u + 1))
                        nc.vector.reciprocal(zst[:, s, 5:6], zst[:, s, 4:5]).then_inc(z_fac.sem, 1)
                        dve.wait_ge(z_fac.sem, z_fac.past(i, u + 1))
                        ts(zst[:, s, 5:6], zst[:, s, 5:6], zst[:, s, 0:1], None, ALU.mult).then_inc(zf_d.sem, 1)
                        dve.wait_ge(zf_d.sem, zf_d.past(i, u + 1))
                        dve.wait_ge(sent[s], i * 32 + 16 * (u // 2))
                        for j in range(2):
                            ins = stt(o[:, s, j * HALF:(j + 1) * HALF], pz[s][j][:], zst[:, s, 5:6],
                                      gp[:, j * HALF:(j + 1) * HALF], ALU.mult, ALU.mult)
                        ins.then_inc(o_d.sem, 1)


class Inputs:

    def __init__(self, x, c, ada_w, ada_b, norm_pre, norm_post, w_in, fox_q_gain, fox_k_gain, fox_f_bias,
                 rwkv_mu, rwkv_w0, rwkv_w2, rwkv_a0, rwkv_a2, rwkv_k_k, rwkv_k_a, rwkv_r_k, rwkv_ln_g,
                 rwkv_ln_b, pool_w, pool_scale, w_out):
        self.x = x
        self.c = c
        self.ada_w = ada_w
        self.ada_b = ada_b
        self.norm_pre = norm_pre
        self.norm_post = norm_post
        self.w_in = w_in
        self.fox_q_gain = fox_q_gain
        self.fox_k_gain = fox_k_gain
        self.fox_f_bias = fox_f_bias
        self.rwkv_mu = rwkv_mu
        self.rwkv_w0 = rwkv_w0
        self.rwkv_w2 = rwkv_w2
        self.rwkv_a0 = rwkv_a0
        self.rwkv_a2 = rwkv_a2
        self.rwkv_k_k = rwkv_k_k
        self.rwkv_k_a = rwkv_k_a
        self.rwkv_r_k = rwkv_r_k
        self.rwkv_ln_g = rwkv_ln_g
        self.rwkv_ln_b = rwkv_ln_b
        self.pool_w = pool_w
        self.pool_scale = pool_scale
        self.w_out = w_out


def hymba_layer(nc, a, out):
    with ExitStack() as ctx:
        m = persistent(nc, ctx)
        m.out = out
        m.QK = nc.dram_tensor("scratch_qk", [2, 2, FOX_W, SEQ], F16).ap()
        m.V = nc.dram_tensor("scratch_v", [SEQ, 2, FOX_W], F16).ap()
        m.Z = nc.dram_tensor("scratch_z", [ZC, m.HALO + SEQ], F32).ap()
        m.G = nc.dram_tensor("scratch_g", [SEQ, DM], F32).ap()
        m.Y = nc.dram_tensor("scratch_y", [SEQ, DM], F32).ap()
        m.NC = nc.dram_tensor("scratch_nc", [FOX_HEADS, SEQ], F32).ap()
        with ExitStack() as weights:
            m.wh = weights.enter_context(nc.sbuf_tensor("wh", [P, KT, D_IN], F16))
            m.wl = weights.enter_context(nc.sbuf_tensor("wl", [P, KT, D_IN], F16))
            prepare(nc, a, m)
            project(nc, a, m)
        decay(nc, a, m)
        recur(nc, a, m)
        attend(nc, a, m)
        output(nc, a, m)


INPUTS = ("x", "c", "ada_w", "ada_b", "norm_pre", "norm_post", "w_in", "fox_q_gain", "fox_k_gain", "fox_f_bias",
          "rwkv_mu", "rwkv_w0", "rwkv_w2", "rwkv_a0", "rwkv_a2", "rwkv_k_k", "rwkv_k_a", "rwkv_r_k", "rwkv_ln_g",
          "rwkv_ln_b", "pool_w", "pool_scale", "w_out")


def kernel(**inputs):
    import numpy as np
    import concourse.bacc as bacc
    from concourse.bass_utils import run_bass_kernel_spmd

    nc = bacc.Bacc("TRN2", target_bir_lowering=False, num_devices=1)
    arrays, aps = {}, {}
    for name in INPUTS:
        array = np.ascontiguousarray(inputs[name])
        arrays[f"in_{name}"] = array
        aps[name] = nc.dram_tensor(f"in_{name}", array.shape, mybir.dt.from_np(array.dtype), kind="ExternalInput").ap()
    out = nc.dram_tensor("out", [1, SEQ, DM], F32, kind="ExternalOutput").ap()
    hymba_layer(nc, Inputs(**aps), out)
    result = run_bass_kernel_spmd(nc, [arrays], core_ids=[0])
    return result.results[0]["out"]
```

```python
from contextlib import ExitStack

import concourse.bass as bass
from concourse import mybir

F32 = mybir.dt.float32
F16 = mybir.dt.float16
BF16 = mybir.dt.bfloat16
I32 = mybir.dt.int32
ALU = mybir.AluOpType
ACT = mybir.ActivationFunctionType
AX = mybir.AxisListType
RMAX = bass.bass_isa.ReduceOp.max

P = 128
SEQ, DM = 4096, 1024
HD = 64
FOX_HEADS, RWKV_HEADS = 8, 4
FOX_W, RWKV_W, POOL_W = 512, 256, 256
WINDOWS = (2, 4, 8, 16)
RANK = 64
D_IN = 3720
V_COL, F_COL, Z_COL, G_COL = 1024, 1536, 1544, 2696
ZC = 1152
KT = DM // P
BT = 512
NB = SEQ // BT
NT = SEQ // P
EPS = 1e-6
GN_EPS = 64e-5
DECAY = 0.6065306597126334
TOP = 32768.0


class Count:

    def __init__(self, sem, per, credit=0):
        self.sem, self.per, self.credit = sem, per, credit

    def past(self, turn, k):
        return turn * self.per + (self.credit + k)


class Layer:
    pass


def scope(nc, ctx, stage):
    sems = []

    def clear():
        nc.clear_and_free_semaphores(sems)
        nc.all_engine_barrier()

    ctx.callback(clear)

    def sb(name, shape, dt=F32):
        return ctx.enter_context(nc.sbuf_tensor(name, shape, dt))

    def ps(name, shape=(P, 512), dt=F32):
        return ctx.enter_context(nc.psum_tensor(name, list(shape), dt))

    def sem(name):
        sems.append(nc.alloc_semaphore(name=f"{stage}_{name}"))
        return sems[-1]

    def count(name, per, credit=0):
        return Count(sem(name), per, credit)

    return sb, ps, sem, count


def column(v):
    return v.rearrange("(p o) -> p o", o=1)


def prepare(nc, a, m):
    with ExitStack() as ctx:
        sb, ps, sem, count = scope(nc, ctx, "prepare")
        adaw = sb("adaw", [P, 2, 3 * DM])
        wst = sb("wst", [P, 2, D_IN])
        ccol = sb("ccol", [P, KT])
        csig = sb("csig", [P, KT])
        cbc = sb("cbc", [P, KT, P])
        onesf = sb("onesf", [P, P])
        abcol = sb("abcol", [P, 2 * KT])
        npre = sb("npre", [P, KT])
        rowmax = sb("rowmax", [P, KT])
        rinv = sb("rinv", [P, KT])
        gcol = sb("gcol", [P, KT])
        scol = sb("scol", [P, KT])
        t8 = sb("t8", [P, KT])
        bnd = sb("bnd", [P, 4])
        gains = sb("gains", [P, 2, HD])
        gm = sb("gm", [P, 4])
        pcol = ps("pcol")
        pg = [ps(f"pg{j}") for j in range(2)]

        small, halo = m.small, m.halo
        ada_in = [sem(f"p_ada_in{j}") for j in range(2)]
        w_in = [sem(f"p_w_in{j}") for j in range(2)]
        silu = sem("p_silu")
        ada_mm = sem("p_ada_mm")
        w_max = sem("p_w_max")
        w_hi = sem("p_w_hi")
        w_lo = sem("p_w_lo")
        step = sem("p_step")
        allmax = sem("p_allmax")
        const0 = sem("p_const0")
        zero = sb("zero", [P, m.HALO])
        nsmall = 10

        with nc.Block() as block:
            @block.sync
            def _(sp):
                for k in range(KT):
                    if k >= 2:
                        sp.wait_ge(ada_mm, k - 1)
                    sp.dma_start(adaw[:, k % 2, :], a.ada_w[0, k * P:(k + 1) * P, :]).then_inc(ada_in[k % 2], 16)
                    if k >= 2:
                        sp.wait_ge(w_lo, k - 1)
                    sp.dma_start(wst[:, k % 2, :], a.w_in[0, k * P:(k + 1) * P, :]).then_inc(w_in[k % 2], 16)

            @block.gpsimd
            def _(pool):
                nc.gpsimd.memset(m.ident[:], 0.0).then_inc(const0, 1)
                nc.gpsimd.memset(zero[:], 0.0).then_inc(const0, 1)
                pool.wait_ge(const0, 2)
                nc.gpsimd.affine_select(out=m.ident[:], in_=m.ident[:], compare_op=ALU.not_equal, fill=1.0,
                                        base=0, pattern=[[-1, P]], channel_multiplier=1).then_inc(const0, 1)
                pool.dma_start(ccol[:], a.c.rearrange("o (k p) -> p (o k)", p=P), allow_slow_non_contiguous=True).then_inc(small, 16)
                pool.dma_start(abcol[:], a.ada_b[0, 0:2 * DM].rearrange("(k p) -> p k", p=P), allow_slow_non_contiguous=True).then_inc(small, 16)
                pool.dma_start(npre[:], a.norm_pre[0].rearrange("(k p) -> p k", p=P), allow_slow_non_contiguous=True).then_inc(small, 16)
                pool.dma_start(m.gate[:], a.ada_b[0:1, 2 * DM:3 * DM].partition_broadcast(P)).then_inc(small, 16)
                pool.dma_start(gains[:, 0, :], a.fox_q_gain[0:1, :].partition_broadcast(P)).then_inc(small, 16)
                pool.dma_start(gains[:, 1, :], a.fox_k_gain[0:1, :].partition_broadcast(P)).then_inc(small, 16)
                for j, g in enumerate((a.fox_q_gain, a.fox_k_gain)):
                    for half in range(2):
                        pool.dma_start(m.qkgain[half * HD:(half + 1) * HD, j:j + 1],
                                       column(g[0]), allow_slow_non_contiguous=True).then_inc(small, 16)
                for k in range(ZC // P):
                    pool.dma_start(m.Z[k * P:(k + 1) * P, 0:m.HALO], zero[:]).then_inc(halo, 16)
                pool.wait_ge(w_max, KT + 1)
                nc.gpsimd.partition_all_reduce(bnd[:, 1:2], bnd[:, 0:1], P, RMAX).then_inc(allmax, 1)
                pool.wait_ge(halo, 16 * (ZC // P))

            @block.scalar
            def _(act):
                act.wait_ge(small, 16 * nsmall)
                nc.scalar.activation(csig[:], ccol[:], ACT.Sigmoid).then_inc(silu, 1)
                for k in range(KT):
                    act.wait_ge(w_max, k + 1)
                    nc.scalar.activation(m.wh[:, k, :], wst[:, k % 2, :], ACT.Copy,
                                         scale=rinv[:, k:k + 1]).then_inc(w_hi, 1)

            @block.tensor
            def _(pe):
                pe.wait_ge(silu, 3)
                for k in range(KT):
                    pe.wait_ge(ada_in[k % 2], 16 * (k // 2 + 1))
                    for j in range(2 * KT):
                        nc.tensor.matmul(pcol[:, j:j + 1], adaw[:, k % 2, j * P:(j + 1) * P], ccol[:, k:k + 1],
                                         start=(k == 0 and j == 0), stop=(k == KT - 1), skip_group_check=True)
                    for j in range(2):
                        mm = nc.tensor.matmul(pg[j][:], cbc[:, k, :],
                                              adaw[:, k % 2, 2 * DM + j * 512:2 * DM + (j + 1) * 512],
                                              start=(k == 0), stop=(k == KT - 1))
                    mm.then_inc(ada_mm, 1)

            @block.vector
            def _(dve):
                n = [0]

                def chain(ins):
                    n[0] += 1
                    ins.then_inc(step, 1)
                    dve.wait_ge(step, n[0])

                chain(nc.vector.memset(onesf[:], 1.0))
                nc.vector.memset(m.eps[:, 0:1], EPS)
                nc.vector.memset(m.eps[:, 1:2], GN_EPS)
                nc.vector.memset(m.eps[:, 2:3], 1e-24)
                chain(nc.vector.memset(m.eps[:, 3:4], 1.0))
                chain(nc.vector.memset(m.headmean[:], 0.0))
                for half in range(2):
                    sl = slice(half * HD, (half + 1) * HD)
                    chain(nc.vector.memset(m.headmean[sl, sl], 1.0 / HD))
                dve.wait_ge(silu, 1)
                dve.wait_ge(small, 16 * nsmall)
                nc.vector.tensor_tensor(ccol[:], ccol[:], csig[:], ALU.mult).then_inc(silu, 1)
                dve.wait_ge(silu, 2)
                for k in range(KT):
                    last = nc.vector.tensor_scalar(cbc[:, k, :], onesf[:], ccol[:, k:k + 1], None, ALU.mult)
                last.then_inc(silu, 1)
                chain(nc.vector.tensor_reduce(gm[:, 0:2], gains[:], AX.X, ALU.max, apply_absolute_value=True))
                chain(nc.vector.tensor_scalar(gm[:, 0:2], gm[:, 0:2], 0.5, 1.0 / 32.0, ALU.max, ALU.mult))
                chain(nc.vector.reciprocal(gm[:, 2:4], gm[:, 0:2]))
                chain(nc.vector.tensor_tensor(m.qkgain[:], m.qkgain[:], gm[:, 2:4], ALU.mult))
                chain(nc.vector.scalar_tensor_tensor(m.sc[:, 0:1], gm[:, 0:1], HD ** -0.5, gm[:, 1:2],
                                                     ALU.mult, ALU.mult))
                chain(nc.vector.reciprocal(m.sc[:, 1:2], m.sc[:, 0:1]))
                for k in range(KT):
                    dve.wait_ge(w_in[k % 2], 16 * (k // 2 + 1))
                    chain(nc.vector.tensor_reduce(rowmax[:, k:k + 1], wst[:, k % 2, :], AX.X, ALU.max,
                                                  apply_absolute_value=True))
                    chain(nc.vector.tensor_scalar(rowmax[:, k:k + 1], rowmax[:, k:k + 1], 1e-20, 1.0 / TOP,
                                                  ALU.max, ALU.mult))
                    nc.vector.reciprocal(rinv[:, k:k + 1], rowmax[:, k:k + 1]).then_inc(w_max, 1)
                    dve.wait_ge(w_hi, k + 1)
                    nc.vector.scalar_tensor_tensor(m.wl[:, k, :], wst[:, k % 2, :], rinv[:, k:k + 1],
                                                   m.wh[:, k, :], ALU.mult, ALU.subtract).then_inc(w_lo, 1)
                dve.wait_ge(ada_mm, KT)
                dve.wait_ge(w_lo, KT)
                chain(nc.vector.tensor_tensor(abcol[:], pcol[:, 0:2 * KT], abcol[:], ALU.add))
                for j in range(2):
                    chain(nc.vector.tensor_tensor(m.gate[:, j * 512:(j + 1) * 512], pg[j][:],
                                                  m.gate[:, j * 512:(j + 1) * 512], ALU.add))
                chain(nc.vector.scalar_tensor_tensor(gcol[:], abcol[:, KT:2 * KT], 1.0, npre[:], ALU.add, ALU.mult))
                chain(nc.vector.tensor_tensor(gcol[:], gcol[:], rowmax[:], ALU.mult))
                chain(nc.vector.tensor_tensor(scol[:], abcol[:, 0:KT], rowmax[:], ALU.mult))
                chain(nc.vector.tensor_reduce(bnd[:, 2:3], gcol[:], AX.X, ALU.max, apply_absolute_value=True))
                chain(nc.vector.tensor_reduce(bnd[:, 3:4], scol[:], AX.X, ALU.max, apply_absolute_value=True))
                nc.vector.tensor_tensor(bnd[:, 0:1], bnd[:, 2:3], bnd[:, 3:4], ALU.add).then_inc(w_max, 1)
                dve.wait_ge(allmax, 1)
                chain(nc.vector.tensor_scalar(m.sc[:, 2:3], bnd[:, 1:2], 1e-30, 32.0 / TOP, ALU.max, ALU.mult))
                chain(nc.vector.reciprocal(m.sc[:, 3:4], m.sc[:, 2:3]))
                chain(nc.vector.tensor_scalar(m.sc[:, 4:5], m.sc[:, 2:3], 2.0 ** 20, None, ALU.mult))
                chain(nc.vector.tensor_scalar(m.gcol[:], gcol[:], m.sc[:, 3:4], None, ALU.mult))
                chain(nc.vector.tensor_scalar(m.scol[:], scol[:], m.sc[:, 3:4], None, ALU.mult))


def project(nc, a, m):
    with ExitStack() as ctx:
        sb, ps, sem, count = scope(nc, ctx, "project")
        jobs = [("qk", n) for n in range(8)] + [("z", n) for n in range(ZC // P)] + \
            [("v", t) for t in range(4)] + [("g", (t, j)) for t in range(4) for j in range(2)]
        NJ = len(jobs)
        assert NJ % 2 == 1
        T_JOB = 11
        TURNS = NB // 2
        NQK = 16

        xt = sb("xt", [P, 4, DM])
        sqx = sb("sqx", [P, DM])
        ssq = sb("ssq", [P, 4])
        rstd = sb("rstd", [P, 4])
        rstd2 = sb("rstd2", [P, 4])
        h32 = sb("h32", [P, 2, BT])
        hh = sb("hh", [P, 2, KT, BT], F16)
        hl = sb("hl", [P, 2, KT, BT], F16)
        uq = sb("uq", [P, 2, BT])
        sq = sb("sq", [P, 2, BT])
        stdb = sb("stdb", [P, BT])
        rec = sb("rec", [P, BT])
        qn = sb("qn", [P, BT])
        sig = sb("sig", [P, BT])
        stage = [sb(f"stage{j}", [P, BT]) for j in range(2)]
        stage16 = [s[:, :].bitcast(F16).rearrange("p (two t) -> p two t", two=2) for s in stage]
        fbc = sb("fbc", [P, 4, FOX_HEADS])
        ptr = [ps(f"ptr{j}") for j in range(2)]
        pmm = [ps(f"pmm{j}") for j in range(2)]
        pss = ps("pss")
        pf = ps("pf")

        x_in = [sem(f"x_in{j}") for j in range(4)]
        sq_done, std_done = count("sq_done", 4), count("std_done", 1)
        rstd_done, xn_done = count("rstd_done", 1), count("xn_done", 4, 4)
        tr_done = count("tr_done", KT, KT)
        h32_done, hi_done, lo_done = count("h32_done", KT, 1), count("hi_done", KT), count("lo_done", KT, 1)
        f_mm, f_out = count("f_mm", 1), count("f_out", 1, 1)
        mm_done = count("mm_done", 2 * NJ)
        qk_sq, qk_ss, qk_std = count("qk_sq", NQK), count("qk_ss", NQK, 1), count("qk_std", NQK)
        qk_rec, qk_n, qk_hi, qk_u = count("qk_rec", NQK), count("qk_n", NQK, 1), count("qk_hi", NQK), count("qk_u", NQK)
        v_hi, sig_done = count("v_hi", 8), count("sig_done", 16)
        ready = [count(f"stage_ready{j}", NJ) for j in range(2)]
        sent = [count(f"stage_sent{j}", 16 * NJ) for j in range(2)]
        fb_in = sem("fb_in")
        passed, pool_passed = sem("passed"), sem("pool_passed")

        def slot(u, n):
            return (u * NJ + n) % 2, (u * NJ + n) // 2

        def wait_filled(eng, i, u, n):
            s, used = slot(u, n)
            eng.wait_ge(ready[s].sem, ready[s].past(i, used + 1))

        with nc.Block() as block:
            @block.sync
            def _(sp):
                for t in range(4):
                    sp.dma_start(fbc[:, t, :], a.fox_f_bias[0:1, :].partition_broadcast(P)).then_inc(fb_in, 16)

                def load_x(seq, blk):
                    sp.wait_ge(tr_done.sem, tr_done.past(seq, 0))
                    sp.sem_inc(passed, 1)
                    for j in range(4):
                        sp.dma_start(xt[:, j, :], a.x[0, bass.ds(blk * BT + j * P, P), :]).then_inc(x_in[j], 16)

                def store(i, u, n):
                    kind, w = jobs[n]
                    s, used = slot(u, n)
                    t0 = (i * 2 + u) * BT
                    if kind == "qk":
                        c0 = (w % 4) * P
                        dst = m.QK[w // 4, :, c0:c0 + P, bass.ds(t0, BT)].rearrange("two c t -> c two t")
                        src = stage16[s]
                    elif kind == "z":
                        dst, src = m.Z[w * P:(w + 1) * P, bass.ds(t0 + m.HALO, BT)], stage[s][:]
                    elif kind == "v":
                        dst, src = m.V[bass.ds(t0 + w * P, P), :, :], stage16[s]
                    else:
                        dst, src = m.G[bass.ds(t0 + w[0] * P, P), w[1] * 512:(w[1] + 1) * 512], stage[s][:]
                    sp.wait_ge(ready[s].sem, ready[s].past(i, used + 1))
                    sp.sem_inc(passed, 1)
                    sp.dma_start(dst, src).then_inc(sent[s].sem, 16)

                load_x(0, 0)
                with sp.Fori(0, TURNS) as i:
                    for u in range(2):
                        load_x(i * 2 + (u + 1), (i * 2 + (u + 1)) % NB)
                        for n in range(NJ):
                            store(i, u, n)
                for s in range(2):
                    sp.wait_ge(sent[s].sem, 16 * TURNS * NJ)

            @block.tensor
            def _(pe):
                pe.sem_inc(tr_done.sem, tr_done.credit)
                pe.sem_inc(qk_ss.sem, qk_ss.credit)

                def turn_x(seq, k):
                    if k == 0:
                        pe.wait_ge(xn_done.sem, xn_done.past(seq, 4))
                    pe.wait_ge(h32_done.sem, h32_done.past(seq, k - 1))
                    for j in range(4):
                        t = nc.tensor.transpose(ptr[k % 2][:, j * P:(j + 1) * P], xt[:, j, k * P:(k + 1) * P], m.ident[:])
                    t.then_inc(tr_done.sem, 1)

                def products(out, lhs, rhs):
                    for k in range(KT):
                        for c, (l, r) in enumerate(((0, 0), (0, 1), (1, 0))):
                            mm = nc.tensor.matmul(out, lhs(l, k), rhs(r, k), start=(k == 0 and c == 0),
                                                  stop=(k == KT - 1 and c == 2))
                    return mm

                h, w = (hh, hl), (m.wh, m.wl)

                def job(i, u, n):
                    kind, x = jobs[n]
                    s, used = slot(u, n)
                    if 2 <= n < 10:
                        pe.wait_ge(qk_u.sem, qk_u.past(i, u * 8 + n - 1))
                    else:
                        wait_filled(pe, i, u, n - 2)
                    if kind in ("qk", "z"):
                        c0 = x * P if kind == "qk" else Z_COL + x * P
                        products(pmm[s][:], lambda l, k: w[l][:, k, c0:c0 + P],
                                 lambda r, k: h[r][:, u, k, :]).then_inc(mm_done.sem, 1)
                    else:
                        t, c0 = (x, V_COL) if kind == "v" else (x[0], G_COL + x[1] * 512)
                        products(pmm[s][:], lambda l, k: h[l][:, u, k, t * P:(t + 1) * P],
                                 lambda r, k: w[r][:, k, c0:c0 + 512]).then_inc(mm_done.sem, 1)

                def head_means(i, u, x):
                    pe.wait_ge(qk_sq.sem, qk_sq.past(i, u * 8 + x + 1))
                    pe.wait_ge(qk_std.sem, qk_std.past(i, u * 8 + x))
                    nc.tensor.matmul(pss[:], m.headmean[:], sq[:, x % 2, :], start=True, stop=True).then_inc(qk_ss.sem, 1)

                for k in range(KT):
                    turn_x(0, k)
                with pe.Fori(0, TURNS) as i:
                    for u in range(2):
                        blk = i * 2 + u
                        pe.wait_ge(hi_done.sem, hi_done.past(blk, KT))
                        pe.wait_ge(lo_done.sem, lo_done.past(blk, KT))
                        pe.wait_ge(f_out.sem, f_out.past(blk, 0))
                        for t in range(4):
                            mm = products(pf[:, t * 8:(t + 1) * 8], lambda l, k: h[l][:, u, k, t * P:(t + 1) * P],
                                          lambda r, k: w[r][:, k, F_COL:F_COL + FOX_HEADS])
                        mm.then_inc(f_mm.sem, 1)
                        for n in range(NJ):
                            job(i, u, n)
                            if 1 <= n <= 8:
                                head_means(i, u, n - 1)
                            if T_JOB <= n < T_JOB + KT:
                                turn_x(i * 2 + (u + 1), n - T_JOB)

            @block.scalar
            def _(act):
                act.sem_inc(h32_done.sem, h32_done.credit)

                def x_squares(seq, j):
                    act.wait_ge(x_in[j], (seq + 1) * 16)
                    nc.scalar.activation(sqx[:], xt[:, j, :], ACT.Square, accum_out=ssq[:, j:j + 1]).then_inc(sq_done.sem, 1)
                    act.wait_ge(sq_done.sem, sq_done.past(seq, j + 1))

                def x_std(seq):
                    act.wait_ge(xn_done.sem, xn_done.past(seq, 0))
                    nc.scalar.activation(rstd[:], ssq[:], ACT.Sqrt, bias=m.eps[:, 0:1], scale=1.0 / DM)\
                        .then_inc(std_done.sem, 1)
                    act.wait_ge(std_done.sem, std_done.past(seq, 1))

                def h_hi(seq, side, k):
                    act.wait_ge(tr_done.sem, tr_done.past(seq, k + 1))
                    act.wait_ge(lo_done.sem, lo_done.past(seq, k - 1))
                    nc.scalar.activation(h32[:, k % 2, :], ptr[k % 2][:], ACT.Identity, bias=m.scol[:, k:k + 1],
                                         scale=m.gcol[:, k:k + 1]).then_inc(h32_done.sem, 1)
                    act.wait_ge(h32_done.sem, h32_done.past(seq, k + 1))
                    nc.scalar.activation(hh[:, side, k, :], h32[:, k % 2, :], ACT.Copy).then_inc(hi_done.sem, 1)

                def evacuate(i, u, n):
                    kind, x = jobs[n]
                    s, used = slot(u, n)
                    act.wait_ge(mm_done.sem, mm_done.past(i, u * NJ + n + 1))
                    if kind == "qk":
                        act.wait_ge(qk_ss.sem, qk_ss.past(i, u * 8 + x - 1))
                        nc.scalar.activation(sq[:, x % 2, :], pmm[s][:], ACT.Square, scale=m.sc[:, 2:3])\
                            .then_inc(qk_sq.sem, 1)
                        act.wait_ge(qk_n.sem, qk_n.past(i, u * 8 + x - 1))
                        nc.scalar.activation(uq[:, x % 2, :], pmm[s][:], ACT.Copy, scale=m.sc[:, 2:3])\
                            .then_inc(qk_u.sem, 1)
                    elif kind == "z":
                        act.wait_ge(sent[s].sem, sent[s].past(i, 16 * used))
                        nc.scalar.activation(stage[s][:], pmm[s][:], ACT.Copy, scale=m.sc[:, 2:3])\
                            .then_inc(ready[s].sem, 1)
                    elif kind == "v":
                        act.wait_ge(sent[s].sem, sent[s].past(i, 16 * used))
                        nc.scalar.activation(stage16[s][:, 0, :], pmm[s][:], ACT.Copy, scale=2.0 ** -20)\
                            .then_inc(v_hi.sem, 1)
                    else:
                        wait_filled(act, i, u, n - 1 if n > NJ - 8 else -1)
                        nc.scalar.activation(sig[:], pmm[s][:], ACT.Sigmoid, scale=m.sc[:, 2:3])\
                            .then_inc(sig_done.sem, 1)

                def head_std(i, u, x):
                    act.wait_ge(qk_ss.sem, qk_ss.past(i, u * 8 + x + 1))
                    act.wait_ge(qk_rec.sem, qk_rec.past(i, u * 8 + x))
                    nc.scalar.activation(stdb[:], pss[:], ACT.Sqrt, bias=m.eps[:, 0:1]).then_inc(qk_std.sem, 1)

                for j in range(4):
                    x_squares(0, j)
                x_std(0)
                for k in range(KT):
                    h_hi(0, 0, k)
                with act.Fori(0, TURNS) as i:
                    for u in range(2):
                        seq = i * 2 + (u + 1)
                        for n in range(NJ):
                            evacuate(i, u, n)
                            if 1 <= n <= 8:
                                head_std(i, u, n - 1)
                            if 2 <= n <= 5:
                                x_squares(seq, n - 2)
                            if n == 6:
                                x_std(seq)
                            if T_JOB <= n < T_JOB + KT:
                                h_hi(seq, 1 - u, n - T_JOB)

            @block.vector
            def _(dve):
                dve.sem_inc(xn_done.sem, xn_done.credit)
                dve.sem_inc(lo_done.sem, lo_done.credit)
                dve.sem_inc(f_out.sem, f_out.credit)
                dve.sem_inc(qk_n.sem, qk_n.credit)

                def x_scaled(seq):
                    dve.wait_ge(std_done.sem, std_done.past(seq, 1))
                    nc.vector.reciprocal(rstd2[:], rstd[:]).then_inc(rstd_done.sem, 1)
                    dve.wait_ge(rstd_done.sem, rstd_done.past(seq, 1))
                    for j in range(4):
                        nc.vector.tensor_scalar(xt[:, j, :], xt[:, j, :], rstd2[:, j:j + 1], None, ALU.mult)\
                            .then_inc(xn_done.sem, 1)

                def h_lo(seq, side, k):
                    dve.wait_ge(hi_done.sem, hi_done.past(seq, k + 1))
                    nc.vector.tensor_tensor(hl[:, side, k, :], h32[:, k % 2, :], hh[:, side, k, :], ALU.subtract)\
                        .then_inc(lo_done.sem, 1)

                def normalise(i, u, x):
                    dve.wait_ge(qk_std.sem, qk_std.past(i, u * 8 + x + 1))
                    nc.vector.reciprocal(rec[:], stdb[:]).then_inc(qk_rec.sem, 1)
                    dve.wait_ge(qk_rec.sem, qk_rec.past(i, u * 8 + x + 1))
                    wait_filled(dve, i, u, x - 1 if x else -2)
                    nc.vector.scalar_tensor_tensor(qn[:], uq[:, x % 2, :], m.qkgain[:, x // 4:x // 4 + 1], rec[:],
                                                   ALU.mult, ALU.mult).then_inc(qk_n.sem, 1)

                def finish(i, u, n):
                    kind, x = jobs[n]
                    s, used = slot(u, n)
                    if kind == "v":
                        dve.wait_ge(v_hi.sem, v_hi.past(i, u * 4 + x + 1))
                        nc.vector.scalar_tensor_tensor(stage16[s][:, 1, :], pmm[s][:], 2.0 ** -20, stage16[s][:, 0, :],
                                                       ALU.mult, ALU.subtract)\
                            .then_inc(ready[s].sem, 1)
                    elif kind == "g":
                        dve.wait_ge(sig_done.sem, sig_done.past(i, u * 8 + n - (NJ - 8) + 1))
                        dve.wait_ge(sent[s].sem, sent[s].past(i, 16 * used))
                        nc.vector.scalar_tensor_tensor(stage[s][:], pmm[s][:], m.sc[:, 2:3], sig[:], ALU.mult, ALU.mult)\
                            .then_inc(ready[s].sem, 1)

                x_scaled(0)
                for k in range(KT):
                    h_lo(0, 0, k)
                dve.wait_ge(fb_in, 64)
                with dve.Fori(0, TURNS) as i:
                    for u in range(2):
                        seq = i * 2 + (u + 1)
                        blk = i * 2 + u
                        dve.wait_ge(f_mm.sem, f_mm.past(blk, 1))
                        nc.vector.scalar_tensor_tensor(
                            m.fl[:, bass.ds(blk * (4 * FOX_HEADS), 4 * FOX_HEADS)], pf[:, 0:32],
                            m.sc[:, 2:3], fbc[:].rearrange("p t h -> p (t h)"), ALU.mult, ALU.add).then_inc(f_out.sem, 1)
                        for n in range(NJ):
                            finish(i, u, n)
                            if 1 <= n <= 8:
                                normalise(i, u, n - 1)
                            if n == 9:
                                x_scaled(seq)
                            if T_JOB <= n < T_JOB + KT:
                                h_lo(seq, 1 - u, n - T_JOB)

            @block.gpsimd
            def _(pool):
                with pool.Fori(0, TURNS) as i:
                    for u in range(2):
                        for x in range(8):
                            s, used = slot(u, x)
                            pool.wait_ge(qk_n.sem, qk_n.past(i, u * 8 + x + 1))
                            pool.wait_ge(sent[s].sem, sent[s].past(i, 16 * used))
                            pool.sem_inc(pool_passed, 1)
                            nc.gpsimd.tensor_copy(stage16[s][:, 0, :], qn[:]).then_inc(qk_hi.sem, 1)
                            pool.wait_ge(qk_hi.sem, qk_hi.past(i, u * 8 + x + 1))
                            nc.gpsimd.tensor_tensor(stage16[s][:, 1, :], qn[:], stage16[s][:, 0, :], ALU.subtract)\
                                .then_inc(ready[s].sem, 1)


def decay(nc, a, m):
    with ExitStack() as ctx:
        sb, ps, sem, count = scope(nc, ctx, "decay")
        NF = NT * FOX_HEADS
        tri = sb("tri", [P, P])
        ones = sb("ones", [P, P])
        ab, ex, ln = sb("ab", [P, NF]), sb("ex", [P, NF]), sb("ln", [P, NF])
        tot = sb("tot", [P, FOX_HEADS, NT])
        crow = sb("crow", [P, 2, P])
        clamp = sb("clamp", [P, 1])
        pw, pt, pc = ps("pw"), ps("pt"), ps("pc")
        made, ones_made = sem("d_made"), sem("d_ones")
        abs_done, exp_done, ln_done, log_done = (sem("d_" + n) for n in ("abs", "exp", "ln", "log"))
        sums, cum_done, turned, rows, stored, step = (sem("d_" + n) for n in ("sums", "cum", "turned", "rows", "stored", "step"))
        with nc.Block() as block:
            @block.gpsimd
            def _(pool):
                nc.gpsimd.memset(tri[:], 1.0).then_inc(made, 1)
                pool.wait_ge(made, 1)
                nc.gpsimd.affine_select(out=tri[:], in_=tri[:], compare_op=ALU.is_ge, fill=0.0, base=0,
                                        pattern=[[1, P]], channel_multiplier=-1).then_inc(made, 1)

            @block.scalar
            def _(act):
                act.wait_ge(abs_done, 1)
                nc.scalar.activation(ex[:], ab[:], ACT.Exp, scale=-1.0).then_inc(exp_done, 1)
                act.wait_ge(exp_done, 1)
                nc.scalar.activation(ln[:], ex[:], ACT.Ln, bias=m.eps[:, 3:4]).then_inc(ln_done, 1)

            @block.tensor
            def _(pe):
                pe.wait_ge(made, 2)
                pe.wait_ge(ones_made, 1)
                pe.wait_ge(log_done, 1)
                nc.tensor.matmul(pw[:, 0:NF], tri[:], m.fl[:], start=True, stop=True)
                nc.tensor.matmul(pt[:, 0:NF], ones[:], m.fl[:], start=True, stop=True).then_inc(sums, 1)
                pe.wait_ge(cum_done, 1)
                cums = m.cum[:].rearrange("p h t -> p (h t)")
                for j in range(2):
                    t = nc.tensor.transpose(pc[:, j * P:(j + 1) * P], cums[:, j * P:(j + 1) * P], m.ident[:])
                t.then_inc(turned, 1)

            @block.vector
            def _(dve):
                n = [0]

                def chain(ins):
                    n[0] += 1
                    ins.then_inc(step, 1)
                    dve.wait_ge(step, n[0])

                nc.vector.memset(ones[:], 1.0).then_inc(ones_made, 1)
                nc.vector.scalar_tensor_tensor(ab[:], m.fl[:], -1.0, m.fl[:], ALU.mult, ALU.max).then_inc(abs_done, 1)
                chain(nc.vector.tensor_scalar(clamp[:], m.sc[:, 0:1], -500.0 * 1024.0 * HD ** 0.5, None, ALU.mult))
                dve.wait_ge(ln_done, 1)
                chain(nc.vector.scalar_tensor_tensor(ab[:], m.fl[:], 0.0, ln[:], ALU.min, ALU.subtract))
                nc.vector.tensor_scalar(m.fl[:], ab[:], clamp[:, 0:1], None, ALU.max).then_inc(log_done, 1)
                dve.wait_ge(sums, 1)
                chain(nc.vector.tensor_copy(tot[:], pt[:, 0:NF].rearrange("p (t h) -> p h t", h=FOX_HEADS)))
                chain(nc.vector.memset(m.off[:], 0.0))
                for h in range(FOX_HEADS):
                    chain(nc.vector.tensor_tensor_scan(m.off[:, h, 1:NT], ones[:, 0:NT - 1], tot[:, h, 0:NT - 1], 0.0,
                                                       ALU.mult, ALU.add))
                nc.vector.tensor_tensor(m.cum[:], pw[:, 0:NF].rearrange("p (t h) -> p h t", h=FOX_HEADS), m.off[:],
                                        ALU.add).then_inc(cum_done, 1)
                dve.wait_ge(turned, 1)
                nc.vector.tensor_scalar(crow[:].rearrange("p j t -> p (j t)"), pc[:, 0:2 * P], m.sc[:, 1:2], -1.0,
                                        ALU.mult, ALU.mult).then_inc(rows, 1)

            @block.sync
            def _(sp):
                sp.wait_ge(rows, 1)
                sp.dma_start(m.NC.rearrange("h (t p) -> (h t) p", p=P).rearrange("(j q) p -> q j p", j=2), crow[:])\
                    .then_inc(stored, 16)
                sp.wait_ge(stored, 16)


def persistent(nc, ctx):
    sb, ps, sem, count = scope(nc, ctx, "layer")
    m = Layer()
    m.HALO = 16
    m.first = sem("attend_first")
    m.small, m.halo = sem("small_in"), sem("halo_out")
    m.passed = sem("passed_on")
    m.ident = sb("ident", [P, P])
    m.headmean = sb("headmean", [P, P])
    m.eps = sb("eps", [P, 4])
    m.sc = sb("sc", [P, 8])
    m.gcol = sb("gcol_s", [P, KT])
    m.scol = sb("scol_s", [P, KT])
    m.gate = sb("gate", [P, DM])
    m.qkgain = sb("qkgain", [P, 2])
    m.fl = sb("fl", [P, NT * FOX_HEADS])
    m.cum = sb("cum", [P, FOX_HEADS, NT])
    m.off = sb("off", [P, FOX_HEADS, NT])
    return m


def recur(nc, a, m):
    with ExitStack() as ctx:
        sb, ps, sem, count = scope(nc, ctx, "recur")
        C, CB = P, 2
        W = C * CB
        BLOCKS = SEQ // W
        TURNS = BLOCKS // 2
        NR = 7
        H = RWKV_HEADS
        NL = 6
        G = 2 * H

        zin = sb("zin", [P, NR, W + 1])
        zf = sb("zf", [P, NR, W])
        mu = sb("mu", [P, NR])
        vec = sb("vec", [P, 5, 2])
        wa = sb("wa", [P, 2, 2, P])
        rkc = sb("rkc", [P, 2, H])
        sw = sb("sw", [P, 2, W])
        av = sb("av", [P, 2, W])
        ls = sb("ls", [P, 2 * CB, C + 1])
        lc = sb("lc", [P, 2 * CB, C + 1])
        ec = sb("ec", [P, 2 * CB, C + 1])
        ei = sb("ei", [P, 2 * CB, C + 1])
        kk = sb("kk", [P, 2, W])
        ksq = sb("ksq", [P, 2, W])
        bt, kt = sb("bt", [P, 2, W]), sb("kt", [P, 2, W])
        ends = sb("ends", [P, 2, 2, 2 * CB])
        rk = sb("rk", [P, 2, 2, W])
        ar = sb("ar", [P, 2, 2, CB, 2, 2, C])
        abr = sb("abr", [P, 2, CB, H, 2, C])
        akr = sb("akr", [P, 2, CB, H, 2, C])
        XT = sb("XT", [P, 2, CB, H, C])
        bkt = sb("bkt", [P, 2, CB, 4, P])
        vt = sb("vt", [P, 2, CB, 2 * P])
        ost = sb("ost", [P, 2, CB, 2 * P])
        bon = sb("bon", [P, 2, CB, H])
        yp = sb("yp", [P, 2, CB, 2 * P])
        X = sb("X", [P, CB, H, C])
        T = sb("T", [P, CB, H, C])
        r1 = sb("r1", [P, 2 * P])
        U = sb("U", [P, 2 * P])
        S = sb("S", [P, 2, P])
        Zc = sb("Zc", [P, 2, 2, P])
        Zs = sb("Zs", [P, 2, P])
        osq = sb("osq", [P, CB, 2 * P])
        bv = sb("bv", [P, CB, 2 * P])
        st = sb("st", [P, 5, G])
        onesf = sb("onesr", [P, C])
        mA = sb("mA", [P, 2, 2, C], I32)
        mX1 = sb("mX1", [P, C], I32)
        mN = sb("mN", [P, 5, C], I32)
        mT = sb("mT", [P, 2, C], I32)
        mf = sb("mf", [P, C])
        lng, lnb, psc = (sb(n, [P, 2 * P]) for n in ("lng", "lnb", "psc"))
        pwb = sb("pwb", [P, 2, P])
        pin = sb("pin", [P, 2, W + m.HALO])
        s2, s4 = (sb(n, [P, 2, W + m.HALO]) for n in ("s2", "s4"))
        rc = sb("rc", [P, 2, W])
        it16 = sb("it16", [P, 16])
        pooled = sb("pooled", [P, 2, W])
        bank = [ps(f"bank{j}") for j in range(8)]

        cst, par, cstep, dset, rc_set = sem("r_cst"), sem("r_par"), sem("r_cstep"), sem("r_dset"), sem("rc_set")
        z_in, p_in, y_out, yp_out = sem("z_in"), sem("p_in"), [sem(f"y_out{s}") for s in range(2)], \
            [sem(f"yp_out{s}") for s in range(2)]
        zsub, shifted, tanh_d, wa_mm, gates_d, lc_d, exp_d, ksq_d, kk_mm, kstd_d, ops_d = (count(n, 1) for n in (
            "zsub", "shifted", "tanh_d", "wa_mm", "gates_d", "lc_d", "exp_d", "ksq_d", "kk_mm", "kstd_d", "ops_d"))
        rt_d = count("rt_d", 4)
        gn_mean, gn_sq, gn_var, gn_std, gn_rec, y_d, pool_d, pp_mm, pp_d = (count(n, 1) for n in (
            "gn_mean", "gn_sq", "gn_var", "gn_std", "gn_rec", "y_d", "pool_d", "pp_mm", "pp_d"))
        tr_mm, tok_d, a_mm, a_d, r_mm, r_d, u_mm, u_d, s_mm, s_d, z_d, o_mm, o_d = (count("c_" + n, CB) for n in (
            "tr_mm", "tok_d", "a_mm", "a_d", "r_mm", "r_d", "u_mm", "u_d", "s_mm", "s_d", "z_d", "o_mm", "o_d"))
        t_mm, t_d, d_mm = count("t_mm", NL * CB), count("t_d", NL * CB), count("d_mm", NL * CB)
        x_d = count("x_d", (NL + 1) * CB)
        estep, xstep, lstep, gstep, zstep = count("estep", 8), count("xstep", 2 * CB), count("lstep", (NL - 2) * CB), \
            count("gstep", 1), count("zstep", CB)
        pstep, ystep, rc4 = count("pstep", 9), count("ystep", 5), count("rc4", 4)
        npar = 18

        def at(l, c):
            return l * CB + c + 1

        def chunked(t):
            return t[:].rearrange("p k (c t) -> p (k c) t", t=C)

        def heads(mask):
            return mask.unsqueeze(1).to_broadcast([P, H, C])

        def flat(t):
            return t.rearrange("p h t -> p (h t)")

        with nc.Block() as block:
            @block.sync
            def _(sp):
                n = [0]

                def load(dst, src):
                    n[0] += 1
                    sp.dma_start(dst, src, allow_slow_non_contiguous=True).then_inc(par, 16)

                def load_z(blk):
                    sp.dma_start(zin[:], m.Z[0:NR * P, bass.ds(blk * W + (m.HALO - 1), W + 1)]
                                 .rearrange("(k p) t -> p k t", p=P)).then_inc(z_in, 16)

                def load_p(blk):
                    sp.dma_start(pin[:], m.Z[NR * P:ZC, bass.ds(blk * W, W + m.HALO)]
                                 .rearrange("(k p) t -> p k t", p=P)).then_inc(p_in, 16)

                load_z(0)
                load_p(0)
                load(mu[:], a.rwkv_mu[0].rearrange("(k p) -> p k", p=P))
                for j, v in enumerate((a.rwkv_w0, a.rwkv_a0, a.rwkv_k_k, a.rwkv_k_a)):
                    load(vec[:, j, :], v[0].rearrange("(k p) -> p k", p=P))
                sp.wait_ge(cst, 1)
                load(wa[0:RANK, 0, :, :], a.rwkv_w2[0].rearrange("r (k c) -> r k c", c=P))
                load(wa[RANK:P, 1, :, :], a.rwkv_a2[0].rearrange("r (k c) -> r k c", c=P))
                for g in range(4):
                    hs = slice((g % 2) * 64, (g % 2) * 64 + 64)
                    load(pwb[hs, g // 2, hs], a.pool_w[0, g])
                    load(rkc[hs, g // 2, g:g + 1], column(a.rwkv_r_k[0, g]))
                load(lng[:], a.rwkv_ln_g[0:1, :].partition_broadcast(P))
                load(lnb[:], a.rwkv_ln_b[0:1, :].partition_broadcast(P))
                load(psc[:], a.pool_scale[0:1, :].partition_broadcast(P))
                assert n[0] == npar, n
                sp.wait_ge(shifted.sem, 1)
                load_z(1)

                def store(dst, cols, src, done):
                    sp.dma_start(m.Y[bass.ds(dst * W, W), cols].rearrange("(c p) f -> p c f", p=P), src).then_inc(done, 16)

                rwkv, pool = slice(FOX_W, FOX_W + RWKV_W), slice(FOX_W + RWKV_W, DM)
                with sp.Fori(0, TURNS) as i:
                    for u in range(2):
                        n = i * 2 + u
                        sp.wait_ge(shifted.sem, shifted.past(n, 2))
                        sp.sem_inc(m.passed, 1)
                        load_z((n + 2) % BLOCKS)
                        sp.wait_ge(pool_d.sem, pool_d.past(n, 1))
                        sp.sem_inc(m.passed, 1)
                        load_p((n + 1) % BLOCKS)
                        sp.wait_ge(y_d.sem, y_d.past(n, 1))
                        sp.sem_inc(m.passed, 1)
                        store((n + (BLOCKS - 1)) % BLOCKS, rwkv, ost[:, 1 - u, :, :], y_out[1 - u])
                        sp.wait_ge(pp_d.sem, pp_d.past(n, 1))
                        sp.sem_inc(m.passed, 1)
                        store(n, pool, yp[:, u, :, :], yp_out[u])
                sp.wait_ge(y_out[1], 16 * TURNS)
                sp.wait_ge(y_d.sem, y_d.past(BLOCKS, 1))
                store(BLOCKS - 1, rwkv, ost[:, 1, :, :], y_out[1])
                sp.wait_ge(y_out[0], 16 * TURNS)
                sp.wait_ge(y_out[1], 16 * (TURNS + 1))
                for s in range(2):
                    sp.wait_ge(yp_out[s], 16 * TURNS)
                sp.wait_ge(z_in, 16 * (BLOCKS + 2))
                sp.wait_ge(p_in, 16 * (BLOCKS + 1))

            @block.gpsimd
            def _(pool):
                n = [0]
                tt = nc.gpsimd.tensor_tensor

                def chain(ins):
                    n[0] += 1
                    ins.then_inc(cstep, 1)
                    pool.wait_ge(cstep, n[0])

                def difference(seq):
                    pool.wait_ge(z_in, (seq + 1) * 16)
                    tt(zf[:], zin[:, :, 0:W], zin[:, :, 1:W + 1], ALU.subtract).then_inc(zsub.sem, 1)

                def r_side(seq, s):
                    pool.wait_ge(exp_d.sem, exp_d.past(seq, 1))
                    for h in range(2):
                        hs = slice(h * 64, h * 64 + 64)
                        for k in range(2):
                            tt(ar[hs, s, k, :, h, 1, :], zf[hs, k, :].rearrange("p (c t) -> p c t", t=C),
                               ec[hs, k * CB:(k + 1) * CB, 1:C + 1], ALU.mult).then_inc(rt_d.sem, 1)
                            pool.wait_ge(rt_d.sem, rt_d.past(seq, 2 * h + k + 1))

                def group_norm(seq, s, last=False):
                    o3 = ost[:, s, :, :].rearrange("p c (h v) -> p (c h) v", v=HD)
                    v3 = vt[:, s, :, :].rearrange("p c (h v) -> p (c h) v", v=HD)
                    b3 = bv[:].rearrange("p c (h v) -> p (c h) v", v=HD)

                    def wide(x):
                        return x.unsqueeze(2).to_broadcast([P, G, HD])

                    def step(k, ins):
                        ins.then_inc(ystep.sem, 1)
                        pool.wait_ge(ystep.sem, ystep.past(seq, k))

                    pool.wait_ge(gn_mean.sem, gn_mean.past(seq, 1))
                    step(1, tt(o3, o3, wide(st[:, 1, :]), ALU.subtract))
                    tt(osq[:], ost[:, s, :, :], ost[:, s, :, :], ALU.mult).then_inc(gn_sq.sem, 1)
                    step(2, tt(b3, v3, wide(bon[:, s, :, :].rearrange("p c h -> p (c h)")), ALU.mult))
                    step(3, tt(bv[:], bv[:], lnb[:].unsqueeze(1).to_broadcast([P, CB, 2 * P]), ALU.add))
                    if not last:
                        pooling_sums()
                    pool.wait_ge(gn_rec.sem, gn_rec.past(seq, 1))
                    step(4, tt(o3, o3, wide(st[:, 4, :]), ALU.mult))
                    step(5, tt(ost[:, s, :, :], ost[:, s, :, :], lng[:].unsqueeze(1).to_broadcast([P, CB, 2 * P]), ALU.mult))
                    tt(ost[:, s, :, :], ost[:, s, :, :], bv[:], ALU.add).then_inc(y_d.sem, 1)
                    pool.wait_ge(y_d.sem, y_d.past(seq, 1))

                for t in (wa, pwb, rkc):
                    chain(nc.gpsimd.memset(t[:], 0.0))
                pool.sem_inc(cst, 1)
                difference(0)
                for t in (ar, abr, akr, S, ost, bon, vt):
                    chain(nc.gpsimd.memset(t[:], 0.0))

                def keep(f, base, pattern, mult):
                    chain(nc.gpsimd.affine_select(out=f, in_=f, compare_op=ALU.is_ge, fill=0.0, base=base,
                                                  pattern=pattern, channel_multiplier=mult))

                for s, base in ((0, -1), (1, 0)):
                    chain(nc.gpsimd.memset(mf[:], 1.0))
                    keep(mf[:], base, [[1, C]], -1)
                    for j in range(2):
                        chain(nc.gpsimd.tensor_copy(mA[:, j, s, :], mf[:]))
                for n0, dst in [(2 << l, mN[:, l, :]) for l in range(5)] + [(-1, mX1[:]), (-32, mT[:, 0, :]), (-64, mT[:, 1, :])]:
                    nn = abs(n0)
                    nb = C // (2 * nn)
                    f = mf[:].rearrange("p (b x) -> p b x", x=2 * nn)
                    chain(nc.gpsimd.memset(mf[:], 0.0))
                    chain(nc.gpsimd.memset(f[:, :, 0:nn] if n0 > 0 else f[:, :, nn:2 * nn], 1.0))
                    lo = nn if n0 > 0 else 0
                    keep(f, -lo, [[-2 * nn, nb], [0, 2 * nn]], 1)
                    keep(f, lo + nn - 1, [[2 * nn, nb], [0, 2 * nn]], -1)
                    chain(nc.gpsimd.tensor_copy(dst, mf[:]))
                chain(nc.gpsimd.iota(it16[:], pattern=[[1, 16]], base=1, channel_multiplier=0,
                                     allow_small_or_imprecise_dtypes=True))
                pool.sem_inc(cst, 1)
                pool.wait_ge(rc_set, 1)
                pool.wait_ge(par, 16 * npar)
                r_side(0, 0)
                pool.wait_ge(ops_d.sem, 1)
                pool.wait_ge(tr_mm.sem, CB)
                difference(1)
                with pool.Fori(0, TURNS) as i:
                    for u in range(2):
                        n = i * 2 + u

                        def pooling_sums():
                            def step(k, ins):
                                ins.then_inc(pstep.sem, 1)
                                pool.wait_ge(pstep.sem, pstep.past(n, k))

                            E = W + m.HALO
                            pool.wait_ge(p_in, (n + 1) * 16)
                            step(1, tt(s2[:, :, 1:E], pin[:, :, 1:E], pin[:, :, 0:E - 1], ALU.add))
                            step(2, tt(s4[64:P, 0, 3:E], s2[64:P, 0, 3:E], s2[64:P, 0, 1:E - 2], ALU.add))
                            step(3, tt(s4[:, 1, 3:E], s2[:, 1, 3:E], s2[:, 1, 1:E - 2], ALU.add))
                            step(4, tt(s2[:, 1, 7:E], s4[:, 1, 7:E], s4[:, 1, 3:E - 4], ALU.add))
                            step(5, tt(s4[64:P, 1, 15:E], s2[64:P, 1, 15:E], s2[64:P, 1, 7:E - 8], ALU.add))
                            pool.wait_ge(pp_mm.sem, pp_mm.past(n, 0))
                            for g, sN in enumerate((s2, s4, s2, s4)):
                                hs = slice((g % 2) * 64, (g % 2) * 64 + 64)
                                step(6 + g, tt(pooled[hs, g // 2, :], sN[hs, g // 2, 16:E], rc[hs, g // 2, :], ALU.mult))
                            tt(pooled[:], pooled[:], pin[:, :, 16:E], ALU.subtract).then_inc(pool_d.sem, 1)

                        group_norm(n, 1 - u)
                        if u == 0:
                            for g, wn in enumerate(WINDOWS):
                                hs = slice((g % 2) * 64, (g % 2) * 64 + 64)
                                pool.sem_inc(m.passed, 1)
                                nc.gpsimd.memset(rc[hs, g // 2, 0:16], 1.0 / wn).then_inc(rc4.sem, 1)
                                pool.wait_ge(rc4.sem, rc4.past(i, g + 1))
                        r_side(n + 1, 1 - u)
                        pool.wait_ge(ops_d.sem, ops_d.past(n, 2))
                        pool.wait_ge(tr_mm.sem, tr_mm.past(n, 2 * CB))
                        difference(n + 2)
                group_norm(BLOCKS, 1, last=True)

            @block.scalar
            def _(act):
                activate = nc.scalar.activation

                def tanh(seq):
                    act.wait_ge(shifted.sem, shifted.past(seq, 1))
                    activate(zf[0:RANK, 6, :], zf[0:RANK, 6, :], ACT.Tanh).then_inc(tanh_d.sem, 1)

                def gates(seq):
                    act.wait_ge(wa_mm.sem, wa_mm.past(seq, 1))
                    for j in range(2):
                        activate(sw[:, j, :], bank[0][:, j * W:(j + 1) * W], ACT.Sigmoid, bias=vec[:, 0, j:j + 1])
                    for j in range(2):
                        g = activate(av[:, j, :], bank[1][:, j * W:(j + 1) * W], ACT.Sigmoid, bias=vec[:, 1, j:j + 1])
                    g.then_inc(gates_d.sem, 1)

                def kk_norm(seq):
                    act.wait_ge(kk_mm.sem, kk_mm.past(seq, 1))
                    activate(ksq[:].rearrange("p k t -> p (k t)"), bank[2][:], ACT.Sqrt, scale=float(HD)).then_inc(kstd_d.sem, 1)

                def exps(seq):
                    act.wait_ge(lc_d.sem, lc_d.past(seq, 1))
                    activate(ec[:], lc[:], ACT.Exp, scale=-DECAY)
                    activate(ei[:], lc[:], ACT.Exp, scale=DECAY).then_inc(exp_d.sem, 1)

                def deviation(seq):
                    act.wait_ge(gn_var.sem, gn_var.past(seq, 1))
                    activate(st[:, 3, :], st[:, 2, :], ACT.Sqrt, bias=m.eps[:, 1:2], scale=1.0 / HD).then_inc(gn_std.sem, 1)

                def by_token(seq, s, c):
                    act.wait_ge(tr_mm.sem, tr_mm.past(seq, c + 1))
                    activate(bkt[:, s, c, :, :].rearrange("p k t -> p (k t)"), bank[4 + 2 * c][:], ACT.Copy)
                    activate(vt[:, s, c, :], bank[5 + 2 * c][:, 0:2 * P], ACT.Copy).then_inc(tok_d.sem, 1)

                def r1_out(seq, c):
                    act.wait_ge(r_mm.sem, r_mm.past(seq, c + 1))
                    activate(r1[:], bank[0][:, 0:2 * P], ACT.Copy).then_inc(r_d.sem, 1)

                def o_out(seq, s, c):
                    act.wait_ge(o_mm.sem, o_mm.past(seq, c + 1))
                    activate(ost[:, s, c, :], bank[3][:, 0:2 * P], ACT.Copy)
                    activate(bon[:, s, c, :], bank[3][:, 2 * P:2 * P + H], ACT.Copy).then_inc(o_d.sem, 1)

                act.wait_ge(par, 16 * npar)
                act.wait_ge(cst, 2)
                tanh(0)
                gates(0)
                kk_norm(0)
                exps(0)
                for c in range(CB):
                    by_token(0, 0, c)
                with act.Fori(0, TURNS) as i:
                    for u in range(2):
                        n = i * 2 + u
                        for l in range(NL):
                            for c in range(CB):
                                act.wait_ge(t_mm.sem, t_mm.past(n, at(l, c)))
                                activate(flat(T[:, c, :, :]), bank[4 + 2 * c][:], ACT.Copy).then_inc(t_d.sem, 1)
                            if l == 0:
                                tanh(n + 1)
                            elif l == 1:
                                gates(n + 1)
                            elif l == 3:
                                kk_norm(n + 1)
                                deviation(n)
                            elif l == 4:
                                exps(n + 1)
                        act.wait_ge(y_d.sem, y_d.past(n, 1))
                        if u == 0:
                            act.wait_ge(y_out[0], i * 16)
                        else:
                            act.wait_ge(y_out[1], i * 16 + 16)
                        r1_out(n, 0)
                        by_token(n + 1, 1 - u, 0)
                        by_token(n + 1, 1 - u, 1)
                        o_out(n, u, 0)
                        r1_out(n, 1)
                        o_out(n, u, 1)
                deviation(BLOCKS)

            @block.tensor
            def _(pe):
                mm = nc.tensor.matmul

                def turn(seq, c):
                    t0 = c * C
                    for j, src in enumerate((bt, kt)):
                        for k in range(2):
                            nc.tensor.transpose(bank[4 + 2 * c][:, (2 * j + k) * P:(2 * j + k + 1) * P],
                                                src[:, k, t0:t0 + C], m.ident[:])
                    for k in range(2):
                        g = nc.tensor.transpose(bank[5 + 2 * c][:, k * P:(k + 1) * P], zf[:, 4 + k, t0:t0 + C], m.ident[:])
                    g.then_inc(tr_mm.sem, 1)

                def logits(seq):
                    pe.wait_ge(tanh_d.sem, tanh_d.past(seq, 1))
                    for j in range(2):
                        for k in range(2):
                            g = mm(bank[j][:, k * W:(k + 1) * W], wa[:, j, k, :], zf[:, 6, :], start=True, stop=True)
                    g.then_inc(wa_mm.sem, 1)

                def kk_means(seq):
                    pe.wait_ge(ksq_d.sem, ksq_d.past(seq, 1))
                    mm(bank[2][:], m.headmean[:], ksq[:].rearrange("p k t -> p (k t)"), start=True, stop=True)\
                        .then_inc(kk_mm.sem, 1)

                def scores(seq, s, c):
                    t0 = c * C
                    for j, src in enumerate((bt, kt)):
                        for k in range(2):
                            g = mm(bank[4 + 2 * j + k][:], src[:, k, t0:t0 + C],
                                   ar[:, s, k, c, :, :, :].rearrange("p h j t -> p (h j t)"), start=True, stop=True)
                    g.then_inc(a_mm.sem, 1)

                def right_side(n, u, c):
                    pe.wait_ge(z_d.sem, z_d.past(n, c + 1))
                    for k in range(2):
                        for h in (2 * k, 2 * k + 1):
                            o = bank[0][:, h * HD:(h + 1) * HD]
                            mm(o, ar[:, u, k, c, h % 2, 0, :], Zc[:, c, k, (h % 2) * HD:(h % 2 + 1) * HD], start=(h == 0), stop=False,
                               skip_group_check=True)
                            g = mm(o, akr[:, u, c, h, 0, :], vt[:, u, c, h * HD:(h + 1) * HD], start=False, stop=(h == H - 1),
                                   skip_group_check=True)
                    g.then_inc(r_mm.sem, 1)

                def solve(n, u, c):
                    pe.wait_ge(r_d.sem, r_d.past(n, c + 1))
                    for h in range(H):
                        g = mm(bank[1][:, h * HD:(h + 1) * HD], XT[:, u, c, h, :], r1[:, h * HD:(h + 1) * HD],
                               start=True, stop=True)
                    g.then_inc(u_mm.sem, 1)

                def state(n, u, c):
                    pe.wait_ge(u_d.sem, u_d.past(n, c + 1))
                    for k in range(2):
                        mm(bank[2][:, k * P:(k + 1) * P], bkt[:, u, c, k, :], U[:, k * P:(k + 1) * P], start=True, stop=False)
                        g = mm(bank[2][:, k * P:(k + 1) * P], bkt[:, u, c, 2 + k, :], vt[:, u, c, k * P:(k + 1) * P],
                               start=False, stop=True)
                    g.then_inc(s_mm.sem, 1)

                def output(n, u, c):
                    t0 = c * C
                    pe.wait_ge(o_d.sem, o_d.past(n, c))
                    for k in range(2):
                        mm(bank[3][:, 2 * P:2 * P + H], rk[:, u, k, t0:t0 + C], rkc[:, k, :], start=(k == 0), stop=False,
                           skip_group_check=True)
                    for h in range(H):
                        o = bank[3][:, h * HD:(h + 1) * HD]
                        k = h // 2
                        mm(o, ar[:, u, k, c, h % 2, 1, :], Zc[:, c, k, (h % 2) * HD:(h % 2 + 1) * HD], start=False, stop=False,
                           skip_group_check=True)
                        mm(o, abr[:, u, c, h, 1, :], U[:, h * HD:(h + 1) * HD], start=False, stop=False, skip_group_check=True)
                        g = mm(o, akr[:, u, c, h, 1, :], vt[:, u, c, h * HD:(h + 1) * HD], start=False, stop=(h == H - 1),
                               skip_group_check=True)
                    g.then_inc(o_mm.sem, 1)

                pe.wait_ge(cst, 2)
                pe.wait_ge(par, 16 * npar)
                logits(0)
                kk_means(0)
                pe.wait_ge(ops_d.sem, 1)
                turn(0, 0)
                turn(0, 1)
                pe.wait_ge(rt_d.sem, 4)
                pe.wait_ge(tok_d.sem, 2)
                scores(0, 0, 0)
                pe.wait_ge(a_d.sem, 1)
                scores(0, 0, 1)
                with pe.Fori(0, TURNS) as i:
                    for u in range(2):
                        n = i * 2 + u
                        pe.wait_ge(a_d.sem, a_d.past(n, CB))
                        for l in range(NL):
                            for c in range(CB):
                                pe.wait_ge(x_d.sem, x_d.past(n, at(l, c)))
                                for h in range(H):
                                    g = mm(bank[4 + 2 * c][:, h * C:(h + 1) * C], abr[:, u, c, h, 0, :], X[:, c, h, :],
                                           start=True, stop=True)
                                g.then_inc(t_mm.sem, 1)
                            for c in range(CB):
                                pe.wait_ge(t_d.sem, t_d.past(n, at(l, c)))
                                for h in range(H):
                                    if l < NL - 1:
                                        g = mm(bank[5 + 2 * c][:, h * C:(h + 1) * C], XT[:, u, c, h, :], T[:, c, h, :],
                                               start=True, stop=True)
                                    if l >= NL - 2:
                                        tb = bank[4 + 2 * c] if l == NL - 2 else bank[5 + 2 * c]
                                        g = mm(tb[:, h * C:(h + 1) * C], T[:, c, h, :], XT[:, u, c, h, :], start=True, stop=True)
                                g.then_inc(d_mm.sem, 1)
                            if l == 1:
                                logits(n + 1)
                            elif l == 2:
                                kk_means(n + 1)
                            elif l == 5:
                                pe.wait_ge(pool_d.sem, pool_d.past(n, 1))
                                pe.wait_ge(o_d.sem, o_d.past(n, 0))
                                for c in range(CB):
                                    for k in range(2):
                                        g = mm(bank[3][:, c * 2 * P + k * P:c * 2 * P + (k + 1) * P],
                                               pooled[:, k, c * C:(c + 1) * C], pwb[:, k, :], start=True, stop=True)
                                g.then_inc(pp_mm.sem, 1)
                        pe.wait_ge(gates_d.sem, gates_d.past(n, 2))
                        pe.wait_ge(kstd_d.sem, kstd_d.past(n, 2))
                        right_side(n, u, 0)
                        pe.wait_ge(x_d.sem, x_d.past(n, at(NL, CB - 1)))
                        pe.wait_ge(ops_d.sem, ops_d.past(n, 2))
                        turn(n + 1, 0)
                        solve(n, u, 0)
                        turn(n + 1, 1)
                        state(n, u, 0)
                        pe.wait_ge(pp_d.sem, pp_d.past(n, 1))
                        output(n, u, 0)
                        right_side(n, u, 1)
                        pe.wait_ge(rt_d.sem, rt_d.past(n, 8))
                        pe.wait_ge(tok_d.sem, tok_d.past(n, 2 * CB))
                        scores(n + 1, 1 - u, 0)
                        solve(n, u, 1)
                        state(n, u, 1)
                        output(n, u, 1)
                        pe.wait_ge(a_d.sem, a_d.past(n, CB + 1))
                        scores(n + 1, 1 - u, 1)

            @block.vector
            def _(dve):
                tt, stt, ts = nc.vector.tensor_tensor, nc.vector.scalar_tensor_tensor, nc.vector.tensor_scalar
                copy_if = nc.vector.copy_predicated
                n = [0]

                def chain(ins):
                    n[0] += 1
                    ins.then_inc(dset, 1)
                    dve.wait_ge(dset, n[0])

                def done(cnt, seq, k, ins):
                    ins.then_inc(cnt.sem, 1)
                    dve.wait_ge(cnt.sem, cnt.past(seq, k))

                def shift(seq):
                    dve.wait_ge(zsub.sem, zsub.past(seq, 1))
                    for j in range(NR):
                        g = stt(zf[:, j, :], zf[:, j, :], mu[:, j:j + 1], zin[:, j, 1:W + 1], ALU.mult, ALU.add)
                    done(shifted, seq, 1, g)

                def kk_squares(seq):
                    for j in range(2):
                        g = ts(kk[:, j, :], zf[:, 2 + j, :], vec[:, 2, j:j + 1], None, ALU.mult)
                    done(estep, seq, 1, g)
                    tt(ksq[:], kk[:], kk[:], ALU.mult).then_inc(ksq_d.sem, 1)

                def running_sums(seq):
                    dve.wait_ge(gates_d.sem, gates_d.past(seq, 1))
                    for x in range(2 * CB):
                        g = nc.vector.tensor_tensor_scan(ls[:, x, 1:C + 1], onesf[:], chunked(sw)[:, x, :], 0.0, ALU.mult, ALU.add)
                    done(estep, seq, 2, g)
                    tt(lc[:], ls[:], ls[:, :, C // 2:C // 2 + 1].to_broadcast([P, 2 * CB, C + 1]), ALU.subtract).then_inc(lc_d.sem, 1)

                def kk_unit(seq):
                    dve.wait_ge(kstd_d.sem, kstd_d.past(seq, 1))
                    done(estep, seq, 3, ts(ksq[:], ksq[:], 1e-12, None, ALU.max))
                    done(estep, seq, 4, nc.vector.reciprocal(ksq[:], ksq[:]))
                    done(estep, seq, 5, tt(kk[:], kk[:], ksq[:], ALU.mult))

                def k_and_a(seq, s):
                    for j in range(2):
                        g = ts(ksq[:, j, :], av[:, j, :], vec[:, 3, j:j + 1], vec[:, 4, j:j + 1], ALU.mult, ALU.add)
                    done(estep, seq, 6, g)
                    done(estep, seq, 7, tt(zf[:, 2:4, :], zf[:, 2:4, :], ksq[:], ALU.mult))
                    tt(rk[:, s, :, :], zf[:, 0:2, :], zf[:, 2:4, :], ALU.mult)
                    done(estep, seq, 8, tt(av[:], kk[:], av[:], ALU.mult))

                def operands(seq, s):
                    dve.wait_ge(exp_d.sem, exp_d.past(seq, 1))
                    for h in range(2):
                        hs = slice(h * 64, h * 64 + 64)
                        for k in range(2):
                            stt(ar[hs, s, k, :, h, 0, :], kk[hs, k, :].rearrange("p (c t) -> p c t", t=C), -1.0,
                                ec[hs, k * CB:(k + 1) * CB, 0:C], ALU.mult, ALU.mult)
                    nc.vector.tensor_copy(ends[:, s, 0, :].unsqueeze(2), ei[:, :, 0:1])
                    nc.vector.tensor_copy(ends[:, s, 1, :].unsqueeze(2), ec[:, :, C:C + 1])
                    tt(chunked(bt), chunked(av), ei[:, :, 1:C + 1], ALU.mult)
                    done(ops_d, seq, 1, tt(chunked(kt), zf[:, 2:4, :].rearrange("p k (c t) -> p (k c) t", t=C), ei[:, :, 1:C + 1], ALU.mult))

                def masked(seq, s, c):
                    dve.wait_ge(a_mm.sem, a_mm.past(seq, c + 1))
                    dve.sem_inc(m.passed, 1)
                    for j, dst in enumerate((abr, akr)):
                        for k in range(2):
                            g = copy_if(dst[:, s, c, 2 * k:2 * k + 2, :, :].rearrange("p h j t -> p (h j t)"),
                                        mA[:].rearrange("p h j t -> p (h j t)"), bank[4 + 2 * j + k][:])
                    done(a_d, seq, c + 1, g)
                    done(xstep, seq, 2 * c + 1, nc.vector.tensor_copy(XT[:, s, c, :, :], m.ident[:].unsqueeze(1).to_broadcast([P, H, C])))
                    dve.sem_inc(m.passed, 1)
                    done(xstep, seq, 2 * c + 2, copy_if(XT[:, s, c, :, :], heads(mX1[:]), abr[:, s, c, :, 0, :]))
                    nc.vector.transpose(X[:, c, :, :], XT[:, s, c, :, :]).then_inc(x_d.sem, 1)

                def enter(seq, s, c):
                    for k in range(2):
                        x = k * CB + c
                        g = ts(Zc[:, c, k, :], S[:, k, :], ends[:, s, 0, x:x + 1], None, ALU.mult)
                    done(zstep, seq, c + 1, g)
                    for k in range(2):
                        x = k * CB + c
                        g = ts(Zs[:, k, :], Zc[:, c, k, :], ends[:, s, 1, x:x + 1], None, ALU.mult)
                    done(z_d, seq, c + 1, g)

                def leave(n, u, c):
                    dve.wait_ge(u_mm.sem, u_mm.past(n, c + 1))
                    nc.vector.tensor_copy(U[:], bank[1][:, 0:2 * P]).then_inc(u_d.sem, 1)
                    dve.wait_ge(s_mm.sem, s_mm.past(n, c + 1))
                    for k in range(2):
                        for h in range(2):
                            hs = slice(h * 64, h * 64 + 64)
                            x = k * CB + c
                            g = stt(S[hs, k, hs], bank[2][hs, k * P + h * 64:k * P + h * 64 + 64],
                                    ends[hs, u, 1, x:x + 1], Zs[hs, k, hs], ALU.mult, ALU.add)
                    done(s_d, n, c + 1, g)

                def mean(seq, s):
                    done(gstep, seq, 1, nc.vector.tensor_reduce(st[:, 0, :], ost[:, s, :, :].rearrange("p c (h v) -> p (c h) v", v=HD),
                                                                AX.X, ALU.add))
                    ts(st[:, 1, :], st[:, 0, :], 1.0 / HD, None, ALU.mult).then_inc(gn_mean.sem, 1)

                def variance(seq):
                    dve.wait_ge(gn_sq.sem, gn_sq.past(seq, 1))
                    nc.vector.tensor_reduce(st[:, 2, :], osq[:].rearrange("p c (h v) -> p (c h) v", v=HD), AX.X, ALU.add)\
                        .then_inc(gn_var.sem, 1)

                def inverse_deviation(seq):
                    dve.wait_ge(gn_std.sem, gn_std.past(seq, 1))
                    nc.vector.reciprocal(st[:, 4, :], st[:, 3, :]).then_inc(gn_rec.sem, 1)

                chain(nc.vector.memset(onesf[:], 1.0))
                chain(nc.vector.memset(ls[:], 0.0))
                dve.wait_ge(par, 16 * npar)
                dve.wait_ge(cst, 2)
                chain(ts(vec[:, 4, :], vec[:, 3, :], -1.0, 1.0, ALU.mult, ALU.add))
                for g, wn in enumerate(WINDOWS):
                    hs = slice((g % 2) * 64, (g % 2) * 64 + 64)
                    chain(nc.vector.memset(rc[hs, g // 2, :], 1.0 / wn))
                    chain(ts(rc[hs, g // 2, 0:16], it16[hs, :], float(wn), None, ALU.min))
                    chain(nc.vector.reciprocal(rc[hs, g // 2, 0:16], rc[hs, g // 2, 0:16]))
                dve.sem_inc(rc_set, 1)
                shift(0)
                kk_squares(0)
                running_sums(0)
                kk_unit(0)
                k_and_a(0, 0)
                operands(0, 0)
                enter(0, 0, 0)
                masked(0, 0, 0)
                masked(0, 0, 1)
                with dve.Fori(0, TURNS) as i:
                    for u in range(2):
                        n = i * 2 + u
                        for l in range(NL):
                            for c in range(CB):
                                dve.wait_ge(d_mm.sem, d_mm.past(n, at(l, c)))
                                dve.sem_inc(m.passed, 1)
                                D = bank[5 + 2 * c][:].rearrange("p (h t) -> p h t", t=C)
                                if l < NL - 2:
                                    done(lstep, n, at(l, c), copy_if(X[:, c, :, :], heads(mN[:, l, :]), D))
                                    nc.vector.transpose(XT[:, u, c, :, :], X[:, c, :, :]).then_inc(x_d.sem, 1)
                                elif l == NL - 2:
                                    copy_if(X[:, c, :, :], heads(mN[:, l, :]), D)
                                    DT = bank[4 + 2 * c][:].rearrange("p (h t) -> p h t", t=C)
                                    copy_if(XT[:, u, c, :, :], heads(mT[:, 0, :]), DT).then_inc(x_d.sem, 1)
                                else:
                                    copy_if(XT[:, u, c, :, :], heads(mT[:, 1, :]), D).then_inc(x_d.sem, 1)
                            if l == 0:
                                dve.wait_ge(o_d.sem, o_d.past(n, 0))
                                mean(n, 1 - u)
                                shift(n + 1)
                            elif l == 1:
                                kk_squares(n + 1)
                            elif l == 2:
                                running_sums(n + 1)
                                variance(n)
                            elif l == 3:
                                kk_unit(n + 1)
                                inverse_deviation(n)
                            elif l == 4:
                                k_and_a(n + 1, 1 - u)
                            else:
                                operands(n + 1, 1 - u)
                        dve.wait_ge(pp_mm.sem, pp_mm.past(n, 1))
                        dve.wait_ge(yp_out[u], i * 16)
                        tt(yp[:, u, :, :], bank[3][:].rearrange("p (c f) -> p c f", c=2),
                           psc[:].unsqueeze(1).to_broadcast([P, 2, 2 * P]), ALU.mult).then_inc(pp_d.sem, 1)
                        leave(n, u, 0)
                        enter(n, u, 1)
                        masked(n + 1, 1 - u, 0)
                        leave(n, u, 1)
                        enter(n + 1, 1 - u, 0)
                        masked(n + 1, 1 - u, 1)
                dve.wait_ge(o_d.sem, o_d.past(BLOCKS, 0))
                mean(BLOCKS, 1)
                variance(BLOCKS)
                inverse_deviation(BLOCKS)


def attend(nc, a, m):
    with ExitStack() as ctx:
        sb, ps, sem, count = scope(nc, ctx, "attend")
        H, CB = FOX_HEADS, BT // P
        VW = 1 + 2 * HD
        MROW = HD
        NEG = -1e30

        qa = sb("qa", [P, 2, SEQ], F16)
        ka = sb("ka", [P, 2, SEQ], F16)
        qb = sb("qb", [P, 2, SEQ], F16)
        kb = sb("kb", [P, 2, SEQ], F16)
        v = sb("v", [P, 2, NT, VW + 1], F16)
        ncum = sb("ncum", [P, 2, SEQ])
        cumh = sb("cumh", [P, 2, NT])
        offh = sb("offh", [P, 2, NT])
        nb = sb("nb", [P, 2, NB, NT])
        p32 = sb("p32", [P, 4, BT])
        plo = sb("plo", [P, 4, BT], F16)
        junk = sb("junk", [P, 3, BT])
        mx = sb("mx", [P, 2, CB, NB])
        mm_ = sb("mm_", [P, 4, CB])
        mw = sb("mw", [P, CB, P], F16)
        id16 = sb("id16", [P, P], F16)
        idb = sb("idb", [P, P], BF16)
        mq = sb("mq", [P, P], BF16)
        mk = sb("mk", [P, P], BF16)
        oev = sb("oev", [P, 2, 2, VW])
        rl = sb("rl", [P, CB])
        osb = sb("osb", [P, 2, CB, HD])
        pm = [ps(f"pm{j}") for j in range(3)]
        pw = ps("pmw", (P, 4 * P), F16)
        psc = [ps(f"psc{j}") for j in range(2)]
        po = [ps(f"po{j}") for j in range(2)]

        def schedule(b):
            nq, nm = 4 * (b + 1), 4 * ((b + 1) % NB + 1)
            lag = 3
            lead = max(1, nq - 5)
            done = 0
            for x in range(nq + lag):
                if x < nq:
                    yield "qk", x
                want = nm if x >= lead - 1 else (x + 1) * nm // lead
                while done < want:
                    yield "mx", done
                    done += 1
                if x == min(lead, nq - 1):
                    yield "row", 0
                if x >= lag:
                    yield "pv", x - lag

        STEPS = [(u, b) for u in range(2) for b in range(NB)]
        NQK = 2 * sum(4 * (b + 1) for b in range(NB))
        FIRST = 4
        assert NQK % 12 == 0
        TURNS = H // 2

        width = [BT - max(0, j - 4 * b) * P for u, b in STEPS for j in range(4 * (b + 1))]
        start = {}
        for s, (u, b) in enumerate(STEPS):
            start[s] = sum(4 * (bb + 1) for uu, bb in STEPS[:s])

        def by_pool(n):
            return n % 4 == 3

        k_in = [sem(f"k_in{j}") for j in range(2)]
        q_in = [sem(f"q_in{j}") for j in range(2)]
        v_in = [sem(f"v_in{j}") for j in range(2)]
        c_in = [sem(f"c_in{j}") for j in range(2)]
        mx_mm, mx_d = count("mx_mm", NQK), count("mx_d", NQK, 3)
        row_mm, row_d, rows_w = count("row_mm", 16), count("row_d", 16), count("rows_w", 16)
        qk_mm, exp_d = count("qk_mm", NQK), count("exp_d", NQK, 2)
        lo_v, lo_p = count("lo_v", NQK * 3 // 4), count("lo_p", NQK // 4)
        pv_mm = count("pv_mm", NQK, 4)
        o_ev, o_ready = count("o_ev", 16, 1), count("o_ready", 16)
        out_d = [sem(f"fox_out{j}") for j in range(2)]
        made, cstep = sem("a_made"), sem("a_cstep")
        NDV = 16 * 9 + 2 * 2
        dstep = count("a_dstep", NDV)

        with nc.Block() as block:
            @block.sync
            def _(sp):
                def load_k(slot, head):
                    r = bass.ds(head * HD, HD)
                    for half in range(2):
                        sp.dma_start(qa[half * HD:(half + 1) * HD, slot, :], m.QK[0, half, r, :]).then_inc(q_in[slot], 16)
                        sp.dma_start(ka[half * HD:(half + 1) * HD, slot, :], m.QK[1, 0, r, :]).then_inc(k_in[slot], 16)
                    sp.dma_start(ncum[:, slot, :], m.NC[bass.ds(head, 1), :].partition_broadcast(P)).then_inc(c_in[slot], 16)
                    sp.dma_start(qb[0:HD, slot, :], m.QK[0, 0, r, :]).then_inc(q_in[slot], 16)
                    sp.dma_start(kb[0:HD, slot, :], m.QK[1, 1, r, :]).then_inc(k_in[slot], 16)
                    for half in range(2):
                        sp.dma_start(v[:, slot, :, 1 + half * HD:1 + (half + 1) * HD],
                                     m.V[:, half, r].rearrange("(t p) d -> p t d", p=P)).then_inc(v_in[slot], 16)

                sp.wait_ge(made, 1)
                load_k(0, 0)
                with sp.Fori(0, TURNS) as i:
                    for u in range(2):
                        sp.wait_ge(pv_mm.sem, pv_mm.past(i, u * (NQK // 2)))
                        sp.sem_inc(m.passed, 1)
                        sp.wait_ge(qk_mm.sem, qk_mm.past(i, u * (NQK // 2)))
                        sp.sem_inc(m.passed, 1)
                        load_k(1 - u, (i * 2 + (u + 1)) % H)
                        for b in range(NB):
                            s = u * NB + b
                            sp.wait_ge(o_ready.sem, o_ready.past(i, s + 1))
                            sp.sem_inc(m.passed, 1)
                            sp.dma_start(m.Y[b * BT:(b + 1) * BT, bass.ds((i * 2 + u) * HD, HD)]
                                         .rearrange("(c p) d -> p c d", p=P), osb[:, s % 2, :, :]).then_inc(out_d[s % 2], 16)
                for j in range(2):
                    sp.wait_ge(out_d[j], 16 * 8 * TURNS)
                sp.wait_ge(v_in[0], 32 * (TURNS + 1))
                sp.wait_ge(q_in[0], 48 * (TURNS + 1))
                sp.wait_ge(k_in[0], 48 * (TURNS + 1))
                sp.wait_ge(c_in[0], 16 * (TURNS + 1))

            @block.gpsimd
            def _(pool):
                n = [0]

                def chain(ins):
                    n[0] += 1
                    ins.then_inc(cstep, 1)
                    pool.wait_ge(cstep, n[0])

                chain(nc.gpsimd.memset(v[:, :, :, 0:1], 1.0))
                chain(nc.gpsimd.memset(kb[HD:P, :, :], 0.0))
                chain(nc.gpsimd.memset(qb[HD:P, :, :], 0.0))
                pool.sem_inc(made, 1)
                chain(nc.gpsimd.memset(mw[:], 0.0))
                for t in (id16, idb):
                    chain(nc.gpsimd.memset(t[:], 0.0))
                    chain(nc.gpsimd.affine_select(out=t[:], in_=t[:], compare_op=ALU.not_equal, fill=1.0,
                                                  base=0, pattern=[[-1, P]], channel_multiplier=1))
                for t, sign in ((mq, 1), (mk, -1)):
                    chain(nc.gpsimd.memset(t[:], 0.0))
                    chain(nc.gpsimd.affine_select(out=t[:], in_=t[:], compare_op=ALU.is_ge, fill=NEG,
                                                  base=0, pattern=[[-sign, P]], channel_multiplier=sign))
                for row, f in ((0, TOP), (1, 32.0), (2, 1.0 / 32)):
                    for s in range(2):
                        chain(nc.gpsimd.affine_select(out=kb[HD:P, s, :], in_=kb[HD:P, s, :], compare_op=ALU.not_equal, fill=f,
                                                      base=-row, pattern=[[0, SEQ]], channel_multiplier=1))
                pool.sem_inc(made, 1)
                with pool.Fori(0, TURNS) as i:
                    for x in range(NQK // 4):
                        k = 4 * x + 3
                        pool.wait_ge(exp_d.sem, exp_d.past(i, k + 1))
                        pool.wait_ge(pv_mm.sem, pv_mm.past(i, k + 1 - 4))
                        hi = p32[:, 3, :].bitcast(BF16).rearrange("p (t two) -> p t two", two=2)[:, :, 1]
                        w = width[k]
                        nc.gpsimd.tensor_tensor(plo[:, 3, 0:w], p32[:, 3, 0:w], hi[:, 0:w], ALU.subtract)\
                            .then_inc(lo_p.sem, 1)

            @block.scalar
            def _(act):
                act.sem_inc(exp_d.sem, exp_d.credit)
                act.sem_inc(o_ev.sem, o_ev.credit)
                with act.Fori(0, TURNS) as i:
                    for s, (u, b) in enumerate(STEPS):
                        for kind, x in schedule(b):
                            k = start[s] + x
                            if kind == "qk":
                                act.wait_ge(qk_mm.sem, qk_mm.past(i, k + 1))
                                act.wait_ge(pv_mm.sem, pv_mm.past(i, k + 1 - 4))
                                w = width[k]
                                nc.scalar.activation(p32[:, k % 4, 0:w], psc[k % 2][:, 0:w], ACT.Exp,
                                                     bias=nb[:, u, b, x:x + 1], scale=m.sc[:, 0:1]).then_inc(exp_d.sem, 1)
                        act.wait_ge(pv_mm.sem, pv_mm.past(i, start[s] + 4 * (b + 1)))
                        act.wait_ge(o_ready.sem, o_ready.past(i, s))
                        for j in range(2):
                            g = nc.scalar.activation(oev[:, j, :, :].rearrange("p c d -> p (c d)"), po[j][:, 0:2 * VW], ACT.Copy)
                        g.then_inc(o_ev.sem, 1)

            @block.tensor
            def _(pe):
                pe.sem_inc(pv_mm.sem, pv_mm.credit)
                pe.wait_ge(made, 2)

                def by_query(i, n, u, b, x, g):
                    t, q = x // (b + 1), x % (b + 1)
                    j = 4 * b + t
                    w = min(BT, (j + 1) * P - q * BT)
                    pe.wait_ge(mx_d.sem, n(mx_d, x + 1 - 3))
                    last = q == b
                    if last:
                        nc.tensor.matmul(pm[g][:, w - P:w], idb[:], mq[:], start=True, stop=False, skip_group_check=True)
                    nc.tensor.matmul(pm[g][:, 0:w], qa[:, u, j * P:(j + 1) * P], ka[:, u, q * BT:q * BT + w],
                                     start=not last, stop=True, skip_group_check=last).then_inc(mx_mm.sem, 1)

                def turn_row(i, val):
                    pe.wait_ge(row_d.sem, val(row_d, 1))
                    for t in range(CB):
                        g = nc.tensor.transpose(pw[:, t * P:(t + 1) * P], mw[:, t, :], id16[:])
                    g.then_inc(row_mm.sem, 1)

                pe.wait_ge(q_in[0], 48)
                pe.wait_ge(k_in[0], 48)
                for x in range(FIRST):
                    by_query(0, lambda c, k: c.credit + k, 0, 0, x, x % 3)
                turn_row(0, lambda c, k: c.credit + k)
                with pe.Fori(0, TURNS) as i:
                    done = 0
                    for s, (u, b) in enumerate(STEPS):
                        un, bn = STEPS[(s + 1) % 16]
                        if b == 0:
                            pe.wait_ge(v_in[u], (i + 1) * 32)
                        if b == NB - 1:
                            nth = i + 1 if u == 0 else i + 2
                            pe.wait_ge(q_in[1 - u], nth * 48)
                            pe.wait_ge(k_in[1 - u], nth * 48)
                        for kind, x in schedule(b):
                            k = start[s] + x
                            if kind == "qk":
                                if x == 0:
                                    pe.wait_ge(rows_w.sem, i * 16 + (s + 1))
                                d = max(0, x - 4 * b)
                                w = width[k]
                                t0 = b * BT + d * P
                                pe.wait_ge(exp_d.sem, exp_d.past(i, k + 1 - 2))
                                ks = slice(x * P, (x + 1) * P)
                                diag = x >= 4 * b
                                if diag:
                                    nc.tensor.matmul(psc[k % 2][:, 0:P], idb[:], mk[:], start=True, stop=False,
                                                     skip_group_check=True)
                                nc.tensor.matmul(psc[k % 2][:, 0:w], ka[:, u, ks], qa[:, u, t0:t0 + w], start=not diag,
                                                 stop=False, skip_group_check=diag)
                                nc.tensor.matmul(psc[k % 2][:, 0:w], kb[:, u, ks], qb[:, u, t0:t0 + w], start=False,
                                                 stop=True, skip_group_check=diag).then_inc(qk_mm.sem, 1)
                            elif kind == "mx":
                                by_query(i, lambda c, r, base=done: c.past(i, 0) + (base + FIRST + r), un, bn, x, (done + FIRST + x) % 3)
                            elif kind == "row":
                                turn_row(i, lambda c, r: c.past(i, 0) + (s + 1 + r))
                            else:
                                if x == 0:
                                    pe.wait_ge(o_ev.sem, o_ev.past(i, s))
                                if by_pool(k):
                                    pe.wait_ge(lo_p.sem, lo_p.past(i, k // 4 + 1))
                                else:
                                    pe.wait_ge(lo_v.sem, lo_v.past(i, k - k // 4 + 1))
                                d = max(0, x - 4 * b)
                                hi = p32[:, k % 4, :].bitcast(BF16).rearrange("p (t two) -> p t two", two=2)[:, :, 1]
                                for t in range(d, CB):
                                    c0 = (t - d) * P
                                    o = po[t // 2]
                                    oc = (t % 2) * VW
                                    nc.tensor.matmul(o[:, oc:oc + VW], hi[:, c0:c0 + P], v[:, u, x, 0:VW],
                                                     start=(x == 0 and t % 2 == 0), stop=False, skip_group_check=True)
                                    g = nc.tensor.matmul(o[:, oc:oc + 1 + HD], plo[:, k % 4, c0:c0 + P], v[:, u, x, 0:1 + HD],
                                                         start=False, stop=(x == 4 * b + t), skip_group_check=True)
                                g.then_inc(pv_mm.sem, 1)
                        done += 4 * (bn + 1)

            @block.vector
            def _(dve):
                tt, stt, ts = nc.vector.tensor_tensor, nc.vector.scalar_tensor_tensor, nc.vector.tensor_scalar
                dve.sem_inc(mx_d.sem, mx_d.credit)
                c1 = [0]

                def chain(ins):
                    c1[0] += 1
                    ins.then_inc(first, 1)
                    dve.wait_ge(first, c1[0])

                first = m.first

                def head_vectors(go, slot, head, sig):
                    c, o = m.cum[:].rearrange("p h t -> p (h t)"), m.off[:].rearrange("p h t -> p (h t)")
                    nc.vector.tensor_copy(cumh[:, slot, :], c[:, bass.ds(head * NT, NT)])
                    go(nc.vector.tensor_copy(offh[:, slot, :], o[:, bass.ds(head * NT, NT)]))
                    for b in range(NB):
                        g = ts(nb[:, slot, b, :], cumh[:, slot, :], -1.0, offh[:, slot, 4 * b:4 * b + 1], ALU.mult, ALU.add)
                    sig(g)

                def maximum(val, u, b, x, g, side):
                    t, q = x // (b + 1), x % (b + 1)
                    w = min(BT, (4 * b + t + 1) * P - q * BT)
                    dve.wait_ge(mx_mm.sem, val)
                    dve.sem_inc(m.passed, 1)
                    nc.vector.tensor_tensor_reduce(out=junk[:, g, 0:w], in0=pm[g][:, 0:w], in1=ncum[:, u, q * BT:q * BT + w],
                                                   scale=1.0, scalar=-3e38, op0=ALU.add, op1=ALU.max,
                                                   accum_out=mx[:, side, t, q:q + 1]).then_inc(mx_d.sem, 1)

                def parts(go, u, b, side, mxval, rowval, qval):
                    dve.wait_ge(mx_d.sem, mxval)
                    go(nc.vector.tensor_reduce(mm_[:, 0, :], mx[:, side, :, 0:b + 1], AX.X, ALU.max))
                    go(stt(mm_[:, 1, :], offh[:, u, 4 * b:4 * b + 1].to_broadcast([P, CB]), m.sc[:, 1:2], mm_[:, 0, :],
                           ALU.mult, ALU.add))
                    go(ts(mm_[:, 1, :], mm_[:, 1, :], -1.0, None, ALU.mult))
                    go(ts(mw[:, :, MROW], mm_[:, 1, :], 1.0 / TOP, None, ALU.mult))
                    go(stt(mm_[:, 2, :], mw[:, :, MROW], -TOP, mm_[:, 1, :], ALU.mult, ALU.add))
                    go(ts(mw[:, :, MROW + 1], mm_[:, 2, :], 1.0 / 32, None, ALU.mult))
                    go(stt(mm_[:, 3, :], mw[:, :, MROW + 1], -32.0, mm_[:, 2, :], ALU.mult, ALU.add))
                    ts(mw[:, :, MROW + 2], mm_[:, 3, :], 32.0, None, ALU.mult).then_inc(row_d.sem, 1)
                    dve.wait_ge(row_mm.sem, rowval)
                    nc.vector.tensor_copy(qb[MROW:P, u, b * BT:(b + 1) * BT], pw[MROW:P, :]).then_inc(rows_w.sem, 1)

                dve.wait_ge(made, 2)
                dve.wait_ge(c_in[0], 16)
                head_vectors(chain, 0, 0, chain)
                for x in range(FIRST):
                    maximum(x + 1, 0, 0, x, x % 3, 0)
                parts(chain, 0, 0, 0, mx_d.credit + FIRST, 1, None)
                with dve.Fori(0, TURNS) as i:
                    n = [0]

                    def go(ins):
                        n[0] += 1
                        ins.then_inc(dstep.sem, 1)
                        dve.wait_ge(dstep.sem, dstep.past(i, n[0]))

                    done = 0
                    for s, (u, b) in enumerate(STEPS):
                        un, bn = STEPS[(s + 1) % 16]
                        if b == NB - 1:
                            nth = i + 1 if u == 0 else i + 2
                            dve.wait_ge(c_in[1 - u], nth * 16)
                            head_vectors(go, 1 - u, (i * 2 + (u + 1)) % H, go)
                        for kind, x in schedule(b):
                            k = start[s] + x
                            if kind == "qk":
                                if not by_pool(k):
                                    w = width[k]
                                    dve.wait_ge(exp_d.sem, exp_d.past(i, k + 1))
                                    dve.wait_ge(pv_mm.sem, pv_mm.past(i, k + 1 - 4))
                                    hi = p32[:, k % 4, :].bitcast(BF16).rearrange("p (t two) -> p t two", two=2)[:, :, 1]
                                    tt(plo[:, k % 4, 0:w], p32[:, k % 4, 0:w], hi[:, 0:w], ALU.subtract).then_inc(lo_v.sem, 1)
                            elif kind == "mx":
                                maximum(i * NQK + (FIRST + done + x + 1), un, bn, x, (done + FIRST + x) % 3, (s + 1) % 2)
                            elif kind == "row":
                                parts(go, un, bn, (s + 1) % 2, mx_d.past(i, FIRST + done + 4 * (bn + 1)),
                                      i * 16 + (s + 2), None)
                        done += 4 * (bn + 1)
                        dve.wait_ge(o_ev.sem, o_ev.past(i, s + 1))
                        o4 = oev[:].rearrange("p a c d -> p (a c) d")
                        go(nc.vector.reciprocal(rl[:], o4[:, :, 0]))
                        if s >= 2:
                            dve.wait_ge(out_d[s % 2], i * 128 + 16 * (s // 2))
                        else:
                            dve.wait_ge(out_d[s % 2], i * 128)
                        go(tt(osb[:, s % 2, :, :], o4[:, :, 1:1 + HD], o4[:, :, 1 + HD:VW], ALU.add))
                        stt(osb[:, s % 2, :, :], osb[:, s % 2, :, :], m.sc[:, 4:5], rl[:].unsqueeze(2).to_broadcast([P, CB, HD]),
                            ALU.mult, ALU.mult).then_inc(o_ready.sem, 1)
                    assert n[0] == NDV, n[0]


def output(nc, a, m):
    with ExitStack() as ctx:
        sb, ps, sem, count = scope(nc, ctx, "output")
        HALF = 512
        wo32 = sb("wo32", [P, KT, DM])
        woh, wol = sb("woh", [P, KT, DM], F16), sb("wol", [P, KT, DM], F16)
        wmax = sb("wmax", [P, 4])
        gp = sb("gp", [P, DM])
        UN = 4
        y, g, x = (sb(n, [P, UN, DM]) for n in ("y", "g", "xr"))
        sqy, sqz = sb("sqy", [P, DM]), sb("sqz", [P, HALF])
        yst = sb("yst", [P, UN, 4])
        zst = sb("zst", [P, 2, 6])
        yh, yl = sb("yh", [P, 2, 2, HALF], F16), sb("yl", [P, 2, 2, HALF], F16)
        o = sb("o", [P, 2, DM])
        ptr = [ps(f"optr{j}") for j in range(2)]
        pz = [[ps(f"pz{s}{j}") for j in range(2)] for s in range(2)]

        w_in, gp_in, w_max, w_all, w_hi, w_lo, ostep = (sem("o_" + n) for n in (
            "w_in", "gp_in", "w_max", "w_all", "w_hi", "w_lo", "step"))
        yg_in = [sem(f"yg_in{s}") for s in range(UN)]
        xr_in = [sem(f"xr_in{s}") for s in range(UN)]
        gated, sq_d, norm_d, inv_d, scaled = (count("o_" + n, 1) for n in ("gated", "sq_d", "norm_d", "inv_d", "scaled"))
        tr_mm, hi_d, lo_d = count("o_tr_mm", 2, 2), count("o_hi_d", 2), count("o_lo_d", 2)
        z_mm = count("z_mm", 2 * UN)
        zs_d, z_sq, z_sum, z_std, z_fac = (count(n, UN) for n in ("zs_d", "z_sq", "z_sum", "z_std", "z_fac"))
        o_d, sum_d = count("o_o_d", UN, 2), count("sum_d", UN)
        z_fst, zf_d, rn_d = count("z_first", UN), count("zf_d", UN), count("rn_d", 1)
        sent = [sem(f"out_sent{s}") for s in range(2)]
        TURNS = NT // UN

        with nc.Block() as block:
            @block.sync
            def _(sp):
                sp.dma_start(wo32[:], a.w_out[0].rearrange("(k p) n -> p k n", p=P)).then_inc(w_in, 16)
                sp.dma_start(gp[:], a.norm_post[0:1, :].partition_broadcast(P)).then_inc(gp_in, 16)

                def load(seq, tile, s):
                    sp.wait_ge(tr_mm.sem, tr_mm.past(seq, 2 - 2 * UN))
                    sp.sem_inc(m.passed, 1)
                    r = bass.ds(tile * P, P)
                    sp.dma_start(y[:, s, :], m.Y[r, :]).then_inc(yg_in[s], 16)
                    sp.dma_start(g[:, s, :], m.G[r, :]).then_inc(yg_in[s], 16)

                def load_x(tile, s):
                    sp.dma_start(x[:, s, :], a.x[0, bass.ds(tile * P, P), :]).then_inc(xr_in[s], 16)

                for t in range(UN - 1):
                    r = slice(t * P, (t + 1) * P)
                    sp.dma_start(y[:, t, :], m.Y[r, :]).then_inc(yg_in[t], 16)
                    sp.dma_start(g[:, t, :], m.G[r, :]).then_inc(yg_in[t], 16)
                    if t < 2:
                        load_x(t, t)
                with sp.Fori(0, TURNS) as i:
                    for u in range(UN):
                        load(i * UN + (u + 3), (i * UN + (u + 3)) % NT, (u + 3) % UN)
                        load_x((i * UN + (u + 2)) % NT, (u + 2) % UN)
                        sp.wait_ge(sum_d.sem, sum_d.past(i, u + 1))
                        sp.sem_inc(m.passed, 1)
                        sp.dma_start(m.out[0, bass.ds((i * UN + u) * P, P), :], o[:, u % 2, :]).then_inc(sent[u % 2], 16)
                for s in range(2):
                    sp.wait_ge(sent[s], 16 * (NT // 2))
                for s in range(UN - 1):
                    sp.wait_ge(yg_in[s], 32 * (TURNS + 1))
                for s in range(2):
                    sp.wait_ge(xr_in[s], 16 * (TURNS + 1))

            @block.gpsimd
            def _(pool):
                pool.wait_ge(w_max, 1)
                nc.gpsimd.partition_all_reduce(wmax[:, 1:2], wmax[:, 0:1], P, RMAX).then_inc(w_all, 1)
                with pool.Fori(0, TURNS) as i:
                    for u in range(UN):
                        pool.wait_ge(o_d.sem, o_d.past(i, u + 1))
                        pool.wait_ge(xr_in[u], (i + 1) * 16)
                        nc.gpsimd.tensor_tensor(o[:, u % 2, :], o[:, u % 2, :], x[:, u, :], ALU.add).then_inc(sum_d.sem, 1)

            @block.scalar
            def _(act):
                act.wait_ge(w_max, 2)
                for k in range(KT):
                    ins = nc.scalar.activation(woh[:, k, :], wo32[:, k, :], ACT.Copy, scale=wmax[:, 3:4])
                    ins.then_inc(w_hi, 1)

                def norm(seq, s):
                    act.wait_ge(gated.sem, gated.past(seq, 1))
                    nc.scalar.activation(sqy[:], y[:, s, :], ACT.Square, accum_out=yst[:, s, 0:1]).then_inc(sq_d.sem, 1)
                    act.wait_ge(sq_d.sem, sq_d.past(seq, 1))
                    nc.scalar.activation(yst[:, s, 1:2], yst[:, s, 0:1], ACT.Sqrt, bias=m.eps[:, 2:3]).then_inc(norm_d.sem, 1)

                def hi(seq, s):
                    for j in range(2):
                        act.wait_ge(tr_mm.sem, tr_mm.past(seq, j + 1))
                        nc.scalar.activation(yh[:, s % 2, j, :], ptr[j][:], ACT.Copy).then_inc(hi_d.sem, 1)

                def square_z(i, u):
                    for j in range(2):
                        act.wait_ge(z_mm.sem, z_mm.past(i, 2 * u + j + 1))
                        if j == 0:
                            act.wait_ge(zs_d.sem, zs_d.past(i, u + 1))
                        ins = nc.scalar.activation(sqz[:], pz[u % 2][j][:], ACT.Square, scale=zst[:, u % 2, 0:1],
                                                   accum_out=zst[:, u % 2, 1 + j:2 + j])
                        if j == 0:
                            ins.then_inc(z_fst.sem, 1)
                            act.wait_ge(z_fst.sem, z_fst.past(i, u + 1))
                    ins.then_inc(z_sq.sem, 1)
                    act.wait_ge(z_sum.sem, z_sum.past(i, u + 1))
                    nc.scalar.activation(zst[:, u % 2, 4:5], zst[:, u % 2, 3:4], ACT.Sqrt, bias=m.eps[:, 0:1], scale=1.0 / DM)\
                        .then_inc(z_std.sem, 1)

                norm(0, 0)
                norm(1, 1)
                hi(0, 0)
                with act.Fori(0, TURNS) as i:
                    for u in range(UN):
                        hi(i * UN + (u + 1), (u + 1) % UN)
                        norm(i * UN + (u + 2), (u + 2) % UN)
                        square_z(i, u)

            @block.tensor
            def _(pe):
                pe.sem_inc(tr_mm.sem, tr_mm.credit)

                def turn_y(seq, s):
                    pe.wait_ge(scaled.sem, scaled.past(seq, 1))
                    for j in range(2):
                        for k in range(4):
                            c = (4 * j + k) * P
                            t = nc.tensor.transpose(ptr[j][:, k * P:(k + 1) * P], y[:, s, c:c + P], m.ident[:])
                        t.then_inc(tr_mm.sem, 1)

                def product(i, u, j):
                    for k in range(KT):
                        ks = slice((k % 4) * P, (k % 4 + 1) * P)
                        for c, (l, r) in enumerate(((yh, woh), (yh, wol), (yl, woh))):
                            mm = nc.tensor.matmul(pz[u % 2][j][:], l[:, u % 2, k // 4, ks], r[:, k, j * HALF:(j + 1) * HALF],
                                                  start=(k == 0 and c == 0), stop=(k == KT - 1 and c == 2))
                    mm.then_inc(z_mm.sem, 1)

                turn_y(0, 0)
                pe.wait_ge(w_lo, KT)
                with pe.Fori(0, TURNS) as i:
                    for u in range(UN):
                        seq = i * UN + u
                        pe.wait_ge(lo_d.sem, lo_d.past(seq, 2))
                        pe.wait_ge(o_d.sem, o_d.past(i, u - 1))
                        product(i, u, 0)
                        turn_y(i * UN + (u + 1), (u + 1) % UN)
                        product(i, u, 1)

            @block.vector
            def _(dve):
                tt, stt, ts = nc.vector.tensor_tensor, nc.vector.scalar_tensor_tensor, nc.vector.tensor_scalar
                n = [0]

                def chain(ins):
                    n[0] += 1
                    ins.then_inc(ostep, 1)
                    dve.wait_ge(ostep, n[0])

                dve.sem_inc(o_d.sem, o_d.credit)
                dve.wait_ge(gp_in, 16)
                chain(tt(gp[:], gp[:], m.gate[:], ALU.mult))
                dve.wait_ge(w_in, 16)
                nc.vector.tensor_reduce(wmax[:, 0:1], wo32[:].rearrange("p k n -> p (k n)"), AX.X, ALU.max,
                                        apply_absolute_value=True).then_inc(w_max, 1)
                dve.wait_ge(w_all, 1)
                chain(ts(wmax[:, 2:3], wmax[:, 1:2], 1e-30, 1.0 / TOP, ALU.max, ALU.mult))
                nc.vector.reciprocal(wmax[:, 3:4], wmax[:, 2:3]).then_inc(w_max, 1)
                for k in range(KT):
                    dve.wait_ge(w_hi, k + 1)
                    stt(wol[:, k, :], wo32[:, k, :], wmax[:, 3:4], woh[:, k, :], ALU.mult, ALU.subtract).then_inc(w_lo, 1)

                def prepare_y(seq, s, loads):
                    dve.wait_ge(yg_in[s], loads * 32)
                    tt(y[:, s, :], y[:, s, :], g[:, s, :], ALU.mult).then_inc(gated.sem, 1)
                    dve.wait_ge(norm_d.sem, norm_d.past(seq, 1))
                    ts(yst[:, s, 3:4], yst[:, s, 1:2], 1.0 / TOP, None, ALU.mult).then_inc(inv_d.sem, 1)
                    dve.wait_ge(inv_d.sem, inv_d.past(seq, 1))
                    nc.vector.reciprocal(yst[:, s, 2:3], yst[:, s, 3:4]).then_inc(rn_d.sem, 1)
                    dve.wait_ge(rn_d.sem, rn_d.past(seq, 1))
                    ts(y[:, s, :], y[:, s, :], yst[:, s, 2:3], None, ALU.mult).then_inc(scaled.sem, 1)

                def lo(seq, s):
                    for j in range(2):
                        dve.wait_ge(hi_d.sem, hi_d.past(seq, j + 1))
                        tt(yl[:, s % 2, j, :], ptr[j][:], yh[:, s % 2, j, :], ALU.subtract).then_inc(lo_d.sem, 1)

                prepare_y(0, 0, 1)
                prepare_y(1, 1, 1)
                lo(0, 0)
                with dve.Fori(0, TURNS) as i:
                    for u in range(UN):
                        s = u % 2
                        dve.wait_ge(o_d.sem, o_d.past(i, u))
                        ts(zst[:, s, 0:1], yst[:, u, 3:4], wmax[:, 2:3], None, ALU.mult).then_inc(zs_d.sem, 1)
                        dve.wait_ge(zs_d.sem, zs_d.past(i, u + 1))
                        lo(i * UN + (u + 1), (u + 1) % UN)
                        prepare_y(i * UN + (u + 2), (u + 2) % UN, i + (u + 2) // UN + 1)
                        dve.wait_ge(z_sq.sem, z_sq.past(i, u + 1))
                        tt(zst[:, s, 3:4], zst[:, s, 1:2], zst[:, s, 2:3], ALU.add).then_inc(z_sum.sem, 1)
                        dve.wait_ge(z_std.sem, z_std.past(i, u + 1))
                        nc.vector.reciprocal(zst[:, s, 5:6], zst[:, s, 4:5]).then_inc(z_fac.sem, 1)
                        dve.wait_ge(z_fac.sem, z_fac.past(i, u + 1))
                        ts(zst[:, s, 5:6], zst[:, s, 5:6], zst[:, s, 0:1], None, ALU.mult).then_inc(zf_d.sem, 1)
                        dve.wait_ge(zf_d.sem, zf_d.past(i, u + 1))
                        dve.wait_ge(sent[s], i * 32 + 16 * (u // 2))
                        for j in range(2):
                            ins = stt(o[:, s, j * HALF:(j + 1) * HALF], pz[s][j][:], zst[:, s, 5:6],
                                      gp[:, j * HALF:(j + 1) * HALF], ALU.mult, ALU.mult)
                        ins.then_inc(o_d.sem, 1)


class Inputs:

    def __init__(self, x, c, ada_w, ada_b, norm_pre, norm_post, w_in, fox_q_gain, fox_k_gain, fox_f_bias,
                 rwkv_mu, rwkv_w0, rwkv_w2, rwkv_a0, rwkv_a2, rwkv_k_k, rwkv_k_a, rwkv_r_k, rwkv_ln_g,
                 rwkv_ln_b, pool_w, pool_scale, w_out):
        self.x = x
        self.c = c
        self.ada_w = ada_w
        self.ada_b = ada_b
        self.norm_pre = norm_pre
        self.norm_post = norm_post
        self.w_in = w_in
        self.fox_q_gain = fox_q_gain
        self.fox_k_gain = fox_k_gain
        self.fox_f_bias = fox_f_bias
        self.rwkv_mu = rwkv_mu
        self.rwkv_w0 = rwkv_w0
        self.rwkv_w2 = rwkv_w2
        self.rwkv_a0 = rwkv_a0
        self.rwkv_a2 = rwkv_a2
        self.rwkv_k_k = rwkv_k_k
        self.rwkv_k_a = rwkv_k_a
        self.rwkv_r_k = rwkv_r_k
        self.rwkv_ln_g = rwkv_ln_g
        self.rwkv_ln_b = rwkv_ln_b
        self.pool_w = pool_w
        self.pool_scale = pool_scale
        self.w_out = w_out


def hymba_layer(nc, a, out):
    with ExitStack() as ctx:
        m = persistent(nc, ctx)
        m.out = out
        m.QK = nc.dram_tensor("scratch_qk", [2, 2, FOX_W, SEQ], F16).ap()
        m.V = nc.dram_tensor("scratch_v", [SEQ, 2, FOX_W], F16).ap()
        m.Z = nc.dram_tensor("scratch_z", [ZC, m.HALO + SEQ], F32).ap()
        m.G = nc.dram_tensor("scratch_g", [SEQ, DM], F32).ap()
        m.Y = nc.dram_tensor("scratch_y", [SEQ, DM], F32).ap()
        m.NC = nc.dram_tensor("scratch_nc", [FOX_HEADS, SEQ], F32).ap()
        with ExitStack() as weights:
            m.wh = weights.enter_context(nc.sbuf_tensor("wh", [P, KT, D_IN], F16))
            m.wl = weights.enter_context(nc.sbuf_tensor("wl", [P, KT, D_IN], F16))
            prepare(nc, a, m)
            project(nc, a, m)
        decay(nc, a, m)
        recur(nc, a, m)
        attend(nc, a, m)
        output(nc, a, m)


INPUTS = ("x", "c", "ada_w", "ada_b", "norm_pre", "norm_post", "w_in", "fox_q_gain", "fox_k_gain", "fox_f_bias",
          "rwkv_mu", "rwkv_w0", "rwkv_w2", "rwkv_a0", "rwkv_a2", "rwkv_k_k", "rwkv_k_a", "rwkv_r_k", "rwkv_ln_g",
          "rwkv_ln_b", "pool_w", "pool_scale", "w_out")


def kernel(**inputs):
    import numpy as np
    import concourse.bacc as bacc
    from concourse.bass_utils import run_bass_kernel_spmd

    nc = bacc.Bacc("TRN2", target_bir_lowering=False, num_devices=1)
    arrays, aps = {}, {}
    for name in INPUTS:
        array = np.ascontiguousarray(inputs[name])
        arrays[f"in_{name}"] = array
        aps[name] = nc.dram_tensor(f"in_{name}", array.shape, mybir.dt.from_np(array.dtype), kind="ExternalInput").ap()
    out = nc.dram_tensor("out", [1, SEQ, DM], F32, kind="ExternalOutput").ap()
    hymba_layer(nc, Inputs(**aps), out)
    result = run_bass_kernel_spmd(nc, [arrays], core_ids=[0])
    return result.results[0]["out"]
```

```python
from contextlib import ExitStack

import concourse.bass as bass
from concourse import mybir

F32 = mybir.dt.float32
F16 = mybir.dt.float16
BF16 = mybir.dt.bfloat16
I32 = mybir.dt.int32
ALU = mybir.AluOpType
ACT = mybir.ActivationFunctionType
AX = mybir.AxisListType
RMAX = bass.bass_isa.ReduceOp.max

P = 128
SEQ, DM = 4096, 1024
HD = 64
FOX_HEADS, RWKV_HEADS = 8, 4
FOX_W, RWKV_W, POOL_W = 512, 256, 256
WINDOWS = (2, 4, 8, 16)
RANK = 64
D_IN = 3720
V_COL, F_COL, Z_COL, G_COL = 1024, 1536, 1544, 2696
ZC = 1152
KT = DM // P
BT = 512
NB = SEQ // BT
NT = SEQ // P
EPS = 1e-6
GN_EPS = 64e-5
DECAY = 0.6065306597126334
TOP = 32768.0


class Count:

    def __init__(self, sem, per, credit=0):
        self.sem, self.per, self.credit = sem, per, credit

    def past(self, turn, k):
        return turn * self.per + (self.credit + k)


class Layer:
    pass


def scope(nc, ctx, stage):
    sems = []

    def clear():
        nc.clear_and_free_semaphores(sems)
        nc.all_engine_barrier()

    ctx.callback(clear)

    def sb(name, shape, dt=F32):
        return ctx.enter_context(nc.sbuf_tensor(name, shape, dt))

    def ps(name, shape=(P, 512), dt=F32):
        return ctx.enter_context(nc.psum_tensor(name, list(shape), dt))

    def sem(name):
        sems.append(nc.alloc_semaphore(name=f"{stage}_{name}"))
        return sems[-1]

    def count(name, per, credit=0):
        return Count(sem(name), per, credit)

    return sb, ps, sem, count


def column(v):
    return v.rearrange("(p o) -> p o", o=1)


def prepare(nc, a, m):
    with ExitStack() as ctx:
        sb, ps, sem, count = scope(nc, ctx, "prepare")
        adaw = sb("adaw", [P, 2, 3 * DM])
        WS = 3
        wst = sb("wst", [P, WS, D_IN])
        ccol = sb("ccol", [P, KT])
        csig = sb("csig", [P, KT])
        cbc = sb("cbc", [P, KT, P])
        onesf = sb("onesf", [P, P])
        abcol = sb("abcol", [P, 2 * KT])
        npre = sb("npre", [P, KT])
        rowmax = sb("rowmax", [P, KT])
        rinv = sb("rinv", [P, KT])
        gcol = sb("gcol", [P, KT])
        scol = sb("scol", [P, KT])
        t8 = sb("t8", [P, KT])
        bnd = sb("bnd", [P, 4])
        gains = sb("gains", [P, 2, HD])
        gm = sb("gm", [P, 4])
        pcol = ps("pcol")
        pg = [ps(f"pg{j}") for j in range(2)]

        small, halo = m.small, m.halo
        ada_in = [sem(f"p_ada_in{j}") for j in range(2)]
        w_in = [sem(f"p_w_in{j}") for j in range(WS)]
        c_in = sem("c_in")
        silu = sem("p_silu")
        ada_mm = sem("p_ada_mm")
        w_max = sem("p_w_max")
        w_hi = sem("p_w_hi")
        w_lo = sem("p_w_lo")
        step = sem("p_step")
        allmax = sem("p_allmax")
        const0 = sem("p_const0")
        zero = sb("zero", [P, m.HALO])
        nsmall = 9

        with nc.Block() as block:
            @block.sync
            def _(sp):
                for k in range(KT):
                    if k >= WS:
                        sp.wait_ge(w_lo, k - WS + 1)
                    sp.dma_start(wst[:, k % WS, :], a.w_in[0, k * P:(k + 1) * P, :]).then_inc(w_in[k % WS], 16)
                    if k >= 2:
                        sp.wait_ge(ada_mm, k - 1)
                    sp.dma_start(adaw[:, k % 2, :], a.ada_w[0, k * P:(k + 1) * P, :]).then_inc(ada_in[k % 2], 16)

            @block.gpsimd
            def _(pool):
                nc.gpsimd.memset(m.ident[:], 0.0).then_inc(const0, 1)
                nc.gpsimd.memset(zero[:], 0.0).then_inc(const0, 1)
                pool.wait_ge(const0, 2)
                nc.gpsimd.affine_select(out=m.ident[:], in_=m.ident[:], compare_op=ALU.not_equal, fill=1.0,
                                        base=0, pattern=[[-1, P]], channel_multiplier=1).then_inc(const0, 1)
                pool.dma_start(abcol[:], a.ada_b[0, 0:2 * DM].rearrange("(k p) -> p k", p=P), allow_slow_non_contiguous=True).then_inc(small, 16)
                pool.dma_start(npre[:], a.norm_pre[0].rearrange("(k p) -> p k", p=P), allow_slow_non_contiguous=True).then_inc(small, 16)
                pool.dma_start(m.gate[:], a.ada_b[0:1, 2 * DM:3 * DM].partition_broadcast(P)).then_inc(small, 16)
                pool.dma_start(gains[:, 0, :], a.fox_q_gain[0:1, :].partition_broadcast(P)).then_inc(small, 16)
                pool.dma_start(gains[:, 1, :], a.fox_k_gain[0:1, :].partition_broadcast(P)).then_inc(small, 16)
                for j, g in enumerate((a.fox_q_gain, a.fox_k_gain)):
                    for half in range(2):
                        pool.dma_start(m.qkgain[half * HD:(half + 1) * HD, j:j + 1],
                                       column(g[0]), allow_slow_non_contiguous=True).then_inc(small, 16)
                for k in range(ZC // P):
                    pool.dma_start(m.Z[k * P:(k + 1) * P, 0:m.HALO], zero[:]).then_inc(halo, 16)
                pool.wait_ge(w_max, KT + 1)
                nc.gpsimd.partition_all_reduce(bnd[:, 1:2], bnd[:, 0:1], P, RMAX).then_inc(allmax, 1)
                pool.wait_ge(halo, 16 * (ZC // P))

            @block.scalar
            def _(act):
                act.dma_start(ccol[:], a.c.rearrange("o (k p) -> p (o k)", p=P), allow_slow_non_contiguous=True).then_inc(c_in, 16)
                act.wait_ge(c_in, 16)
                nc.scalar.activation(csig[:], ccol[:], ACT.Sigmoid).then_inc(silu, 1)
                for k in range(KT):
                    act.wait_ge(w_max, k + 1)
                    nc.scalar.activation(m.wh[:, k, :], wst[:, k % WS, :], ACT.Copy,
                                         scale=rinv[:, k:k + 1]).then_inc(w_hi, 1)

            @block.tensor
            def _(pe):
                pe.wait_ge(silu, 3)
                for k in range(KT):
                    pe.wait_ge(ada_in[k % 2], 16 * (k // 2 + 1))
                    for j in range(2 * KT):
                        nc.tensor.matmul(pcol[:, j:j + 1], adaw[:, k % 2, j * P:(j + 1) * P], ccol[:, k:k + 1],
                                         start=(k == 0 and j == 0), stop=(k == KT - 1), skip_group_check=True)
                    for j in range(2):
                        mm = nc.tensor.matmul(pg[j][:], cbc[:, k, :],
                                              adaw[:, k % 2, 2 * DM + j * 512:2 * DM + (j + 1) * 512],
                                              start=(k == 0), stop=(k == KT - 1))
                    mm.then_inc(ada_mm, 1)

            @block.vector
            def _(dve):
                n = [0]

                def chain(ins):
                    n[0] += 1
                    ins.then_inc(step, 1)
                    dve.wait_ge(step, n[0])

                chain(nc.vector.memset(onesf[:], 1.0))
                nc.vector.memset(m.eps[:, 0:1], EPS)
                nc.vector.memset(m.eps[:, 1:2], GN_EPS)
                nc.vector.memset(m.eps[:, 2:3], 1e-24)
                chain(nc.vector.memset(m.eps[:, 3:4], 1.0))
                chain(nc.vector.memset(m.headmean[:], 0.0))
                for half in range(2):
                    sl = slice(half * HD, (half + 1) * HD)
                    chain(nc.vector.memset(m.headmean[sl, sl], 1.0 / HD))
                def row_scale(k):
                    dve.wait_ge(w_in[k % WS], 16 * (k // WS + 1))
                    chain(nc.vector.tensor_reduce(rowmax[:, k:k + 1], wst[:, k % WS, :], AX.X, ALU.max,
                                                  apply_absolute_value=True))
                    chain(nc.vector.tensor_scalar(rowmax[:, k:k + 1], rowmax[:, k:k + 1], 1e-20, 1.0 / TOP,
                                                  ALU.max, ALU.mult))
                    nc.vector.reciprocal(rinv[:, k:k + 1], rowmax[:, k:k + 1]).then_inc(w_max, 1)

                dve.wait_ge(silu, 1)
                nc.vector.tensor_tensor(ccol[:], ccol[:], csig[:], ALU.mult).then_inc(silu, 1)
                dve.wait_ge(silu, 2)
                for k in range(KT):
                    last = nc.vector.tensor_scalar(cbc[:, k, :], onesf[:], ccol[:, k:k + 1], None, ALU.mult)
                last.then_inc(silu, 1)
                row_scale(0)
                for k in range(KT):
                    if k + 1 < KT:
                        row_scale(k + 1)
                    dve.wait_ge(w_hi, k + 1)
                    nc.vector.scalar_tensor_tensor(m.wl[:, k, :], wst[:, k % WS, :], rinv[:, k:k + 1],
                                                   m.wh[:, k, :], ALU.mult, ALU.subtract).then_inc(w_lo, 1)
                dve.wait_ge(small, 16 * nsmall)
                chain(nc.vector.tensor_reduce(gm[:, 0:2], gains[:], AX.X, ALU.max, apply_absolute_value=True))
                chain(nc.vector.tensor_scalar(gm[:, 0:2], gm[:, 0:2], 0.5, 1.0 / 32.0, ALU.max, ALU.mult))
                chain(nc.vector.reciprocal(gm[:, 2:4], gm[:, 0:2]))
                chain(nc.vector.tensor_tensor(m.qkgain[:], m.qkgain[:], gm[:, 2:4], ALU.mult))
                chain(nc.vector.scalar_tensor_tensor(m.sc[:, 0:1], gm[:, 0:1], HD ** -0.5, gm[:, 1:2],
                                                     ALU.mult, ALU.mult))
                chain(nc.vector.reciprocal(m.sc[:, 1:2], m.sc[:, 0:1]))
                dve.wait_ge(ada_mm, KT)
                dve.wait_ge(w_lo, KT)
                chain(nc.vector.tensor_tensor(abcol[:], pcol[:, 0:2 * KT], abcol[:], ALU.add))
                for j in range(2):
                    chain(nc.vector.tensor_tensor(m.gate[:, j * 512:(j + 1) * 512], pg[j][:],
                                                  m.gate[:, j * 512:(j + 1) * 512], ALU.add))
                chain(nc.vector.scalar_tensor_tensor(gcol[:], abcol[:, KT:2 * KT], 1.0, npre[:], ALU.add, ALU.mult))
                chain(nc.vector.tensor_tensor(gcol[:], gcol[:], rowmax[:], ALU.mult))
                chain(nc.vector.tensor_tensor(scol[:], abcol[:, 0:KT], rowmax[:], ALU.mult))
                chain(nc.vector.tensor_reduce(bnd[:, 2:3], gcol[:], AX.X, ALU.max, apply_absolute_value=True))
                chain(nc.vector.tensor_reduce(bnd[:, 3:4], scol[:], AX.X, ALU.max, apply_absolute_value=True))
                nc.vector.tensor_tensor(bnd[:, 0:1], bnd[:, 2:3], bnd[:, 3:4], ALU.add).then_inc(w_max, 1)
                dve.wait_ge(allmax, 1)
                chain(nc.vector.tensor_scalar(m.sc[:, 2:3], bnd[:, 1:2], 1e-30, 32.0 / TOP, ALU.max, ALU.mult))
                chain(nc.vector.reciprocal(m.sc[:, 3:4], m.sc[:, 2:3]))
                chain(nc.vector.tensor_scalar(m.sc[:, 4:5], m.sc[:, 2:3], 2.0 ** 20, None, ALU.mult))
                chain(nc.vector.tensor_scalar(m.gcol[:], gcol[:], m.sc[:, 3:4], None, ALU.mult))
                chain(nc.vector.tensor_scalar(m.scol[:], scol[:], m.sc[:, 3:4], None, ALU.mult))


def project(nc, a, m):
    with ExitStack() as ctx:
        sb, ps, sem, count = scope(nc, ctx, "project")
        jobs = [("qk", n) for n in range(8)] + [("z", n) for n in range(ZC // P)] + \
            [("v", t) for t in range(4)] + [("g", (t, j)) for t in range(4) for j in range(2)]
        NJ = len(jobs)
        assert NJ % 2 == 1
        T_JOB = 11
        TURNS = NB // 2
        NQK = 16

        xt = sb("xt", [P, 4, DM])
        sqx = sb("sqx", [P, DM])
        ssq = sb("ssq", [P, 4])
        rstd = sb("rstd", [P, 4])
        rstd2 = sb("rstd2", [P, 4])
        h32 = sb("h32", [P, 2, BT])
        hh = sb("hh", [P, 2, KT, BT], F16)
        hl = sb("hl", [P, 2, KT, BT], F16)
        uq = sb("uq", [P, 2, BT])
        sq = sb("sq", [P, 2, BT])
        stdb = sb("stdb", [P, BT])
        rec = sb("rec", [P, BT])
        qn = sb("qn", [P, BT])
        sig = sb("sig", [P, BT])
        stage = [sb(f"stage{j}", [P, BT]) for j in range(4)]
        stage16 = [s[:, :].bitcast(F16).rearrange("p (two t) -> p two t", two=2) for s in stage]
        fbc = sb("fbc", [P, 4, FOX_HEADS])
        ptr = [ps(f"ptr{j}") for j in range(2)]
        pmm = [ps(f"pmm{j}") for j in range(2)]
        pss = ps("pss")
        pf = ps("pf")

        x_in = [sem(f"x_in{j}") for j in range(4)]
        sq_done, std_done = count("sq_done", 4), count("std_done", 1)
        rstd_done, xn_done = count("rstd_done", 1), count("xn_done", 4, 4)
        tr_done = count("tr_done", KT, KT)
        h32_done, hi_done, lo_done = count("h32_done", KT, 1), count("hi_done", KT), count("lo_done", KT, 1)
        f_mm, f_out = count("f_mm", 1), count("f_out", 1, 1)
        mm_done = count("mm_done", 2 * NJ)
        qk_sq, qk_ss, qk_std = count("qk_sq", NQK), count("qk_ss", NQK, 1), count("qk_std", NQK)
        qk_rec, qk_n, qk_hi, qk_u = count("qk_rec", NQK), count("qk_n", NQK, 1), count("qk_hi", NQK), count("qk_u", NQK)
        v_hi, sig_done = count("v_hi", 8), count("sig_done", 16)
        USES = (8, 8, NJ - 8, NJ - 8)
        ready = [count(f"stage_ready{j}", uses) for j, uses in enumerate(USES)]
        sent = [count(f"stage_sent{j}", 16 * uses) for j, uses in enumerate(USES)]
        fb_in = sem("fb_in")
        passed, pool_passed = sem("passed"), sem("pool_passed")

        def bank(u, n):
            return (u * NJ + n) % 2

        def slot(u, n):
            if n < 8:
                return n % 2, u * 4 + n // 2
            other = u * (NJ - 8) + n - 8
            return 2 + other % 2, other // 2

        def wait_filled(eng, i, u, n):
            if n < 0:
                u, n = u - 1, n + NJ
            s, used = slot(u, n)
            eng.wait_ge(ready[s].sem, ready[s].past(i, used + 1))

        with nc.Block() as block:
            @block.sync
            def _(sp):
                for t in range(4):
                    sp.dma_start(fbc[:, t, :], a.fox_f_bias[0:1, :].partition_broadcast(P)).then_inc(fb_in, 16)

                def load_x(seq, blk):
                    sp.wait_ge(tr_done.sem, tr_done.past(seq, 0))
                    sp.sem_inc(passed, 1)
                    for j in range(4):
                        sp.dma_start(xt[:, j, :], a.x[0, bass.ds(blk * BT + j * P, P), :]).then_inc(x_in[j], 16)

                def store(i, u, n):
                    kind, w = jobs[n]
                    s, used = slot(u, n)
                    t0 = (i * 2 + u) * BT
                    if kind == "qk":
                        c0 = (w % 4) * P
                        dst = m.QK[w // 4, :, c0:c0 + P, bass.ds(t0, BT)].rearrange("two c t -> c two t")
                        src = stage16[s]
                    elif kind == "z":
                        dst, src = m.Z[w * P:(w + 1) * P, bass.ds(t0 + m.HALO, BT)], stage[s][:]
                    elif kind == "v":
                        dst, src = m.V[bass.ds(t0 + w * P, P), :, :], stage16[s]
                    else:
                        dst, src = m.G[bass.ds(t0 + w[0] * P, P), w[1] * 512:(w[1] + 1) * 512], stage[s][:]
                    sp.wait_ge(ready[s].sem, ready[s].past(i, used + 1))
                    sp.sem_inc(passed, 1)
                    sp.dma_start(dst, src).then_inc(sent[s].sem, 16)

                load_x(0, 0)
                with sp.Fori(0, TURNS) as i:
                    for u in range(2):
                        load_x(i * 2 + (u + 1), (i * 2 + (u + 1)) % NB)
                        for n in (*range(7), 8, 7, *range(9, NJ)):
                            store(i, u, n)
                for s in range(4):
                    sp.wait_ge(sent[s].sem, 16 * TURNS * USES[s])

            @block.tensor
            def _(pe):
                pe.sem_inc(tr_done.sem, tr_done.credit)
                pe.sem_inc(qk_ss.sem, qk_ss.credit)

                def turn_x(seq, k):
                    if k == 0:
                        pe.wait_ge(xn_done.sem, xn_done.past(seq, 4))
                    pe.wait_ge(h32_done.sem, h32_done.past(seq, k - 1))
                    for j in range(4):
                        t = nc.tensor.transpose(ptr[k % 2][:, j * P:(j + 1) * P], xt[:, j, k * P:(k + 1) * P], m.ident[:])
                    t.then_inc(tr_done.sem, 1)

                def products(out, lhs, rhs):
                    for k in range(KT):
                        for c, (l, r) in enumerate(((0, 0), (0, 1), (1, 0))):
                            mm = nc.tensor.matmul(out, lhs(l, k), rhs(r, k), start=(k == 0 and c == 0),
                                                  stop=(k == KT - 1 and c == 2))
                    return mm

                h, w = (hh, hl), (m.wh, m.wl)

                def job(i, u, n):
                    kind, x = jobs[n]
                    s, used = slot(u, n)
                    if 2 <= n < 10:
                        pe.wait_ge(qk_u.sem, qk_u.past(i, u * 8 + n - 1))
                    else:
                        wait_filled(pe, i, u, n - 2)
                    if kind in ("qk", "z"):
                        c0 = x * P if kind == "qk" else Z_COL + x * P
                        products(pmm[bank(u, n)][:], lambda l, k: w[l][:, k, c0:c0 + P],
                                 lambda r, k: h[r][:, u, k, :]).then_inc(mm_done.sem, 1)
                    else:
                        t, c0 = (x, V_COL) if kind == "v" else (x[0], G_COL + x[1] * 512)
                        products(pmm[bank(u, n)][:], lambda l, k: h[l][:, u, k, t * P:(t + 1) * P],
                                 lambda r, k: w[r][:, k, c0:c0 + 512]).then_inc(mm_done.sem, 1)

                def head_means(i, u, x):
                    pe.wait_ge(qk_sq.sem, qk_sq.past(i, u * 8 + x + 1))
                    pe.wait_ge(qk_std.sem, qk_std.past(i, u * 8 + x))
                    nc.tensor.matmul(pss[:], m.headmean[:], sq[:, x % 2, :], start=True, stop=True).then_inc(qk_ss.sem, 1)

                for k in range(KT):
                    turn_x(0, k)
                with pe.Fori(0, TURNS) as i:
                    for u in range(2):
                        blk = i * 2 + u
                        pe.wait_ge(hi_done.sem, hi_done.past(blk, KT))
                        pe.wait_ge(lo_done.sem, lo_done.past(blk, KT))
                        pe.wait_ge(f_out.sem, f_out.past(blk, 0))
                        for t in range(4):
                            mm = products(pf[:, t * 8:(t + 1) * 8], lambda l, k: h[l][:, u, k, t * P:(t + 1) * P],
                                          lambda r, k: w[r][:, k, F_COL:F_COL + FOX_HEADS])
                        mm.then_inc(f_mm.sem, 1)
                        for n in range(NJ):
                            job(i, u, n)
                            if 1 <= n <= 8:
                                head_means(i, u, n - 1)
                            if T_JOB <= n < T_JOB + KT:
                                turn_x(i * 2 + (u + 1), n - T_JOB)

            @block.scalar
            def _(act):
                act.sem_inc(h32_done.sem, h32_done.credit)

                def x_squares(seq, j):
                    act.wait_ge(x_in[j], (seq + 1) * 16)
                    nc.scalar.activation(sqx[:], xt[:, j, :], ACT.Square, accum_out=ssq[:, j:j + 1]).then_inc(sq_done.sem, 1)
                    act.wait_ge(sq_done.sem, sq_done.past(seq, j + 1))

                def x_std(seq):
                    act.wait_ge(xn_done.sem, xn_done.past(seq, 0))
                    nc.scalar.activation(rstd[:], ssq[:], ACT.Sqrt, bias=m.eps[:, 0:1], scale=1.0 / DM)\
                        .then_inc(std_done.sem, 1)
                    act.wait_ge(std_done.sem, std_done.past(seq, 1))

                def h_hi(seq, side, k):
                    act.wait_ge(tr_done.sem, tr_done.past(seq, k + 1))
                    act.wait_ge(lo_done.sem, lo_done.past(seq, k - 1))
                    nc.scalar.activation(h32[:, k % 2, :], ptr[k % 2][:], ACT.Identity, bias=m.scol[:, k:k + 1],
                                         scale=m.gcol[:, k:k + 1]).then_inc(h32_done.sem, 1)
                    act.wait_ge(h32_done.sem, h32_done.past(seq, k + 1))
                    nc.scalar.activation(hh[:, side, k, :], h32[:, k % 2, :], ACT.Copy).then_inc(hi_done.sem, 1)

                def evacuate(i, u, n):
                    kind, x = jobs[n]
                    s, used = slot(u, n)
                    act.wait_ge(mm_done.sem, mm_done.past(i, u * NJ + n + 1))
                    if kind == "qk":
                        act.wait_ge(qk_ss.sem, qk_ss.past(i, u * 8 + x - 1))
                        nc.scalar.activation(sq[:, x % 2, :], pmm[bank(u, n)][:], ACT.Square, scale=m.sc[:, 2:3])\
                            .then_inc(qk_sq.sem, 1)
                        act.wait_ge(qk_n.sem, qk_n.past(i, u * 8 + x - 1))
                        nc.scalar.activation(uq[:, x % 2, :], pmm[bank(u, n)][:], ACT.Copy, scale=m.sc[:, 2:3])\
                            .then_inc(qk_u.sem, 1)
                    elif kind == "z":
                        act.wait_ge(sent[s].sem, sent[s].past(i, 16 * used))
                        nc.scalar.activation(stage[s][:], pmm[bank(u, n)][:], ACT.Copy, scale=m.sc[:, 2:3])\
                            .then_inc(ready[s].sem, 1)
                    elif kind == "v":
                        act.wait_ge(sent[s].sem, sent[s].past(i, 16 * used))
                        nc.scalar.activation(stage16[s][:, 0, :], pmm[bank(u, n)][:], ACT.Copy, scale=2.0 ** -20)\
                            .then_inc(v_hi.sem, 1)
                    else:
                        wait_filled(act, i, u, n - 1 if n > NJ - 8 else -1)
                        nc.scalar.activation(sig[:], pmm[bank(u, n)][:], ACT.Sigmoid, scale=m.sc[:, 2:3])\
                            .then_inc(sig_done.sem, 1)

                def head_std(i, u, x):
                    act.wait_ge(qk_ss.sem, qk_ss.past(i, u * 8 + x + 1))
                    act.wait_ge(qk_rec.sem, qk_rec.past(i, u * 8 + x))
                    nc.scalar.activation(stdb[:], pss[:], ACT.Sqrt, bias=m.eps[:, 0:1]).then_inc(qk_std.sem, 1)

                for j in range(4):
                    x_squares(0, j)
                x_std(0)
                for k in range(KT):
                    h_hi(0, 0, k)
                with act.Fori(0, TURNS) as i:
                    for u in range(2):
                        seq = i * 2 + (u + 1)
                        for n in range(NJ):
                            evacuate(i, u, n)
                            if 1 <= n <= 8:
                                head_std(i, u, n - 1)
                            if 2 <= n <= 5:
                                x_squares(seq, n - 2)
                            if n == 6:
                                x_std(seq)
                            if T_JOB <= n < T_JOB + KT:
                                h_hi(seq, 1 - u, n - T_JOB)

            @block.vector
            def _(dve):
                dve.sem_inc(xn_done.sem, xn_done.credit)
                dve.sem_inc(lo_done.sem, lo_done.credit)
                dve.sem_inc(f_out.sem, f_out.credit)
                dve.sem_inc(qk_n.sem, qk_n.credit)

                def x_scaled(seq):
                    dve.wait_ge(std_done.sem, std_done.past(seq, 1))
                    nc.vector.reciprocal(rstd2[:], rstd[:]).then_inc(rstd_done.sem, 1)
                    dve.wait_ge(rstd_done.sem, rstd_done.past(seq, 1))
                    for j in range(4):
                        nc.vector.tensor_scalar(xt[:, j, :], xt[:, j, :], rstd2[:, j:j + 1], None, ALU.mult)\
                            .then_inc(xn_done.sem, 1)

                def h_lo(seq, side, k):
                    dve.wait_ge(hi_done.sem, hi_done.past(seq, k + 1))
                    nc.vector.tensor_tensor(hl[:, side, k, :], h32[:, k % 2, :], hh[:, side, k, :], ALU.subtract)\
                        .then_inc(lo_done.sem, 1)

                def normalise(i, u, x):
                    dve.wait_ge(qk_std.sem, qk_std.past(i, u * 8 + x + 1))
                    dve.wait_ge(qk_n.sem, qk_n.past(i, u * 8 + x))
                    nc.vector.reciprocal(rec[:], stdb[:]).then_inc(qk_rec.sem, 1)
                    dve.wait_ge(qk_rec.sem, qk_rec.past(i, u * 8 + x + 1))
                    wait_filled(dve, i, u if x else u - 1, x - 1 if x else 7)
                    nc.vector.scalar_tensor_tensor(qn[:], uq[:, x % 2, :], m.qkgain[:, x // 4:x // 4 + 1], rec[:],
                                                   ALU.mult, ALU.mult).then_inc(qk_n.sem, 1)

                def finish(i, u, n):
                    kind, x = jobs[n]
                    s, used = slot(u, n)
                    if kind == "v":
                        dve.wait_ge(v_hi.sem, v_hi.past(i, u * 4 + x + 1))
                        nc.vector.scalar_tensor_tensor(stage16[s][:, 1, :], pmm[bank(u, n)][:], 2.0 ** -20, stage16[s][:, 0, :],
                                                       ALU.mult, ALU.subtract)\
                            .then_inc(ready[s].sem, 1)
                    elif kind == "g":
                        dve.wait_ge(sig_done.sem, sig_done.past(i, u * 8 + n - (NJ - 8) + 1))
                        dve.wait_ge(sent[s].sem, sent[s].past(i, 16 * used))
                        nc.vector.scalar_tensor_tensor(stage[s][:], pmm[bank(u, n)][:], m.sc[:, 2:3], sig[:], ALU.mult, ALU.mult)\
                            .then_inc(ready[s].sem, 1)

                x_scaled(0)
                for k in range(KT):
                    h_lo(0, 0, k)
                dve.wait_ge(fb_in, 64)
                with dve.Fori(0, TURNS) as i:
                    for u in range(2):
                        seq = i * 2 + (u + 1)
                        blk = i * 2 + u
                        dve.wait_ge(f_mm.sem, f_mm.past(blk, 1))
                        nc.vector.scalar_tensor_tensor(
                            m.fl[:, bass.ds(blk * (4 * FOX_HEADS), 4 * FOX_HEADS)], pf[:, 0:32],
                            m.sc[:, 2:3], fbc[:].rearrange("p t h -> p (t h)"), ALU.mult, ALU.add).then_inc(f_out.sem, 1)
                        for n in range(NJ):
                            finish(i, u, n)
                            if 1 <= n <= 8:
                                normalise(i, u, n - 1)
                            if n == 9:
                                x_scaled(seq)
                            if T_JOB <= n < T_JOB + KT:
                                h_lo(seq, 1 - u, n - T_JOB)

            @block.gpsimd
            def _(pool):
                with pool.Fori(0, TURNS) as i:
                    for u in range(2):
                        for x in range(8):
                            s, used = slot(u, x)
                            pool.wait_ge(qk_n.sem, qk_n.past(i, u * 8 + x + 1))
                            pool.wait_ge(sent[s].sem, sent[s].past(i, 16 * used))
                            pool.sem_inc(pool_passed, 1)
                            nc.gpsimd.tensor_copy(stage16[s][:, 0, :], qn[:]).then_inc(qk_hi.sem, 1)
                            pool.wait_ge(qk_hi.sem, qk_hi.past(i, u * 8 + x + 1))
                            nc.gpsimd.tensor_tensor(stage16[s][:, 1, :], qn[:], stage16[s][:, 0, :], ALU.subtract)\
                                .then_inc(ready[s].sem, 1)


def decay(nc, a, m):
    with ExitStack() as ctx:
        sb, ps, sem, count = scope(nc, ctx, "decay")
        NF = NT * FOX_HEADS
        tri = sb("tri", [P, P])
        ones = sb("ones", [P, P])
        ab, ex, ln = sb("ab", [P, NF]), sb("ex", [P, NF]), sb("ln", [P, NF])
        tot = sb("tot", [P, FOX_HEADS, NT])
        crow = sb("crow", [P, 2, P])
        wo32 = sb("wo32", [P, KT, DM])
        npost = sb("npost", [P, DM])
        w_in, post_in, w_max, w_all, w_hi = (sem(n) for n in ("w_in", "post_in", "w_max", "w_all", "w_hi"))
        clamp = sb("clamp", [P, 1])
        pw, pt, pc = ps("pw"), ps("pt"), ps("pc")
        made, ones_made = sem("d_made"), sem("d_ones")
        abs_done, exp_done, ln_done, log_done = (sem("d_" + n) for n in ("abs", "exp", "ln", "log"))
        sums, cum_done, turned, rows, stored, step = (sem("d_" + n) for n in ("sums", "cum", "turned", "rows", "stored", "step"))
        with nc.Block() as block:
            @block.gpsimd
            def _(pool):
                nc.gpsimd.memset(tri[:], 1.0).then_inc(made, 1)
                pool.wait_ge(made, 1)
                nc.gpsimd.affine_select(out=tri[:], in_=tri[:], compare_op=ALU.is_ge, fill=0.0, base=0,
                                        pattern=[[1, P]], channel_multiplier=-1).then_inc(made, 1)
                pool.wait_ge(w_max, 1)
                nc.gpsimd.partition_all_reduce(m.wsc[:, 1:2], m.wsc[:, 0:1], P, RMAX).then_inc(w_all, 1)

            @block.scalar
            def _(act):
                act.wait_ge(abs_done, 1)
                nc.scalar.activation(ex[:], ab[:], ACT.Exp, scale=-1.0).then_inc(exp_done, 1)
                act.wait_ge(exp_done, 1)
                nc.scalar.activation(ln[:], ex[:], ACT.Ln, bias=m.eps[:, 3:4]).then_inc(ln_done, 1)
                act.wait_ge(w_max, 2)
                for k in range(KT):
                    nc.scalar.activation(m.woh[:, k, :], wo32[:, k, :], ACT.Copy, scale=m.wsc[:, 3:4]).then_inc(w_hi, 1)

            @block.tensor
            def _(pe):
                pe.wait_ge(made, 2)
                pe.wait_ge(ones_made, 1)
                pe.wait_ge(log_done, 1)
                nc.tensor.matmul(pw[:, 0:NF], tri[:], m.fl[:], start=True, stop=True)
                nc.tensor.matmul(pt[:, 0:NF], ones[:], m.fl[:], start=True, stop=True).then_inc(sums, 1)
                pe.wait_ge(cum_done, 1)
                cums = m.cum[:].rearrange("p h t -> p (h t)")
                for j in range(2):
                    t = nc.tensor.transpose(pc[:, j * P:(j + 1) * P], cums[:, j * P:(j + 1) * P], m.ident[:])
                t.then_inc(turned, 1)

            @block.vector
            def _(dve):
                n = [0]

                def chain(ins):
                    n[0] += 1
                    ins.then_inc(step, 1)
                    dve.wait_ge(step, n[0])

                nc.vector.memset(ones[:], 1.0).then_inc(ones_made, 1)
                nc.vector.scalar_tensor_tensor(ab[:], m.fl[:], -1.0, m.fl[:], ALU.mult, ALU.max).then_inc(abs_done, 1)
                chain(nc.vector.tensor_scalar(clamp[:], m.sc[:, 0:1], -500.0 * 1024.0 * HD ** 0.5, None, ALU.mult))
                dve.wait_ge(ln_done, 1)
                chain(nc.vector.scalar_tensor_tensor(ab[:], m.fl[:], 0.0, ln[:], ALU.min, ALU.subtract))
                nc.vector.tensor_scalar(m.fl[:], ab[:], clamp[:, 0:1], None, ALU.max).then_inc(log_done, 1)
                dve.wait_ge(sums, 1)
                chain(nc.vector.tensor_copy(tot[:], pt[:, 0:NF].rearrange("p (t h) -> p h t", h=FOX_HEADS)))
                chain(nc.vector.memset(m.off[:], 0.0))
                for h in range(FOX_HEADS):
                    chain(nc.vector.tensor_tensor_scan(m.off[:, h, 1:NT], ones[:, 0:NT - 1], tot[:, h, 0:NT - 1], 0.0,
                                                       ALU.mult, ALU.add))
                nc.vector.tensor_tensor(m.cum[:], pw[:, 0:NF].rearrange("p (t h) -> p h t", h=FOX_HEADS), m.off[:],
                                        ALU.add).then_inc(cum_done, 1)
                dve.wait_ge(w_in, 16)
                nc.vector.tensor_reduce(m.wsc[:, 0:1], wo32[:].rearrange("p k n -> p (k n)"), AX.X, ALU.max,
                                        apply_absolute_value=True).then_inc(w_max, 1)
                dve.wait_ge(w_all, 1)
                dve.wait_ge(turned, 1)
                nc.vector.tensor_scalar(crow[:].rearrange("p j t -> p (j t)"), pc[:, 0:2 * P], m.sc[:, 1:2], -1.0,
                                        ALU.mult, ALU.mult).then_inc(rows, 1)
                chain(nc.vector.tensor_scalar(m.wsc[:, 2:3], m.wsc[:, 1:2], 1e-30, 1.0 / TOP, ALU.max, ALU.mult))
                nc.vector.reciprocal(m.wsc[:, 3:4], m.wsc[:, 2:3]).then_inc(w_max, 1)
                dve.wait_ge(post_in, 16)
                chain(nc.vector.tensor_tensor(m.gate[:], m.gate[:], npost[:], ALU.mult))
                for k in range(KT):
                    dve.wait_ge(w_hi, k + 1)
                    nc.vector.scalar_tensor_tensor(m.wol[:, k, :], wo32[:, k, :], m.wsc[:, 3:4], m.woh[:, k, :],
                                                   ALU.mult, ALU.subtract)

            @block.sync
            def _(sp):
                sp.dma_start(wo32[:], a.w_out[0].rearrange("(k p) n -> p k n", p=P)).then_inc(w_in, 16)
                sp.dma_start(npost[:], a.norm_post[0:1, :].partition_broadcast(P)).then_inc(post_in, 16)
                sp.wait_ge(rows, 1)
                sp.dma_start(m.NC.rearrange("h (t p) -> (h t) p", p=P).rearrange("(j q) p -> q j p", j=2), crow[:])\
                    .then_inc(stored, 16)
                sp.wait_ge(stored, 16)


def persistent(nc, ctx):
    sb, ps, sem, count = scope(nc, ctx, "layer")
    m = Layer()
    m.HALO = 16
    m.first = sem("attend_first")
    m.small, m.halo = sem("small_in"), sem("halo_out")
    m.passed = sem("passed_on")
    m.ident = sb("ident", [P, P])
    m.headmean = sb("headmean", [P, P])
    m.eps = sb("eps", [P, 4])
    m.sc = sb("sc", [P, 8])
    m.gcol = sb("gcol_s", [P, KT])
    m.scol = sb("scol_s", [P, KT])
    m.gate = sb("gate", [P, DM])
    m.qkgain = sb("qkgain", [P, 2])
    m.fl = sb("fl", [P, NT * FOX_HEADS])
    m.cum = sb("cum", [P, FOX_HEADS, NT])
    m.off = sb("off", [P, FOX_HEADS, NT])
    return m


def recur(nc, a, m):
    with ExitStack() as ctx:
        sb, ps, sem, count = scope(nc, ctx, "recur")
        C, CB = P, 2
        W = C * CB
        BLOCKS = SEQ // W
        TURNS = BLOCKS // 2
        NR = 7
        H = RWKV_HEADS
        NL = 6
        G = 2 * H

        zin = sb("zin", [P, NR, W + 1])
        zf = sb("zf", [P, NR, W])
        mu = sb("mu", [P, NR])
        vec = sb("vec", [P, 5, 2])
        wa = sb("wa", [P, 2, 2, P])
        rkc = sb("rkc", [P, 2, H])
        sw = sb("sw", [P, 2, W])
        av = sb("av", [P, 2, W])
        ls = sb("ls", [P, 2 * CB, C + 1])
        lc = sb("lc", [P, 2 * CB, C + 1])
        ec = sb("ec", [P, 2 * CB, C + 1])
        ei = sb("ei", [P, 2 * CB, C + 1])
        kk = sb("kk", [P, 2, W])
        ksq = sb("ksq", [P, 2, W])
        ka = sb("kfac", [P, 2, W])
        bt, kt = sb("bt", [P, 2, W]), sb("kt", [P, 2, W])
        ends = sb("ends", [P, 2, 2, 2 * CB])
        rk = sb("rk", [P, 2, 2, W])
        ar = sb("ar", [P, 2, 2, CB, 2, 2, C])
        abr = sb("abr", [P, 2, CB, H, 2, C])
        akr = sb("akr", [P, 2, CB, H, 2, C])
        XT = sb("XT", [P, 2, CB, H, C])
        bkt = sb("bkt", [P, 2, CB, 4, P])
        vt = sb("vt", [P, 2, CB, 2 * P])
        ost = sb("ost", [P, 2, CB, 2 * P])
        bon = sb("bon", [P, 2, CB, H])
        yp = sb("yp", [P, 2, CB, 2 * P])
        X = sb("X", [P, CB, H, C])
        T = sb("T", [P, CB, H, C])
        r1 = sb("r1", [P, 2 * P])
        U = sb("U", [P, 2 * P])
        S = sb("S", [P, 2, P])
        Zc = sb("Zc", [P, 2, 2, P])
        Zs = sb("Zs", [P, 2, P])
        osq = sb("osq", [P, CB, 2 * P])
        bv = sb("bv", [P, CB, 2 * P])
        st = sb("st", [P, 5, G])
        kinv = sb("kinv", [P, 2, W])
        onesf = sb("onesr", [P, C])
        mA = sb("mA", [P, 2, 2, C], I32)
        mX1 = sb("mX1", [P, C], I32)
        mN = sb("mN", [P, 5, C], I32)
        mT = sb("mT", [P, 2, C], I32)
        mf = sb("mf", [P, C])
        lng, lnb, psc = (sb(n, [P, 2 * P]) for n in ("lng", "lnb", "psc"))
        pwb = sb("pwb", [P, 2, P])
        pin = sb("pin", [P, 2, W + m.HALO])
        s2, s4 = (sb(n, [P, 2, W + m.HALO]) for n in ("s2", "s4"))
        rc = sb("rc", [P, 2, W])
        it16 = sb("it16", [P, 16])
        pooled = sb("pooled", [P, 2, W])
        bank = [ps(f"bank{j}") for j in range(8)]

        cst, par, cstep, dset, rc_set = sem("cst"), sem("par"), sem("cstep"), sem("dset"), sem("rc_set")
        factor_set, zeros = sem("factor_set"), sem("zeros")
        z_in, p_in, y_out, yp_out = sem("z_in"), sem("p_in"), [sem(f"y_out{s}") for s in range(2)], \
            [sem(f"yp_out{s}") for s in range(2)]
        shifted, tanh_d, wa_mm, gates_d, lc_d, exp_d, ksq_d, kk_mm, kss_d, kinv_d, ka_d, ops_d = (count(n, 1) for n in (
            "shifted", "tanh_d", "wa_mm", "gates_d", "lc_d", "exp_d", "ksq_d", "kk_mm", "kss_d", "kinv_d", "ka_d", "ops_d"))
        kk_d, kln_d, gn_ln = count("kk_d", 1), count("kln_d", 1), count("gn_ln", 1)
        zstep_p, ar_d = count("zstep_p", 2), count("ar_d", 8)
        gn_mean, gn_sq, gn_var, gn_rec, y_d, pool_d, pp_mm, pp_d = (count(n, 1) for n in (
            "gn_mean", "gn_sq", "gn_var", "gn_rec", "y_d", "pool_d", "pp_mm", "pp_d"))
        tr_mm, tok_d, b_mm, b_d, k_mm, k_d, r_mm, r_d, u_mm, u_d, s_mm, s_d, z_d, o_mm, o_d = (count("c_" + n, CB) for n in (
            "tr_mm", "tok_d", "b_mm", "b_d", "k_mm", "k_d", "r_mm", "r_d", "u_mm", "u_d", "s_mm", "s_d", "z_d", "o_mm", "o_d"))
        t_mm, t_d, d_mm = count("t_mm", NL * CB), count("t_d", NL * CB), count("d_mm", NL * CB)
        x_d = count("x_d", (NL + 1) * CB)
        estep, xstep, lstep, gstep, zstep = count("estep", 3), count("xstep", 2 * CB), count("lstep", (NL - 2) * CB), \
            count("gstep", 1), count("zstep", CB)
        pstep, ystep, rc4 = count("pstep", 9), count("ystep", 5), count("rc4", 4)
        npar = 18

        def at(l, c):
            return l * CB + c + 1

        def chunked(t):
            return t[:].rearrange("p k (c t) -> p (k c) t", t=C)

        def heads(mask):
            return mask.unsqueeze(1).to_broadcast([P, H, C])

        def flat(t):
            return t.rearrange("p h t -> p (h t)")

        with nc.Block() as block:
            @block.sync
            def _(sp):
                n = [0]

                def load(dst, src):
                    n[0] += 1
                    sp.dma_start(dst, src, allow_slow_non_contiguous=True).then_inc(par, 16)

                def load_z(blk):
                    sp.dma_start(zin[:], m.Z[0:NR * P, bass.ds(blk * W + (m.HALO - 1), W + 1)]
                                 .rearrange("(k p) t -> p k t", p=P)).then_inc(z_in, 16)

                def load_p(blk):
                    sp.dma_start(pin[:], m.Z[NR * P:ZC, bass.ds(blk * W, W + m.HALO)]
                                 .rearrange("(k p) t -> p k t", p=P)).then_inc(p_in, 16)

                load_z(0)
                load_p(0)
                load(mu[:], a.rwkv_mu[0].rearrange("(k p) -> p k", p=P))
                for j, v in enumerate((a.rwkv_w0, a.rwkv_a0, a.rwkv_k_k, a.rwkv_k_a)):
                    load(vec[:, j, :], v[0].rearrange("(k p) -> p k", p=P))
                sp.wait_ge(cst, 1)
                load(wa[0:RANK, 0, :, :], a.rwkv_w2[0].rearrange("r (k c) -> r k c", c=P))
                load(wa[RANK:P, 1, :, :], a.rwkv_a2[0].rearrange("r (k c) -> r k c", c=P))
                for g in range(4):
                    hs = slice((g % 2) * 64, (g % 2) * 64 + 64)
                    load(pwb[hs, g // 2, hs], a.pool_w[0, g])
                    load(rkc[hs, g // 2, g:g + 1], column(a.rwkv_r_k[0, g]))
                load(lng[:], a.rwkv_ln_g[0:1, :].partition_broadcast(P))
                load(lnb[:], a.rwkv_ln_b[0:1, :].partition_broadcast(P))
                load(psc[:], a.pool_scale[0:1, :].partition_broadcast(P))
                assert n[0] == npar, n
                sp.wait_ge(shifted.sem, 1)
                load_z(1)

                def store(dst, cols, src, done):
                    sp.dma_start(m.Y[bass.ds(dst * W, W), cols].rearrange("(c p) f -> p c f", p=P), src).then_inc(done, 16)

                rwkv, pool = slice(FOX_W, FOX_W + RWKV_W), slice(FOX_W + RWKV_W, DM)
                with sp.Fori(0, TURNS) as i:
                    for u in range(2):
                        n = i * 2 + u
                        sp.wait_ge(shifted.sem, shifted.past(n, 2))
                        sp.sem_inc(m.passed, 1)
                        load_z((n + 2) % BLOCKS)
                        sp.wait_ge(pool_d.sem, pool_d.past(n, 1))
                        sp.sem_inc(m.passed, 1)
                        load_p((n + 1) % BLOCKS)
                        sp.wait_ge(y_d.sem, y_d.past(n, 1))
                        sp.sem_inc(m.passed, 1)
                        store((n + (BLOCKS - 1)) % BLOCKS, rwkv, ost[:, 1 - u, :, :], y_out[1 - u])
                        sp.wait_ge(pp_d.sem, pp_d.past(n, 1))
                        sp.sem_inc(m.passed, 1)
                        store(n, pool, yp[:, u, :, :], yp_out[u])
                sp.wait_ge(y_out[1], 16 * TURNS)
                sp.wait_ge(y_d.sem, y_d.past(BLOCKS, 1))
                store(BLOCKS - 1, rwkv, ost[:, 1, :, :], y_out[1])
                sp.wait_ge(y_out[0], 16 * TURNS)
                sp.wait_ge(y_out[1], 16 * (TURNS + 1))
                for s in range(2):
                    sp.wait_ge(yp_out[s], 16 * TURNS)
                sp.wait_ge(z_in, 16 * (BLOCKS + 2))
                sp.wait_ge(p_in, 16 * (BLOCKS + 1))

            @block.gpsimd
            def _(pool):
                n = [0]
                tt = nc.gpsimd.tensor_tensor

                def chain(ins):
                    n[0] += 1
                    ins.then_inc(cstep, 1)
                    pool.wait_ge(cstep, n[0])

                def shift(seq):
                    pool.wait_ge(z_in, (seq + 1) * 16)
                    tt(zf[:], zin[:, :, 0:W], zin[:, :, 1:W + 1], ALU.subtract).then_inc(zstep_p.sem, 1)
                    pool.wait_ge(zstep_p.sem, zstep_p.past(seq, 1))
                    tt(zf[:], zf[:], mu[:].unsqueeze(2).to_broadcast([P, NR, W]), ALU.mult).then_inc(zstep_p.sem, 1)
                    pool.wait_ge(zstep_p.sem, zstep_p.past(seq, 2))
                    tt(zf[:], zf[:], zin[:, :, 1:W + 1], ALU.add).then_inc(shifted.sem, 1)

                def a_and_r(seq, s):
                    pool.wait_ge(exp_d.sem, exp_d.past(seq, 1))
                    pool.wait_ge(kk_d.sem, kk_d.past(seq, 1))
                    for j, src in enumerate((kk, zf)):
                        for h in range(2):
                            hs = slice(h * 64, h * 64 + 64)
                            for k in range(2):
                                tt(ar[hs, s, k, :, h, j, :], src[hs, k, :].rearrange("p (c t) -> p c t", t=C),
                                   ec[hs, k * CB:(k + 1) * CB, j:C + j], ALU.mult).then_inc(ar_d.sem, 1)
                                pool.wait_ge(ar_d.sem, ar_d.past(seq, 4 * j + 2 * h + k + 1))

                def group_norm(seq, s, last=False):
                    o3 = ost[:, s, :, :].rearrange("p c (h v) -> p (c h) v", v=HD)
                    v3 = vt[:, s, :, :].rearrange("p c (h v) -> p (c h) v", v=HD)
                    b3 = bv[:].rearrange("p c (h v) -> p (c h) v", v=HD)

                    def wide(x):
                        return x.unsqueeze(2).to_broadcast([P, G, HD])

                    def step(k, ins):
                        ins.then_inc(ystep.sem, 1)
                        pool.wait_ge(ystep.sem, ystep.past(seq, k))

                    pool.wait_ge(gn_mean.sem, gn_mean.past(seq, 1))
                    step(1, tt(o3, o3, wide(st[:, 1, :]), ALU.subtract))
                    tt(osq[:], ost[:, s, :, :], ost[:, s, :, :], ALU.mult).then_inc(gn_sq.sem, 1)
                    step(2, tt(b3, v3, wide(bon[:, s, :, :].rearrange("p c h -> p (c h)")), ALU.mult))
                    step(3, tt(bv[:], bv[:], lnb[:].unsqueeze(1).to_broadcast([P, CB, 2 * P]), ALU.add))
                    if not last:
                        pooling_sums()
                    pool.wait_ge(gn_rec.sem, gn_rec.past(seq, 1))
                    step(4, tt(o3, o3, wide(st[:, 4, :]), ALU.mult))
                    step(5, tt(ost[:, s, :, :], ost[:, s, :, :], lng[:].unsqueeze(1).to_broadcast([P, CB, 2 * P]), ALU.mult))
                    tt(ost[:, s, :, :], ost[:, s, :, :], bv[:], ALU.add).then_inc(y_d.sem, 1)
                    pool.wait_ge(y_d.sem, y_d.past(seq, 1))

                for t in (wa, pwb, rkc):
                    chain(nc.gpsimd.memset(t[:], 0.0))
                pool.sem_inc(cst, 1)

                def keep(f, base, pattern, mult):
                    chain(nc.gpsimd.affine_select(out=f, in_=f, compare_op=ALU.is_ge, fill=0.0, base=base,
                                                  pattern=pattern, channel_multiplier=mult))

                for s, base in ((0, -1), (1, 0)):
                    chain(nc.gpsimd.memset(mf[:], 1.0))
                    keep(mf[:], base, [[1, C]], -1)
                    for j in range(2):
                        chain(nc.gpsimd.tensor_copy(mA[:, j, s, :], mf[:]))
                for n0, dst in [(2 << l, mN[:, l, :]) for l in range(5)] + [(-1, mX1[:]), (-32, mT[:, 0, :]), (-64, mT[:, 1, :])]:
                    nn = abs(n0)
                    nb = C // (2 * nn)
                    f = mf[:].rearrange("p (b x) -> p b x", x=2 * nn)
                    chain(nc.gpsimd.memset(mf[:], 0.0))
                    chain(nc.gpsimd.memset(f[:, :, 0:nn] if n0 > 0 else f[:, :, nn:2 * nn], 1.0))
                    lo = nn if n0 > 0 else 0
                    keep(f, -lo, [[-2 * nn, nb], [0, 2 * nn]], 1)
                    keep(f, lo + nn - 1, [[2 * nn, nb], [0, 2 * nn]], -1)
                    chain(nc.gpsimd.tensor_copy(dst, mf[:]))
                chain(nc.gpsimd.iota(it16[:], pattern=[[1, 16]], base=1, channel_multiplier=0,
                                     allow_small_or_imprecise_dtypes=True))
                pool.sem_inc(cst, 1)
                pool.wait_ge(par, 16 * npar)
                shift(0)
                pool.wait_ge(shifted.sem, 1)
                pool.wait_ge(rc_set, 1)
                pool.wait_ge(zeros, 7)
                a_and_r(0, 0)
                pool.wait_ge(ops_d.sem, 1)
                pool.wait_ge(tr_mm.sem, CB)
                shift(1)
                with pool.Fori(0, TURNS) as i:
                    for u in range(2):
                        n = i * 2 + u

                        def pooling_sums():
                            def step(k, ins):
                                ins.then_inc(pstep.sem, 1)
                                pool.wait_ge(pstep.sem, pstep.past(n, k))

                            E = W + m.HALO
                            pool.wait_ge(p_in, (n + 1) * 16)
                            step(1, tt(s2[:, :, 1:E], pin[:, :, 1:E], pin[:, :, 0:E - 1], ALU.add))
                            step(2, tt(s4[64:P, 0, 3:E], s2[64:P, 0, 3:E], s2[64:P, 0, 1:E - 2], ALU.add))
                            step(3, tt(s4[:, 1, 3:E], s2[:, 1, 3:E], s2[:, 1, 1:E - 2], ALU.add))
                            step(4, tt(s2[:, 1, 7:E], s4[:, 1, 7:E], s4[:, 1, 3:E - 4], ALU.add))
                            step(5, tt(s4[64:P, 1, 15:E], s2[64:P, 1, 15:E], s2[64:P, 1, 7:E - 8], ALU.add))
                            pool.wait_ge(pp_mm.sem, pp_mm.past(n, 0))
                            for g, sN in enumerate((s2, s4, s2, s4)):
                                hs = slice((g % 2) * 64, (g % 2) * 64 + 64)
                                step(6 + g, tt(pooled[hs, g // 2, :], sN[hs, g // 2, 16:E], rc[hs, g // 2, :], ALU.mult))
                            tt(pooled[:], pooled[:], pin[:, :, 16:E], ALU.subtract).then_inc(pool_d.sem, 1)

                        group_norm(n, 1 - u)
                        if u == 0:
                            for g, wn in enumerate(WINDOWS):
                                hs = slice((g % 2) * 64, (g % 2) * 64 + 64)
                                pool.sem_inc(m.passed, 1)
                                nc.gpsimd.memset(rc[hs, g // 2, 0:16], 1.0 / wn).then_inc(rc4.sem, 1)
                                pool.wait_ge(rc4.sem, rc4.past(i, g + 1))
                        a_and_r(n + 1, 1 - u)
                        pool.wait_ge(ops_d.sem, ops_d.past(n, 2))
                        pool.wait_ge(tr_mm.sem, tr_mm.past(n, 2 * CB))
                        shift(n + 2)
                group_norm(BLOCKS, 1, last=True)

            @block.scalar
            def _(act):
                activate = nc.scalar.activation

                def tanh(seq):
                    act.wait_ge(shifted.sem, shifted.past(seq, 1))
                    activate(zf[0:RANK, 6, :], zf[0:RANK, 6, :], ACT.Tanh).then_inc(tanh_d.sem, 1)

                def gates(seq):
                    act.wait_ge(wa_mm.sem, wa_mm.past(seq, 1))
                    for j in range(2):
                        activate(sw[:, j, :], bank[0][:, j * W:(j + 1) * W], ACT.Sigmoid, bias=vec[:, 0, j:j + 1])
                    for j in range(2):
                        g = activate(av[:, j, :], bank[1][:, j * W:(j + 1) * W], ACT.Sigmoid, bias=vec[:, 1, j:j + 1])
                    g.then_inc(gates_d.sem, 1)

                def kk_squares(seq):
                    for j in range(2):
                        g = activate(ksq[:, j, :], zf[:, 2 + j, :], ACT.Square, scale=vec[:, 2, j:j + 1])
                    g.then_inc(ksq_d.sem, 1)

                def k_factor(seq):
                    act.wait_ge(gates_d.sem, gates_d.past(seq, 1))
                    for j in range(2):
                        g = activate(ka[:, j, :], av[:, j, :], ACT.Identity, scale=vec[:, 3, j:j + 1], bias=vec[:, 4, j:j + 1])
                    g.then_inc(ka_d.sem, 1)

                def logs(seq, before):
                    act.wait_ge(kss_d.sem, kss_d.past(seq, 1))
                    activate(kinv[:], kinv[:], ACT.Ln).then_inc(kln_d.sem, 1)
                    act.wait_ge(gn_var.sem, gn_var.past(before, 1))
                    activate(st[:, 3, :], st[:, 2, :], ACT.Ln, bias=m.eps[:, 1:2], scale=1.0 / HD).then_inc(gn_ln.sem, 1)

                def kk_inverse(seq):
                    act.wait_ge(kln_d.sem, kln_d.past(seq, 1))
                    activate(kinv[:], kinv[:], ACT.Exp, scale=-0.5).then_inc(kinv_d.sem, 1)

                def inverse_deviation(seq):
                    act.wait_ge(gn_ln.sem, gn_ln.past(seq, 1))
                    activate(st[:, 4, :], st[:, 3, :], ACT.Exp, scale=-0.5).then_inc(gn_rec.sem, 1)

                def exps(seq):
                    act.wait_ge(lc_d.sem, lc_d.past(seq, 1))
                    activate(ec[:], lc[:], ACT.Exp, scale=-DECAY)
                    activate(ei[:], lc[:], ACT.Exp, scale=DECAY).then_inc(exp_d.sem, 1)

                def by_token(seq, s, c):
                    act.wait_ge(tr_mm.sem, tr_mm.past(seq, c + 1))
                    activate(bkt[:, s, c, :, :].rearrange("p k t -> p (k t)"), bank[4 + 2 * c][:], ACT.Copy)
                    activate(vt[:, s, c, :], bank[5 + 2 * c][:, 0:2 * P], ACT.Copy).then_inc(tok_d.sem, 1)

                def r1_out(seq, c):
                    act.wait_ge(r_mm.sem, r_mm.past(seq, c + 1))
                    activate(r1[:], bank[0][:, 0:2 * P], ACT.Copy).then_inc(r_d.sem, 1)

                def u_out(seq, c):
                    act.wait_ge(u_mm.sem, u_mm.past(seq, c + 1))
                    activate(U[:], bank[1][:, 0:2 * P], ACT.Copy).then_inc(u_d.sem, 1)

                def o_out(seq, s, c):
                    act.wait_ge(o_mm.sem, o_mm.past(seq, c + 1))
                    activate(ost[:, s, c, :], bank[3][:, 0:2 * P], ACT.Copy)
                    activate(bon[:, s, c, :], bank[3][:, 2 * P:2 * P + H], ACT.Copy).then_inc(o_d.sem, 1)

                act.wait_ge(par, 16 * npar)
                act.wait_ge(cst, 2)
                act.wait_ge(factor_set, 1)
                act.wait_ge(zeros, 7)
                tanh(0)
                kk_squares(0)
                gates(0)
                k_factor(0)
                act.wait_ge(kss_d.sem, 1)
                activate(kinv[:], kinv[:], ACT.Ln).then_inc(kln_d.sem, 1)
                kk_inverse(0)
                exps(0)
                for c in range(CB):
                    by_token(0, 0, c)
                tanh(1)
                kk_squares(1)
                with act.Fori(0, TURNS) as i:
                    for u in range(2):
                        n = i * 2 + u
                        for l in range(NL):
                            for c in range(CB):
                                act.wait_ge(t_mm.sem, t_mm.past(n, at(l, c)))
                                activate(flat(T[:, c, :, :]), bank[4 + 2 * c][:], ACT.Copy).then_inc(t_d.sem, 1)
                            if l == 1:
                                gates(n + 1)
                                k_factor(n + 1)
                            elif l == 2:
                                logs(n + 1, n)
                            elif l == 3:
                                kk_inverse(n + 1)
                                inverse_deviation(n)
                                exps(n + 1)
                        act.wait_ge(y_d.sem, y_d.past(n, 1))
                        if u == 0:
                            act.wait_ge(y_out[0], i * 16)
                        else:
                            act.wait_ge(y_out[1], i * 16 + 16)
                        r1_out(n, 0)
                        by_token(n + 1, 1 - u, 0)
                        u_out(n, 0)
                        by_token(n + 1, 1 - u, 1)
                        o_out(n, u, 0)
                        r1_out(n, 1)
                        u_out(n, 1)
                        o_out(n, u, 1)
                        tanh(n + 2)
                        kk_squares(n + 2)
                act.wait_ge(gn_var.sem, gn_var.past(BLOCKS, 1))
                activate(st[:, 3, :], st[:, 2, :], ACT.Ln, bias=m.eps[:, 1:2], scale=1.0 / HD).then_inc(gn_ln.sem, 1)
                inverse_deviation(BLOCKS)

            @block.tensor
            def _(pe):
                mm = nc.tensor.matmul

                def turn(seq, c):
                    t0 = c * C
                    for j, src in enumerate((bt, kt)):
                        for k in range(2):
                            nc.tensor.transpose(bank[4 + 2 * c][:, (2 * j + k) * P:(2 * j + k + 1) * P],
                                                src[:, k, t0:t0 + C], m.ident[:])
                    for k in range(2):
                        g = nc.tensor.transpose(bank[5 + 2 * c][:, k * P:(k + 1) * P], zf[:, 4 + k, t0:t0 + C], m.ident[:])
                    g.then_inc(tr_mm.sem, 1)

                def logits(seq):
                    pe.wait_ge(tanh_d.sem, tanh_d.past(seq, 1))
                    for j in range(2):
                        for k in range(2):
                            g = mm(bank[j][:, k * W:(k + 1) * W], wa[:, j, k, :], zf[:, 6, :], start=True, stop=True)
                    g.then_inc(wa_mm.sem, 1)

                def kk_means(seq):
                    pe.wait_ge(ksq_d.sem, ksq_d.past(seq, 1))
                    mm(bank[2][:], m.headmean[:], ksq[:].rearrange("p k t -> p (k t)"), start=True, stop=True)\
                        .then_inc(kk_mm.sem, 1)

                def scores(seq, s, c, src, b, done):
                    for k in range(2):
                        g = mm(bank[b + k][:], src[:, k, c * C:(c + 1) * C],
                               ar[:, s, k, c, :, :, :].rearrange("p h j t -> p (h j t)"), start=True, stop=True)
                    g.then_inc(done.sem, 1)

                def right_side(n, u, c):
                    pe.wait_ge(z_d.sem, z_d.past(n, c + 1))
                    for k in range(2):
                        for h in (2 * k, 2 * k + 1):
                            o = bank[0][:, h * HD:(h + 1) * HD]
                            mm(o, ar[:, u, k, c, h % 2, 0, :], Zc[:, c, k, (h % 2) * HD:(h % 2 + 1) * HD], start=(h == 0), stop=False,
                               skip_group_check=True)
                            g = mm(o, akr[:, u, c, h, 0, :], vt[:, u, c, h * HD:(h + 1) * HD], start=False, stop=(h == H - 1),
                                   skip_group_check=True)
                    g.then_inc(r_mm.sem, 1)

                def solve(n, u, c):
                    pe.wait_ge(r_d.sem, r_d.past(n, c + 1))
                    for h in range(H):
                        g = mm(bank[1][:, h * HD:(h + 1) * HD], XT[:, u, c, h, :], r1[:, h * HD:(h + 1) * HD],
                               start=True, stop=True)
                    g.then_inc(u_mm.sem, 1)

                def state(n, u, c):
                    pe.wait_ge(u_d.sem, u_d.past(n, c + 1))
                    for k in range(2):
                        mm(bank[2][:, k * P:(k + 1) * P], bkt[:, u, c, k, :], U[:, k * P:(k + 1) * P], start=True, stop=False)
                        g = mm(bank[2][:, k * P:(k + 1) * P], bkt[:, u, c, 2 + k, :], vt[:, u, c, k * P:(k + 1) * P],
                               start=False, stop=True)
                    g.then_inc(s_mm.sem, 1)

                def output(n, u, c):
                    t0 = c * C
                    pe.wait_ge(o_d.sem, o_d.past(n, c))
                    for k in range(2):
                        mm(bank[3][:, 2 * P:2 * P + H], rk[:, u, k, t0:t0 + C], rkc[:, k, :], start=(k == 0), stop=False,
                           skip_group_check=True)
                    for h in range(H):
                        o = bank[3][:, h * HD:(h + 1) * HD]
                        k = h // 2
                        mm(o, ar[:, u, k, c, h % 2, 1, :], Zc[:, c, k, (h % 2) * HD:(h % 2 + 1) * HD], start=False, stop=False,
                           skip_group_check=True)
                        mm(o, abr[:, u, c, h, 1, :], U[:, h * HD:(h + 1) * HD], start=False, stop=False, skip_group_check=True)
                        g = mm(o, akr[:, u, c, h, 1, :], vt[:, u, c, h * HD:(h + 1) * HD], start=False, stop=(h == H - 1),
                               skip_group_check=True)
                    g.then_inc(o_mm.sem, 1)

                pe.wait_ge(cst, 2)
                pe.wait_ge(par, 16 * npar)
                logits(0)
                kk_means(0)
                pe.wait_ge(ops_d.sem, 1)
                turn(0, 0)
                turn(0, 1)
                pe.wait_ge(ar_d.sem, 8)
                for c in range(CB):
                    pe.wait_ge(tok_d.sem, c + 1)
                    scores(0, 0, c, bt, 4 + 2 * c, b_mm)
                with pe.Fori(0, TURNS) as i:
                    for u in range(2):
                        n = i * 2 + u
                        for l in range(NL):
                            for c in range(CB):
                                pe.wait_ge(x_d.sem, x_d.past(n, at(l, c)))
                                for h in range(H):
                                    g = mm(bank[4 + 2 * c][:, h * C:(h + 1) * C], abr[:, u, c, h, 0, :], X[:, c, h, :],
                                           start=True, stop=True)
                                g.then_inc(t_mm.sem, 1)
                            for c in range(CB):
                                pe.wait_ge(t_d.sem, t_d.past(n, at(l, c)))
                                for h in range(H):
                                    if l < NL - 1:
                                        g = mm(bank[5 + 2 * c][:, h * C:(h + 1) * C], XT[:, u, c, h, :], T[:, c, h, :],
                                               start=True, stop=True)
                                    if l >= NL - 2:
                                        tb = bank[4 + 2 * c] if l == NL - 2 else bank[5 + 2 * c]
                                        g = mm(tb[:, h * C:(h + 1) * C], T[:, c, h, :], XT[:, u, c, h, :], start=True, stop=True)
                                g.then_inc(d_mm.sem, 1)
                            if l == 0:
                                logits(n + 1)
                                pe.wait_ge(s_d.sem, s_d.past(n, 0))
                                kk_means(n + 1)
                            elif l == 1:
                                pe.wait_ge(kss_d.sem, kss_d.past(n, 2))
                                pe.wait_ge(o_d.sem, o_d.past(n, 0))
                                scores(n, u, 0, kt, 2, k_mm)
                            elif l == 2:
                                pe.wait_ge(gates_d.sem, gates_d.past(n, 2))
                                scores(n, u, 1, kt, 0, k_mm)
                            elif l == 5:
                                pe.wait_ge(pool_d.sem, pool_d.past(n, 1))
                                pe.wait_ge(k_d.sem, k_d.past(n, 2))
                                for c in range(CB):
                                    for k in range(2):
                                        g = mm(bank[3][:, c * 2 * P + k * P:c * 2 * P + (k + 1) * P],
                                               pooled[:, k, c * C:(c + 1) * C], pwb[:, k, :], start=True, stop=True)
                                g.then_inc(pp_mm.sem, 1)
                        right_side(n, u, 0)
                        pe.wait_ge(x_d.sem, x_d.past(n, at(NL, CB - 1)))
                        pe.wait_ge(ops_d.sem, ops_d.past(n, 2))
                        turn(n + 1, 0)
                        solve(n, u, 0)
                        turn(n + 1, 1)
                        state(n, u, 0)
                        pe.wait_ge(pp_d.sem, pp_d.past(n, 1))
                        output(n, u, 0)
                        right_side(n, u, 1)
                        pe.wait_ge(ar_d.sem, ar_d.past(n, 16))
                        pe.wait_ge(tok_d.sem, tok_d.past(n, 2 * CB))
                        scores(n + 1, 1 - u, 0, bt, 4, b_mm)
                        solve(n, u, 1)
                        scores(n + 1, 1 - u, 1, bt, 6, b_mm)
                        state(n, u, 1)
                        output(n, u, 1)

            @block.vector
            def _(dve):
                tt, stt, ts = nc.vector.tensor_tensor, nc.vector.scalar_tensor_tensor, nc.vector.tensor_scalar
                copy_if = nc.vector.copy_predicated
                n = [0]

                def chain(ins):
                    n[0] += 1
                    ins.then_inc(dset, 1)
                    dve.wait_ge(dset, n[0])

                def done(cnt, seq, k, ins):
                    ins.then_inc(cnt.sem, 1)
                    dve.wait_ge(cnt.sem, cnt.past(seq, k))

                def running_sums(seq):
                    dve.wait_ge(gates_d.sem, gates_d.past(seq, 1))
                    for x in range(2 * CB):
                        g = nc.vector.tensor_tensor_scan(ls[:, x, 1:C + 1], onesf[:], chunked(sw)[:, x, :], 0.0, ALU.mult, ALU.add)
                    done(estep, seq, 1, g)
                    tt(lc[:], ls[:], ls[:, :, C // 2:C // 2 + 1].to_broadcast([P, 2 * CB, C + 1]), ALU.subtract).then_inc(lc_d.sem, 1)

                def norm_guard(seq):
                    dve.wait_ge(kk_mm.sem, kk_mm.past(seq, 1))
                    ts(kinv[:].rearrange("p k t -> p (k t)"), bank[2][:], float(HD), 1e-24, ALU.mult, ALU.max).then_inc(kss_d.sem, 1)

                def k_new(seq, s):
                    dve.wait_ge(ka_d.sem, ka_d.past(seq, 1))
                    done(estep, seq, 2, tt(ka[:], zf[:, 2:4, :], ka[:], ALU.mult))
                    tt(rk[:, s, :, :], zf[:, 0:2, :], ka[:], ALU.mult)

                def kk_unit(seq):
                    dve.wait_ge(kinv_d.sem, kinv_d.past(seq, 1))
                    for j in range(2):
                        g = stt(kk[:, j, :], zf[:, 2 + j, :], vec[:, 2, j:j + 1], kinv[:, j, :], ALU.mult, ALU.mult)
                    done(kk_d, seq, 1, g)
                    done(estep, seq, 3, stt(av[:], kk[:], -1.0, av[:], ALU.mult, ALU.mult))

                def operands(seq, s):
                    dve.wait_ge(exp_d.sem, exp_d.past(seq, 1))
                    nc.vector.tensor_copy(ends[:, s, 0, :].unsqueeze(2), ei[:, :, 0:1])
                    nc.vector.tensor_copy(ends[:, s, 1, :].unsqueeze(2), ec[:, :, C:C + 1])
                    tt(chunked(bt), chunked(av), ei[:, :, 1:C + 1], ALU.mult)
                    done(ops_d, seq, 1, tt(chunked(kt), chunked(ka), ei[:, :, 1:C + 1], ALU.mult))

                def masked(seq, s, c, dst, b, src, result):
                    dve.wait_ge(src.sem, src.past(seq, c + 1))
                    dve.sem_inc(m.passed, 1)
                    for k in range(2):
                        g = copy_if(dst[:, s, c, 2 * k:2 * k + 2, :, :].rearrange("p h j t -> p (h j t)"),
                                    mA[:].rearrange("p h j t -> p (h j t)"), bank[b + k][:])
                    done(result, seq, c + 1, g)

                def start_inverse(seq, s, c):
                    done(xstep, seq, 2 * c + 1, nc.vector.tensor_copy(XT[:, s, c, :, :], m.ident[:].unsqueeze(1).to_broadcast([P, H, C])))
                    dve.sem_inc(m.passed, 1)
                    done(xstep, seq, 2 * c + 2, copy_if(XT[:, s, c, :, :], heads(mX1[:]), abr[:, s, c, :, 0, :]))
                    nc.vector.transpose(X[:, c, :, :], XT[:, s, c, :, :]).then_inc(x_d.sem, 1)

                def enter(seq, s, c):
                    for k in range(2):
                        x = k * CB + c
                        g = ts(Zc[:, c, k, :], S[:, k, :], ends[:, s, 0, x:x + 1], None, ALU.mult)
                    done(zstep, seq, c + 1, g)
                    for k in range(2):
                        x = k * CB + c
                        g = ts(Zs[:, k, :], Zc[:, c, k, :], ends[:, s, 1, x:x + 1], None, ALU.mult)
                    done(z_d, seq, c + 1, g)

                def leave(n, u, c):
                    dve.wait_ge(s_mm.sem, s_mm.past(n, c + 1))
                    for k in range(2):
                        for h in range(2):
                            hs = slice(h * 64, h * 64 + 64)
                            x = k * CB + c
                            g = stt(S[hs, k, hs], bank[2][hs, k * P + h * 64:k * P + h * 64 + 64],
                                    ends[hs, u, 1, x:x + 1], Zs[hs, k, hs], ALU.mult, ALU.add)
                    done(s_d, n, c + 1, g)

                def mean(seq, s):
                    done(gstep, seq, 1, nc.vector.tensor_reduce(st[:, 0, :], ost[:, s, :, :].rearrange("p c (h v) -> p (c h) v", v=HD),
                                                                AX.X, ALU.add))
                    ts(st[:, 1, :], st[:, 0, :], 1.0 / HD, None, ALU.mult).then_inc(gn_mean.sem, 1)

                def variance(seq):
                    dve.wait_ge(gn_sq.sem, gn_sq.past(seq, 1))
                    nc.vector.tensor_reduce(st[:, 2, :], osq[:].rearrange("p c (h v) -> p (c h) v", v=HD), AX.X, ALU.add)\
                        .then_inc(gn_var.sem, 1)

                chain(nc.vector.memset(onesf[:], 1.0))
                chain(nc.vector.memset(ls[:], 0.0))
                for t in (ar, abr, akr, S, ost, bon, vt):
                    nc.vector.memset(t[:], 0.0).then_inc(zeros, 1)
                dve.wait_ge(zeros, 7)
                dve.wait_ge(par, 16 * npar)
                dve.wait_ge(cst, 2)
                chain(ts(vec[:, 4, :], vec[:, 3, :], -1.0, 1.0, ALU.mult, ALU.add))
                dve.sem_inc(factor_set, 1)
                for g, wn in enumerate(WINDOWS):
                    hs = slice((g % 2) * 64, (g % 2) * 64 + 64)
                    chain(nc.vector.memset(rc[hs, g // 2, :], 1.0 / wn))
                    chain(ts(rc[hs, g // 2, 0:16], it16[hs, :], float(wn), None, ALU.min))
                    chain(nc.vector.reciprocal(rc[hs, g // 2, 0:16], rc[hs, g // 2, 0:16]))
                dve.sem_inc(rc_set, 1)
                running_sums(0)
                norm_guard(0)
                k_new(0, 0)
                kk_unit(0)
                operands(0, 0)
                enter(0, 0, 0)
                for c in range(CB):
                    masked(0, 0, c, abr, 4 + 2 * c, b_mm, b_d)
                    start_inverse(0, 0, c)
                with dve.Fori(0, TURNS) as i:
                    for u in range(2):
                        n = i * 2 + u
                        for l in range(NL):
                            for c in range(CB):
                                dve.wait_ge(d_mm.sem, d_mm.past(n, at(l, c)))
                                dve.sem_inc(m.passed, 1)
                                D = bank[5 + 2 * c][:].rearrange("p (h t) -> p h t", t=C)
                                if l < NL - 2:
                                    done(lstep, n, at(l, c), copy_if(X[:, c, :, :], heads(mN[:, l, :]), D))
                                    nc.vector.transpose(XT[:, u, c, :, :], X[:, c, :, :]).then_inc(x_d.sem, 1)
                                elif l == NL - 2:
                                    copy_if(X[:, c, :, :], heads(mN[:, l, :]), D)
                                    DT = bank[4 + 2 * c][:].rearrange("p (h t) -> p h t", t=C)
                                    copy_if(XT[:, u, c, :, :], heads(mT[:, 0, :]), DT).then_inc(x_d.sem, 1)
                                else:
                                    copy_if(XT[:, u, c, :, :], heads(mT[:, 1, :]), D).then_inc(x_d.sem, 1)
                            if l == 0:
                                dve.wait_ge(o_d.sem, o_d.past(n, 0))
                                mean(n, 1 - u)
                                norm_guard(n + 1)
                            elif l == 1:
                                variance(n)
                            elif l == 2:
                                running_sums(n + 1)
                                masked(n, u, 0, akr, 2, k_mm, k_d)
                            elif l == 3:
                                masked(n, u, 1, akr, 0, k_mm, k_d)
                                k_new(n + 1, 1 - u)
                            elif l == 4:
                                kk_unit(n + 1)
                            else:
                                operands(n + 1, 1 - u)
                        dve.wait_ge(pp_mm.sem, pp_mm.past(n, 1))
                        dve.wait_ge(yp_out[u], i * 16)
                        tt(yp[:, u, :, :], bank[3][:].rearrange("p (c f) -> p c f", c=2),
                           psc[:].unsqueeze(1).to_broadcast([P, 2, 2 * P]), ALU.mult).then_inc(pp_d.sem, 1)
                        leave(n, u, 0)
                        enter(n, u, 1)
                        masked(n + 1, 1 - u, 0, abr, 4, b_mm, b_d)
                        start_inverse(n + 1, 1 - u, 0)
                        leave(n, u, 1)
                        masked(n + 1, 1 - u, 1, abr, 6, b_mm, b_d)
                        start_inverse(n + 1, 1 - u, 1)
                        enter(n + 1, 1 - u, 0)
                dve.wait_ge(o_d.sem, o_d.past(BLOCKS, 0))
                mean(BLOCKS, 1)
                variance(BLOCKS)


def attend(nc, a, m):
    with ExitStack() as ctx:
        sb, ps, sem, count = scope(nc, ctx, "attend")
        H, CB = FOX_HEADS, BT // P
        VW = 1 + 2 * HD
        MROW = HD
        NEG = -1e30

        qa = sb("qa", [P, 2, SEQ], F16)
        ka = sb("ka", [P, 2, SEQ], F16)
        qb = sb("qb", [P, 2, SEQ], F16)
        kb = sb("kb", [P, 2, SEQ], F16)
        v = sb("v", [P, 2, NT, VW + 1], F16)
        ncum = sb("ncum", [P, 2, SEQ])
        cumh = sb("cumh", [P, 2, NT])
        offh = sb("offh", [P, 2, NT])
        offs = sb("offs", [P, 2, NT])
        nb = sb("nb", [P, 2, NB, NT])
        p32 = sb("p32", [P, 4, BT])
        plo = sb("plo", [P, 4, BT], F16)
        junk = sb("junk", [P, 3, BT])
        mx = sb("mx", [P, 2 * NB, CB, NB])
        mp = sb("mp", [P, 4, CB])
        mw = sb("mw", [P, 2, CB, P], F16)
        factors = sb("factors", [P, 2])
        id16 = sb("id16", [P, P], F16)
        idb = sb("idb", [P, P], BF16)
        mq = sb("mq", [P, P], BF16)
        mk = sb("mk", [P, P], BF16)
        oev = sb("oev", [P, 2, 2, VW])
        rl = sb("rl", [P, CB])
        osb = sb("osb", [P, 2, CB, HD])
        pm = [ps(f"pm{j}") for j in range(3)]
        pw = ps("pmw", (P, 4 * P), F16)
        psc = [ps(f"psc{j}") for j in range(2)]
        po = [ps(f"po{j}") for j in range(2)]

        STEPS = [(u, b) for u in range(2) for b in range(NB)]
        NS = len(STEPS)
        NQK = 2 * sum(4 * (b + 1) for b in range(NB))
        TURNS = H // 2
        units = [(s, x) for s, (u, b) in enumerate(STEPS) for x in range(4 * (b + 1))]
        start = [units.index((s, 0)) for s in range(NS)] + [NQK]
        AHEAD = 4 * NB + 16
        PV_LAG = 3
        ROW_LAG, COPY_LAG, MSTEPS = 5, 6, 7
        EARLY_T = BT * (STEPS[units[AHEAD][0]][1] + 1)
        EARLY = sum(start[s + 1] <= AHEAD for s in range(NS))
        assert NQK % 12 == 0 and AHEAD % 12 == 0

        def ahead(k):
            s, x = units[(k + AHEAD) % NQK]
            return s, x, x == 4 * (STEPS[s][1] + 1) - 1

        def complete_at(k):
            return 0 <= k and ahead(k)[2]

        def rows_before(k):
            return EARLY + sum(ahead(kk)[2] for kk in range(k))

        width = [BT - max(0, x - 4 * STEPS[s][1]) * P for s, x in units]

        def by_pool(n):
            return n % 12 in (1, 3, 5, 7, 9, 11, 0)

        pool_units = [k for k in range(NQK) if by_pool(k)]
        dve_units = [k for k in range(NQK) if not by_pool(k)]

        k_in = [sem(f"k_in{j}") for j in range(2)]
        q_in = [sem(f"q_in{j}") for j in range(2)]
        v_in = [sem(f"v_in{j}") for j in range(2)]
        c_in = [sem(f"c_in{j}") for j in range(2)]
        early_in, kb_made, qb_made = sem("early_in"), sem("kb_made"), sem("qb_made")
        mx_mm, mx_d = count("mx_mm", NQK, NQK), count("mx_d", NQK, NQK + 3)
        row_mm, row_d, rows_w = count("row_mm", 16), count("row_d", 16), count("rows_w", 16)
        qk_mm, exp_d = count("qk_mm", NQK), count("exp_d", NQK, 2)
        lo_v, lo_p = count("lo_v", len(dve_units)), count("lo_p", len(pool_units))
        pv_mm = count("pv_mm", NQK, 4)
        o_ev, o_ready = count("o_ev", 16, 1), count("o_ready", 16)
        out_d = [sem(f"fox_out{j}") for j in range(2)]
        made, cstep = sem("a_made"), sem("a_cstep")
        NDV = 2 * 2
        mstep, o_sum = count("mstep", 16 * (MSTEPS - 1)), count("o_sum", 16)
        dstep = count("a_dstep", NDV)

        with nc.Block() as block:
            @block.sync
            def _(sp):
                def load_k(slot, head, t0=0):
                    r = bass.ds(head * HD, HD)
                    ts = slice(t0, SEQ)
                    for half in range(2):
                        sp.dma_start(qa[half * HD:(half + 1) * HD, slot, ts], m.QK[0, half, r, ts]).then_inc(q_in[slot], 16)
                        sp.dma_start(ka[half * HD:(half + 1) * HD, slot, ts], m.QK[1, 0, r, ts]).then_inc(k_in[slot], 16)
                    sp.dma_start(ncum[:, slot, ts], m.NC[bass.ds(head, 1), ts].partition_broadcast(P)).then_inc(c_in[slot], 16)
                    sp.dma_start(qb[0:HD, slot, :], m.QK[0, 0, r, :]).then_inc(q_in[slot], 16)
                    sp.dma_start(kb[0:HD, slot, :], m.QK[1, 1, r, :]).then_inc(k_in[slot], 16)
                    for half in range(2):
                        sp.dma_start(v[:, slot, :, 1 + half * HD:1 + (half + 1) * HD],
                                     m.V[:, half, r].rearrange("(t p) d -> p t d", p=P)).then_inc(v_in[slot], 16)

                early = slice(0, EARLY_T)
                for half in range(2):
                    sp.dma_start(qa[half * HD:(half + 1) * HD, 0, early], m.QK[0, half, 0:HD, early]).then_inc(early_in, 16)
                    sp.dma_start(ka[half * HD:(half + 1) * HD, 0, early], m.QK[1, 0, 0:HD, early]).then_inc(early_in, 16)
                sp.dma_start(ncum[:, 0, early], m.NC[0:1, early].partition_broadcast(P)).then_inc(early_in, 16)
                sp.wait_ge(made, 1)
                load_k(0, 0, EARLY_T)
                with sp.Fori(0, TURNS) as i:
                    for u in range(2):
                        sp.wait_ge(pv_mm.sem, pv_mm.past(i, u * (NQK // 2)))
                        sp.sem_inc(m.passed, 1)
                        sp.wait_ge(qk_mm.sem, qk_mm.past(i, u * (NQK // 2)))
                        sp.sem_inc(m.passed, 1)
                        load_k(1 - u, (i * 2 + (u + 1)) % H)
                        for b in range(NB):
                            s = u * NB + b
                            sp.wait_ge(o_ready.sem, o_ready.past(i, s + 1))
                            sp.sem_inc(m.passed, 1)
                            sp.dma_start(m.Y[b * BT:(b + 1) * BT, bass.ds((i * 2 + u) * HD, HD)]
                                         .rearrange("(c p) d -> p c d", p=P), osb[:, s % 2, :, :]).then_inc(out_d[s % 2], 16)
                for j in range(2):
                    sp.wait_ge(out_d[j], 16 * 8 * TURNS)
                sp.wait_ge(v_in[0], 32 * (TURNS + 1))
                sp.wait_ge(q_in[0], 48 * (TURNS + 1))
                sp.wait_ge(k_in[0], 48 * (TURNS + 1))
                sp.wait_ge(c_in[0], 16 * (TURNS + 1))

            @block.gpsimd
            def _(pool):
                n = [0]

                def chain(ins):
                    n[0] += 1
                    ins.then_inc(cstep, 1)
                    pool.wait_ge(cstep, n[0])

                chain(nc.gpsimd.memset(v[:, :, :, 0:1], 1.0))
                pool.sem_inc(made, 1)
                chain(nc.gpsimd.memset(factors[:], 0.0))
                for row, f in ((0, TOP), (1, 32.0), (2, 1.0 / 32)):
                    chain(nc.gpsimd.affine_select(out=factors[HD:P, :], in_=factors[HD:P, :], compare_op=ALU.not_equal, fill=f,
                                                  base=-row, pattern=[[0, 2]], channel_multiplier=1))
                pool.sem_inc(made, 1)
                chain(nc.gpsimd.memset(mw[:], 0.0))
                for t in (id16, idb):
                    chain(nc.gpsimd.memset(t[:], 0.0))
                    chain(nc.gpsimd.affine_select(out=t[:], in_=t[:], compare_op=ALU.not_equal, fill=1.0,
                                                  base=0, pattern=[[-1, P]], channel_multiplier=1))
                for t, sign in ((mq, 1), (mk, -1)):
                    chain(nc.gpsimd.memset(t[:], 0.0))
                    chain(nc.gpsimd.affine_select(out=t[:], in_=t[:], compare_op=ALU.is_ge, fill=NEG,
                                                  base=0, pattern=[[-sign, P]], channel_multiplier=sign))
                pool.sem_inc(made, 1)
                with pool.Fori(0, TURNS) as i:
                    for k in pool_units:
                        pool.wait_ge(exp_d.sem, exp_d.past(i, k + 1))
                        pool.wait_ge(pv_mm.sem, pv_mm.past(i, k + 1 - 4))
                        hi = p32[:, k % 4, :].bitcast(BF16).rearrange("p (t two) -> p t two", two=2)[:, :, 1]
                        w = width[k]
                        nc.gpsimd.tensor_tensor(plo[:, k % 4, 0:w], p32[:, k % 4, 0:w], hi[:, 0:w], ALU.subtract)\
                            .then_inc(lo_p.sem, 1)

            @block.scalar
            def _(act):
                act.wait_ge(made, 2)
                nc.scalar.activation(kb[HD:P, :, :], factors[HD:P, :].unsqueeze(2).to_broadcast([HD, 2, SEQ]), ACT.Copy)\
                    .then_inc(kb_made, 1)
                act.sem_inc(exp_d.sem, exp_d.credit)
                act.sem_inc(o_ev.sem, o_ev.credit)
                with act.Fori(0, TURNS) as i:
                    def evacuate(s):
                        act.wait_ge(pv_mm.sem, pv_mm.past(i, start[s + 1]))
                        act.wait_ge(o_ready.sem, o_ready.past(i, s))
                        for j in range(2):
                            g = nc.scalar.activation(oev[:, j, :, :].rearrange("p c d -> p (c d)"), po[j][:, 0:2 * VW], ACT.Copy)
                        g.then_inc(o_ev.sem, 1)

                    for k, (s, x) in enumerate(units):
                        u, b = STEPS[s]
                        act.wait_ge(qk_mm.sem, qk_mm.past(i, k + 1))
                        act.wait_ge(pv_mm.sem, pv_mm.past(i, k + 1 - 4))
                        w = width[k]
                        nc.scalar.activation(p32[:, k % 4, 0:w], psc[k % 2][:, 0:w], ACT.Exp,
                                             bias=nb[:, u, b, x:x + 1], scale=m.sc[:, 0:1]).then_inc(exp_d.sem, 1)
                        if s and x == PV_LAG - 1:
                            evacuate(s - 1)
                    evacuate(NS - 1)

            @block.tensor
            def _(pe):
                pe.sem_inc(pv_mm.sem, pv_mm.credit)
                pe.sem_inc(mx_mm.sem, mx_mm.credit)
                pe.wait_ge(made, 3)

                def by_query(n, u, b, x, g):
                    t, q = x // (b + 1), x % (b + 1)
                    j = 4 * b + t
                    w = min(BT, (j + 1) * P - q * BT)
                    pe.wait_ge(mx_d.sem, n(mx_d, 1 - 3))
                    last = q == b
                    if last:
                        nc.tensor.matmul(pm[g][:, w - P:w], idb[:], mq[:], start=True, stop=False, skip_group_check=True)
                    nc.tensor.matmul(pm[g][:, 0:w], qa[:, u, j * P:(j + 1) * P], ka[:, u, q * BT:q * BT + w],
                                     start=not last, stop=True, skip_group_check=last).then_inc(mx_mm.sem, 1)

                def turn_row(nth, side):
                    pe.wait_ge(row_d.sem, nth)
                    for t in range(CB):
                        g = nc.tensor.transpose(pw[:, t * P:(t + 1) * P], mw[:, side, t, :], id16[:])
                    g.then_inc(row_mm.sem, 1)

                pe.wait_ge(early_in, 80)
                rows = 0
                for n in range(AHEAD):
                    s, x = units[n]
                    u, b = STEPS[s]
                    by_query(lambda c, k: c.credit + n + k, u, b, x, n % 3)
                    if x == 4 * (b + 1) - 1:
                        rows += 1
                        turn_row(rows, (rows - 1) % 2)
                pe.wait_ge(q_in[0], 48)
                pe.wait_ge(k_in[0], 48)
                pe.wait_ge(kb_made, 1)
                with pe.Fori(0, TURNS) as i:
                    def output(k):
                        s, x = units[k]
                        u, b = STEPS[s]
                        if x == 0:
                            pe.wait_ge(o_ev.sem, o_ev.past(i, s))
                            if b == 0:
                                pe.wait_ge(v_in[u], (i + 1) * 32)
                        if by_pool(k):
                            pe.wait_ge(lo_p.sem, lo_p.past(i, pool_units.index(k) + 1))
                        else:
                            pe.wait_ge(lo_v.sem, lo_v.past(i, dve_units.index(k) + 1))
                        d = max(0, x - 4 * b)
                        hi = p32[:, k % 4, :].bitcast(BF16).rearrange("p (t two) -> p t two", two=2)[:, :, 1]
                        for t in range(d, CB):
                            c0 = (t - d) * P
                            o = po[t // 2]
                            oc = (t % 2) * VW
                            nc.tensor.matmul(o[:, oc:oc + VW], hi[:, c0:c0 + P], v[:, u, x, 0:VW],
                                             start=(x == 0 and t % 2 == 0), stop=False, skip_group_check=True)
                            g = nc.tensor.matmul(o[:, oc:oc + 1 + HD], plo[:, k % 4, c0:c0 + P], v[:, u, x, 0:1 + HD],
                                                 start=False, stop=(x == 4 * b + t), skip_group_check=True)
                        g.then_inc(pv_mm.sem, 1)

                    for k, (s, x) in enumerate(units):
                        u, b = STEPS[s]
                        if x == 0:
                            pe.wait_ge(rows_w.sem, i * NS + (s + 1))
                        d = max(0, x - 4 * b)
                        w = width[k]
                        t0 = b * BT + d * P
                        pe.wait_ge(exp_d.sem, exp_d.past(i, k + 1 - 2))
                        ks = slice(x * P, (x + 1) * P)
                        diag = x >= 4 * b
                        if diag:
                            nc.tensor.matmul(psc[k % 2][:, 0:P], idb[:], mk[:], start=True, stop=False,
                                             skip_group_check=True)
                        nc.tensor.matmul(psc[k % 2][:, 0:w], ka[:, u, ks], qa[:, u, t0:t0 + w], start=not diag,
                                         stop=False, skip_group_check=diag)
                        nc.tensor.matmul(psc[k % 2][:, 0:w], kb[:, u, ks], qb[:, u, t0:t0 + w], start=False,
                                         stop=True, skip_group_check=diag).then_inc(qk_mm.sem, 1)
                        sa, xa, _ = ahead(k)
                        ua, ba = STEPS[sa]
                        if xa == 0 and ba == 0:
                            nth = i + 1 if ua == 1 else i + 2
                            pe.wait_ge(q_in[ua], nth * 48)
                            pe.wait_ge(k_in[ua], nth * 48)
                        by_query(lambda c, r: c.past(i, AHEAD + k + r), ua, ba, xa, k % 3)
                        if complete_at(k - ROW_LAG):
                            nth = rows_before(k - ROW_LAG + 1)
                            turn_row(i * NS + nth, (nth - 1) % 2)
                        if k >= PV_LAG:
                            output(k - PV_LAG)
                    for k in range(NQK - PV_LAG, NQK):
                        output(k)

            @block.vector
            def _(dve):
                tt, stt, ts = nc.vector.tensor_tensor, nc.vector.scalar_tensor_tensor, nc.vector.tensor_scalar
                nc.vector.memset(qb[HD:P, :, :], 0.0).then_inc(qb_made, 1)
                dve.sem_inc(mx_d.sem, mx_d.credit)
                c1 = [0]

                def chain(ins):
                    c1[0] += 1
                    ins.then_inc(first, 1)
                    dve.wait_ge(first, c1[0])

                first = m.first

                def head_vectors(go, slot, head, sig):
                    c, o = m.cum[:].rearrange("p h t -> p (h t)"), m.off[:].rearrange("p h t -> p (h t)")
                    nc.vector.tensor_copy(cumh[:, slot, :], c[:, bass.ds(head * NT, NT)])
                    go(nc.vector.tensor_copy(offh[:, slot, :], o[:, bass.ds(head * NT, NT)]))
                    ts(offs[:, slot, :], offh[:, slot, :], m.sc[:, 1:2], None, ALU.mult)
                    for b in range(NB):
                        g = ts(nb[:, slot, b, :], cumh[:, slot, :], -1.0, offh[:, slot, 4 * b:4 * b + 1], ALU.mult, ALU.add)
                    sig(g)

                def maximum(val, s, x, g):
                    u, b = STEPS[s]
                    t, q = x // (b + 1), x % (b + 1)
                    w = min(BT, (4 * b + t + 1) * P - q * BT)
                    dve.wait_ge(mx_mm.sem, val)
                    dve.sem_inc(m.passed, 1)
                    nc.vector.tensor_tensor_reduce(out=junk[:, g, 0:w], in0=pm[g][:, 0:w], in1=ncum[:, u, q * BT:q * BT + w],
                                                   scale=1.0, scalar=-3e38, op0=ALU.add, op1=ALU.max,
                                                   accum_out=mx[:, s, t, q:q + 1]).then_inc(mx_d.sem, 1)

                def m_step(j, s, side):
                    u, b = STEPS[s]
                    a1, a2, a3 = (mw[:, side, :, MROW + n] for n in range(3))
                    if j == 0:
                        return nc.vector.tensor_reduce(mp[:, 0, :], mx[:, s, :, 0:b + 1], AX.X, ALU.max)
                    if j == 1:
                        return stt(mp[:, 1, :], mp[:, 0, :], -1.0, offs[:, u, 4 * b:4 * b + 1].to_broadcast([P, CB]),
                                   ALU.mult, ALU.subtract)
                    if j == 2:
                        return ts(a1, mp[:, 1, :], 1.0 / TOP, None, ALU.mult)
                    if j == 3:
                        return stt(mp[:, 2, :], a1, -TOP, mp[:, 1, :], ALU.mult, ALU.add)
                    if j == 4:
                        return ts(a2, mp[:, 2, :], 1.0 / 32, None, ALU.mult)
                    if j == 5:
                        return stt(mp[:, 3, :], a2, -32.0, mp[:, 2, :], ALU.mult, ALU.add)
                    return ts(a3, mp[:, 3, :], 32.0, None, ALU.mult)

                def copy_row(s, nth):
                    u, b = STEPS[s]
                    dve.wait_ge(row_mm.sem, nth)
                    nc.vector.tensor_copy(qb[MROW:P, u, b * BT:(b + 1) * BT], pw[MROW:P, :]).then_inc(rows_w.sem, 1)

                dve.wait_ge(made, 3)
                dve.wait_ge(qb_made, 1)
                dve.wait_ge(early_in, 80)
                head_vectors(chain, 0, 0, chain)
                rows = 0
                for n0 in range(AHEAD):
                    s, x = units[n0]
                    maximum(mx_mm.credit + n0 + 1, s, x, n0 % 3)
                    if x == 4 * (STEPS[s][1] + 1) - 1:
                        rows += 1
                        dve.wait_ge(mx_d.sem, mx_d.credit + n0 + 1)
                        for j in range(MSTEPS - 1):
                            chain(m_step(j, s, (rows - 1) % 2))
                        m_step(MSTEPS - 1, s, (rows - 1) % 2).then_inc(row_d.sem, 1)
                        copy_row(s, rows)
                dve.wait_ge(c_in[0], 16)
                with dve.Fori(0, TURNS) as i:
                    n = [0]

                    def go(ins):
                        n[0] += 1
                        ins.then_inc(dstep.sem, 1)
                        dve.wait_ge(dstep.sem, dstep.past(i, n[0]))

                    def lower(k):
                        if not by_pool(k):
                            w = width[k]
                            dve.wait_ge(exp_d.sem, exp_d.past(i, k + 1))
                            dve.wait_ge(pv_mm.sem, pv_mm.past(i, k + 1 - 4))
                            hi = p32[:, k % 4, :].bitcast(BF16).rearrange("p (t two) -> p t two", two=2)[:, :, 1]
                            tt(plo[:, k % 4, 0:w], p32[:, k % 4, 0:w], hi[:, 0:w], ALU.subtract).then_inc(lo_v.sem, 1)

                    def result(s):
                        dve.wait_ge(o_ev.sem, o_ev.past(i, s + 1))
                        o4 = oev[:].rearrange("p a c d -> p (a c) d")
                        nc.vector.reciprocal(rl[:], o4[:, :, 0])
                        dve.wait_ge(out_d[s % 2], i * 128 + 16 * (s // 2))
                        tt(osb[:, s % 2, :, :], o4[:, :, 1:1 + HD], o4[:, :, 1 + HD:VW], ALU.add).then_inc(o_sum.sem, 1)

                    def result_scaled(s):
                        dve.wait_ge(o_sum.sem, o_sum.past(i, s + 1))
                        stt(osb[:, s % 2, :, :], osb[:, s % 2, :, :], m.sc[:, 4:5], rl[:].unsqueeze(2).to_broadcast([P, CB, HD]),
                            ALU.mult, ALU.mult).then_inc(o_ready.sem, 1)

                    def m_steps(k, part):
                        for d in range((MSTEPS + 1) // 2):
                            j = 2 * d + part
                            if j < MSTEPS and complete_at(k - d):
                                s = ahead(k - d)[0]
                                nth = rows_before(k - d + 1)
                                if j == 0:
                                    dve.wait_ge(mx_d.sem, mx_d.past(i, AHEAD + k + 1))
                                else:
                                    dve.wait_ge(mstep.sem, mstep.past(i, (nth - 1 - EARLY) * (MSTEPS - 1) + j))
                                ins = m_step(j, s, (nth - 1) % 2)
                                ins.then_inc(row_d.sem if j == MSTEPS - 1 else mstep.sem, 1)

                    for k, (s, x) in enumerate(units):
                        sa, xa, complete = ahead(k)
                        if xa == 0 and STEPS[sa][1] == 0:
                            ua = STEPS[sa][0]
                            dve.wait_ge(c_in[ua], (i + 1 if ua == 1 else i + 2) * 16)
                            head_vectors(go, ua, (i * 2 + (1 if ua == 1 else 2)) % H, go)
                        maximum(mx_mm.past(i, AHEAD + k + 1), sa, xa, k % 3)
                        m_steps(k, 0)
                        if k:
                            lower(k - 1)
                        m_steps(k, 1)
                        if complete_at(k - COPY_LAG):
                            copy_row(ahead(k - COPY_LAG)[0], i * NS + rows_before(k - COPY_LAG + 1))
                        if s and x == PV_LAG:
                            result(s - 1)
                        if s and x == PV_LAG + 1:
                            result_scaled(s - 1)
                        if s and STEPS[s][1] == 0 and x == PV_LAG:
                            result_scaled(s - 1)
                    lower(NQK - 1)
                    result(NS - 1)
                    result_scaled(NS - 1)
                    assert n[0] == NDV, n[0]


def output(nc, a, m):
    with ExitStack() as ctx:
        sb, ps, sem, count = scope(nc, ctx, "output")
        HALF = 512
        UN = 4
        y, g, x = (sb(n, [P, UN, DM]) for n in ("y", "g", "xr"))
        sqy, sqz = sb("sqy", [P, DM]), sb("sqz", [P, HALF])
        yst = sb("yst", [P, UN, 4])
        zst = sb("zst", [P, 2, 6])
        yh, yl = sb("yh", [P, 2, 2, HALF], F16), sb("yl", [P, 2, 2, HALF], F16)
        o = sb("o", [P, 2, DM])
        ptr = [ps(f"optr{j}") for j in range(2)]
        pz = [[ps(f"pz{s}{j}") for j in range(2)] for s in range(2)]

        yg_in = [sem(f"yg_in{s}") for s in range(UN)]
        xr_in = [sem(f"xr_in{s}") for s in range(UN)]
        gated, sq_d, norm_d, inv_d, scaled = (count("o_" + n, 1) for n in ("gated", "sq_d", "norm_d", "inv_d", "scaled"))
        tr_mm, hi_d, lo_d = count("o_tr_mm", 2, 2), count("o_hi_d", 2), count("o_lo_d", 2)
        z_mm = count("z_mm", 2 * UN)
        zs_d, z_sq, z_sum, z_std, z_fac = (count(n, UN) for n in ("zs_d", "z_sq", "z_sum", "z_std", "z_fac"))
        o_d, sum_d = count("o_o_d", UN, 2), count("sum_d", UN)
        z_fst, zf_d, rn_d = count("z_first", UN), count("zf_d", UN), count("rn_d", 1)
        sent = [sem(f"out_sent{s}") for s in range(2)]
        TURNS = NT // UN

        with nc.Block() as block:
            @block.sync
            def _(sp):
                def load(seq, tile, s):
                    sp.wait_ge(tr_mm.sem, tr_mm.past(seq, 2 - 2 * UN))
                    sp.sem_inc(m.passed, 1)
                    r = bass.ds(tile * P, P)
                    sp.dma_start(y[:, s, :], m.Y[r, :]).then_inc(yg_in[s], 16)
                    sp.dma_start(g[:, s, :], m.G[r, :]).then_inc(yg_in[s], 16)

                def load_x(tile, s):
                    sp.dma_start(x[:, s, :], a.x[0, bass.ds(tile * P, P), :]).then_inc(xr_in[s], 16)

                for t in range(UN - 1):
                    r = slice(t * P, (t + 1) * P)
                    sp.dma_start(y[:, t, :], m.Y[r, :]).then_inc(yg_in[t], 16)
                    sp.dma_start(g[:, t, :], m.G[r, :]).then_inc(yg_in[t], 16)
                    if t < 2:
                        load_x(t, t)
                with sp.Fori(0, TURNS) as i:
                    for u in range(UN):
                        load(i * UN + (u + 3), (i * UN + (u + 3)) % NT, (u + 3) % UN)
                        load_x((i * UN + (u + 2)) % NT, (u + 2) % UN)
                        sp.wait_ge(sum_d.sem, sum_d.past(i, u + 1))
                        sp.sem_inc(m.passed, 1)
                        sp.dma_start(m.out[0, bass.ds((i * UN + u) * P, P), :], o[:, u % 2, :]).then_inc(sent[u % 2], 16)
                for s in range(2):
                    sp.wait_ge(sent[s], 16 * (NT // 2))
                for s in range(UN - 1):
                    sp.wait_ge(yg_in[s], 32 * (TURNS + 1))
                for s in range(2):
                    sp.wait_ge(xr_in[s], 16 * (TURNS + 1))

            @block.gpsimd
            def _(pool):
                with pool.Fori(0, TURNS) as i:
                    for u in range(UN):
                        pool.wait_ge(o_d.sem, o_d.past(i, u + 1))
                        pool.wait_ge(xr_in[u], (i + 1) * 16)
                        nc.gpsimd.tensor_tensor(o[:, u % 2, :], o[:, u % 2, :], x[:, u, :], ALU.add).then_inc(sum_d.sem, 1)

            @block.scalar
            def _(act):
                def norm(seq, s):
                    act.wait_ge(gated.sem, gated.past(seq, 1))
                    nc.scalar.activation(sqy[:], y[:, s, :], ACT.Square, accum_out=yst[:, s, 0:1]).then_inc(sq_d.sem, 1)
                    act.wait_ge(sq_d.sem, sq_d.past(seq, 1))
                    nc.scalar.activation(yst[:, s, 1:2], yst[:, s, 0:1], ACT.Sqrt, bias=m.eps[:, 2:3]).then_inc(norm_d.sem, 1)

                def hi(seq, s):
                    for j in range(2):
                        act.wait_ge(tr_mm.sem, tr_mm.past(seq, j + 1))
                        nc.scalar.activation(yh[:, s % 2, j, :], ptr[j][:], ACT.Copy).then_inc(hi_d.sem, 1)

                def square_z(i, u):
                    for j in range(2):
                        act.wait_ge(z_mm.sem, z_mm.past(i, 2 * u + j + 1))
                        if j == 0:
                            act.wait_ge(zs_d.sem, zs_d.past(i, u + 1))
                        ins = nc.scalar.activation(sqz[:], pz[u % 2][j][:], ACT.Square, scale=zst[:, u % 2, 0:1],
                                                   accum_out=zst[:, u % 2, 1 + j:2 + j])
                        if j == 0:
                            ins.then_inc(z_fst.sem, 1)
                            act.wait_ge(z_fst.sem, z_fst.past(i, u + 1))
                    ins.then_inc(z_sq.sem, 1)
                    act.wait_ge(z_sum.sem, z_sum.past(i, u + 1))
                    nc.scalar.activation(zst[:, u % 2, 4:5], zst[:, u % 2, 3:4], ACT.Sqrt, bias=m.eps[:, 0:1], scale=1.0 / DM)\
                        .then_inc(z_std.sem, 1)

                norm(0, 0)
                norm(1, 1)
                hi(0, 0)
                with act.Fori(0, TURNS) as i:
                    for u in range(UN):
                        hi(i * UN + (u + 1), (u + 1) % UN)
                        norm(i * UN + (u + 2), (u + 2) % UN)
                        square_z(i, u)

            @block.tensor
            def _(pe):
                pe.sem_inc(tr_mm.sem, tr_mm.credit)

                def turn_y(seq, s):
                    pe.wait_ge(scaled.sem, scaled.past(seq, 1))
                    for j in range(2):
                        for k in range(4):
                            c = (4 * j + k) * P
                            t = nc.tensor.transpose(ptr[j][:, k * P:(k + 1) * P], y[:, s, c:c + P], m.ident[:])
                        t.then_inc(tr_mm.sem, 1)

                def product(i, u, j):
                    for k in range(KT):
                        ks = slice((k % 4) * P, (k % 4 + 1) * P)
                        for c, (l, r) in enumerate(((yh, m.woh), (yh, m.wol), (yl, m.woh))):
                            mm = nc.tensor.matmul(pz[u % 2][j][:], l[:, u % 2, k // 4, ks], r[:, k, j * HALF:(j + 1) * HALF],
                                                  start=(k == 0 and c == 0), stop=(k == KT - 1 and c == 2))
                    mm.then_inc(z_mm.sem, 1)

                turn_y(0, 0)
                with pe.Fori(0, TURNS) as i:
                    for u in range(UN):
                        seq = i * UN + u
                        pe.wait_ge(lo_d.sem, lo_d.past(seq, 2))
                        pe.wait_ge(o_d.sem, o_d.past(i, u - 1))
                        product(i, u, 0)
                        turn_y(i * UN + (u + 1), (u + 1) % UN)
                        product(i, u, 1)

            @block.vector
            def _(dve):
                tt, stt, ts = nc.vector.tensor_tensor, nc.vector.scalar_tensor_tensor, nc.vector.tensor_scalar
                dve.sem_inc(o_d.sem, o_d.credit)
                def prepare_y(seq, s, loads):
                    dve.wait_ge(yg_in[s], loads * 32)
                    tt(y[:, s, :], y[:, s, :], g[:, s, :], ALU.mult).then_inc(gated.sem, 1)
                    dve.wait_ge(norm_d.sem, norm_d.past(seq, 1))
                    ts(yst[:, s, 3:4], yst[:, s, 1:2], 1.0 / TOP, None, ALU.mult).then_inc(inv_d.sem, 1)
                    dve.wait_ge(inv_d.sem, inv_d.past(seq, 1))
                    nc.vector.reciprocal(yst[:, s, 2:3], yst[:, s, 3:4]).then_inc(rn_d.sem, 1)
                    dve.wait_ge(rn_d.sem, rn_d.past(seq, 1))
                    ts(y[:, s, :], y[:, s, :], yst[:, s, 2:3], None, ALU.mult).then_inc(scaled.sem, 1)

                def lo(seq, s):
                    for j in range(2):
                        dve.wait_ge(hi_d.sem, hi_d.past(seq, j + 1))
                        tt(yl[:, s % 2, j, :], ptr[j][:], yh[:, s % 2, j, :], ALU.subtract).then_inc(lo_d.sem, 1)

                prepare_y(0, 0, 1)
                prepare_y(1, 1, 1)
                lo(0, 0)
                with dve.Fori(0, TURNS) as i:
                    for u in range(UN):
                        s = u % 2
                        dve.wait_ge(o_d.sem, o_d.past(i, u))
                        ts(zst[:, s, 0:1], yst[:, u, 3:4], m.wsc[:, 2:3], None, ALU.mult).then_inc(zs_d.sem, 1)
                        dve.wait_ge(zs_d.sem, zs_d.past(i, u + 1))
                        lo(i * UN + (u + 1), (u + 1) % UN)
                        prepare_y(i * UN + (u + 2), (u + 2) % UN, i + (u + 2) // UN + 1)
                        dve.wait_ge(z_sq.sem, z_sq.past(i, u + 1))
                        tt(zst[:, s, 3:4], zst[:, s, 1:2], zst[:, s, 2:3], ALU.add).then_inc(z_sum.sem, 1)
                        dve.wait_ge(z_std.sem, z_std.past(i, u + 1))
                        nc.vector.reciprocal(zst[:, s, 5:6], zst[:, s, 4:5]).then_inc(z_fac.sem, 1)
                        dve.wait_ge(z_fac.sem, z_fac.past(i, u + 1))
                        ts(zst[:, s, 5:6], zst[:, s, 5:6], zst[:, s, 0:1], None, ALU.mult).then_inc(zf_d.sem, 1)
                        dve.wait_ge(zf_d.sem, zf_d.past(i, u + 1))
                        dve.wait_ge(sent[s], i * 32 + 16 * (u // 2))
                        for j in range(2):
                            ins = stt(o[:, s, j * HALF:(j + 1) * HALF], pz[s][j][:], zst[:, s, 5:6],
                                      m.gate[:, j * HALF:(j + 1) * HALF], ALU.mult, ALU.mult)
                        ins.then_inc(o_d.sem, 1)


class Inputs:

    def __init__(self, x, c, ada_w, ada_b, norm_pre, norm_post, w_in, fox_q_gain, fox_k_gain, fox_f_bias,
                 rwkv_mu, rwkv_w0, rwkv_w2, rwkv_a0, rwkv_a2, rwkv_k_k, rwkv_k_a, rwkv_r_k, rwkv_ln_g,
                 rwkv_ln_b, pool_w, pool_scale, w_out):
        self.x = x
        self.c = c
        self.ada_w = ada_w
        self.ada_b = ada_b
        self.norm_pre = norm_pre
        self.norm_post = norm_post
        self.w_in = w_in
        self.fox_q_gain = fox_q_gain
        self.fox_k_gain = fox_k_gain
        self.fox_f_bias = fox_f_bias
        self.rwkv_mu = rwkv_mu
        self.rwkv_w0 = rwkv_w0
        self.rwkv_w2 = rwkv_w2
        self.rwkv_a0 = rwkv_a0
        self.rwkv_a2 = rwkv_a2
        self.rwkv_k_k = rwkv_k_k
        self.rwkv_k_a = rwkv_k_a
        self.rwkv_r_k = rwkv_r_k
        self.rwkv_ln_g = rwkv_ln_g
        self.rwkv_ln_b = rwkv_ln_b
        self.pool_w = pool_w
        self.pool_scale = pool_scale
        self.w_out = w_out


def hymba_layer(nc, a, out):
    with ExitStack() as ctx:
        m = persistent(nc, ctx)
        m.out = out
        m.QK = nc.dram_tensor("scratch_qk", [2, 2, FOX_W, SEQ], F16).ap()
        m.V = nc.dram_tensor("scratch_v", [SEQ, 2, FOX_W], F16).ap()
        m.Z = nc.dram_tensor("scratch_z", [ZC, m.HALO + SEQ], F32).ap()
        m.G = nc.dram_tensor("scratch_g", [SEQ, DM], F32).ap()
        m.Y = nc.dram_tensor("scratch_y", [SEQ, DM], F32).ap()
        m.NC = nc.dram_tensor("scratch_nc", [FOX_HEADS, SEQ], F32).ap()
        with ExitStack() as weights:
            m.wh = weights.enter_context(nc.sbuf_tensor("wh", [P, KT, D_IN], F16))
            m.wl = weights.enter_context(nc.sbuf_tensor("wl", [P, KT, D_IN], F16))
            prepare(nc, a, m)
            project(nc, a, m)
        m.woh = ctx.enter_context(nc.sbuf_tensor("woh", [P, KT, DM], F16))
        m.wol = ctx.enter_context(nc.sbuf_tensor("wol", [P, KT, DM], F16))
        m.wsc = ctx.enter_context(nc.sbuf_tensor("wsc", [P, 4], F32))
        decay(nc, a, m)
        recur(nc, a, m)
        attend(nc, a, m)
        output(nc, a, m)


INPUTS = ("x", "c", "ada_w", "ada_b", "norm_pre", "norm_post", "w_in", "fox_q_gain", "fox_k_gain", "fox_f_bias",
          "rwkv_mu", "rwkv_w0", "rwkv_w2", "rwkv_a0", "rwkv_a2", "rwkv_k_k", "rwkv_k_a", "rwkv_r_k", "rwkv_ln_g",
          "rwkv_ln_b", "pool_w", "pool_scale", "w_out")


def kernel(**inputs):
    import numpy as np
    import concourse.bacc as bacc
    from concourse.bass_utils import run_bass_kernel_spmd

    nc = bacc.Bacc("TRN2", target_bir_lowering=False, num_devices=1)
    arrays, aps = {}, {}
    for name in INPUTS:
        array = np.ascontiguousarray(inputs[name])
        arrays[f"in_{name}"] = array
        aps[name] = nc.dram_tensor(f"in_{name}", array.shape, mybir.dt.from_np(array.dtype), kind="ExternalInput").ap()
    out = nc.dram_tensor("out", [1, SEQ, DM], F32, kind="ExternalOutput").ap()
    hymba_layer(nc, Inputs(**aps), out)
    result = run_bass_kernel_spmd(nc, [arrays], core_ids=[0])
    return result.results[0]["out"]
```
